# Optimizing a Trainium2 kernel written in Bass

```python
import math
import jax, jax.numpy as jnp
from jax import lax
import numpy as np

D_MODEL = 2048
BATCH = 1
SEQ = 256
DEPTH = 2

PLE_DIM = 256
D_FF = 4 * D_MODEL
NORM_EPS = 1e-6
ROPE_THETA = 500000.0
ROPE_FRACTION = 4
QBLK = 128
A_WIDTH = D_MODEL // 2
A_DV = 128
A_HEADS = A_WIDTH // A_DV
A_DC = A_DV // 2
A_IN = 3 * A_WIDTH
DIFF_SUBLN_EPS = 1e-5
B_WIDTH = D_MODEL // 2
B_HEAD = 64
B_HEADS = B_WIDTH // B_HEAD
DECAY_LORA = max(32, int(round(1.8 * D_MODEL ** 0.5 / 32)) * 32)
AAA_LORA = max(32, int(round(1.8 * D_MODEL ** 0.5 / 32)) * 32)
GATE_LORA = max(32, int(round(0.6 * D_MODEL ** 0.8 / 32)) * 32)
B_IN = 3 * B_WIDTH + DECAY_LORA + AAA_LORA + GATE_LORA
LNX_EPS = 64e-5
AB_IN = A_IN + B_IN
C_HEADS = 16
C_HEAD_DIM = D_MODEL // C_HEADS
C_KV_HEADS = 4
C_REP = C_HEADS // C_KV_HEADS
C_WIDTH = C_HEADS * C_HEAD_DIM
IDX_HEADS = 16
IDX_DIM = 64
TOPK_MAX = 256
LN_EPS = 1e-6
C_IN = C_WIDTH + 2 * C_KV_HEADS * C_HEAD_DIM + IDX_HEADS * IDX_DIM + IDX_DIM + IDX_HEADS

kernel_name = 'hybrid_diffattn_rwkv7_dsa_block'

def rms_norm(x, g, eps=NORM_EPS):
    xf = x.astype(jnp.float32)
    y = xf * lax.rsqrt(jnp.mean(xf * xf, axis=-1, keepdims=True) + eps)
    return (y * g.astype(jnp.float32)).astype(x.dtype)

def layer_norm(x, g, b, eps=LN_EPS):
    xf = x.astype(jnp.float32)
    mu = jnp.mean(xf, axis=-1, keepdims=True)
    var = jnp.mean(jnp.square(xf - mu), axis=-1, keepdims=True)
    y = (xf - mu) * lax.rsqrt(var + eps)
    return (y * g.astype(jnp.float32) + b.astype(jnp.float32)).astype(x.dtype)

def partial_rope(x, pos):
    dh = x.shape[-1]
    rot = dh // ROPE_FRACTION
    half = rot // 2
    inv_freq = ROPE_THETA ** (-(jnp.arange(half, dtype=jnp.float32) * 2.0 / rot))
    ang = pos.astype(jnp.float32)[..., None] * inv_freq
    cos = jnp.cos(ang)[:, :, None, :]
    sin = jnp.sin(ang)[:, :, None, :]
    x1 = x[..., :half].astype(jnp.float32)
    x2 = x[..., half:rot].astype(jnp.float32)
    r1 = (x1 * cos - x2 * sin).astype(x.dtype)
    r2 = (x2 * cos + x1 * sin).astype(x.dtype)
    return jnp.concatenate([r1, r2, x[..., rot:]], axis=-1)

def to_blocks(t, nb):
    return jnp.moveaxis(t.reshape((t.shape[0], nb, QBLK) + t.shape[2:]), 1, 0)

def diff_attention(q, k, v, lam, subln_g, lambda_init):
    B, T = q.shape[0], q.shape[1]
    nb = T // QBLK
    qb = to_blocks(q * (A_DC ** -0.5), nb)
    kpos = jnp.arange(T)

    def block(args):
        qblk, start = args
        s = jnp.einsum('bqhcd,bshcd->bhcqs', qblk, k).astype(jnp.float32)
        qpos = start + jnp.arange(QBLK)
        causal = kpos[None, :] <= qpos[:, None]
        s = jnp.where(causal, s, -jnp.inf)
        pm = jax.nn.softmax(s, axis=-1)
        attn = pm[:, :, 0] - lam * pm[:, :, 1]
        return jnp.einsum('bhqs,bshd->bqhd', attn.astype(v.dtype), v)

    out = lax.map(block, (qb, jnp.arange(nb) * QBLK))
    out = jnp.moveaxis(out, 0, 1).reshape(B, T, A_HEADS, A_DV)
    out = rms_norm(out, subln_g, DIFF_SUBLN_EPS) * (1.0 - lambda_init)
    return out.reshape(B, T, A_WIDTH)

def wkv7_scan(r, w, k, v, a, b):
    B, T, H, N = r.shape
    xs = tuple(jnp.moveaxis(t.astype(jnp.float32), 1, 0) for t in (r, w, k, v, a, b))

    def step(S, inp):
        r_t, w_t, k_t, v_t, a_t, b_t = inp
        sa = jnp.einsum('bhvk,bhk->bhv', S, a_t)
        S = S * w_t[:, :, None, :] + sa[..., None] * b_t[:, :, None, :] + v_t[..., None] * k_t[:, :, None, :]
        y = jnp.einsum('bhvk,bhk->bhv', S, r_t)
        return S, y

    S0 = jnp.zeros((B, H, N, N), jnp.float32)
    _, ys = lax.scan(step, S0, xs)
    return jnp.moveaxis(ys, 0, 1)

def rwkv7_time_mix(zb, mu, w0, w2, a0, a2, g2, k_k, k_a, r_k, lnx_g, lnx_b):
    B, T, _ = zb.shape
    prev = jnp.pad(zb, ((0, 0), (1, 0), (0, 0)))[:, :T]
    zb = zb + (prev - zb) * mu
    cuts = [B_WIDTH, 2 * B_WIDTH, 3 * B_WIDTH, 3 * B_WIDTH + DECAY_LORA, 3 * B_WIDTH + DECAY_LORA + AAA_LORA]
    r, k, v, xw, xa, xg = jnp.split(zb, cuts, axis=-1)
    w = -jax.nn.softplus(-(w0 + jnp.tanh(xw) @ w2)) - 0.5
    a = jax.nn.sigmoid(a0 + xa @ a2)
    g = jax.nn.sigmoid(xg) @ g2
    heads = lambda t: t.reshape(B, T, B_HEADS, B_HEAD)
    kk = heads(k * k_k).astype(jnp.float32)
    kk = kk / jnp.maximum(jnp.sqrt(jnp.sum(kk * kk, axis=-1, keepdims=True)), 1e-12)
    k = k * (1.0 + (a - 1.0) * k_a)
    decay = jnp.exp(-jnp.exp(w.astype(jnp.float32)))
    y = wkv7_scan(heads(r), heads(decay), heads(k), heads(v), -kk, kk * heads(a).astype(jnp.float32))
    mu_y = jnp.mean(y, axis=-1, keepdims=True)
    var_y = jnp.mean(jnp.square(y - mu_y), axis=-1, keepdims=True)
    y = (y - mu_y) * lax.rsqrt(var_y + LNX_EPS)
    y = y * lnx_g.reshape(B_HEADS, B_HEAD).astype(jnp.float32) + lnx_b.reshape(B_HEADS, B_HEAD).astype(jnp.float32)
    bonus = jnp.sum(heads(r) * heads(k) * r_k, axis=-1, keepdims=True) * heads(v)
    y = (y + bonus.astype(jnp.float32)).reshape(B, T, B_WIDTH) * g.astype(jnp.float32)
    return y.astype(zb.dtype)

def mixer_ab(u, pos, w_in, w_out, lq1, lk1, lq2, lk2, subln_g, mu, w0, w2, a0, a2, g2,
             k_k, k_a, r_k, lnx_g, lnx_b, lambda_init):
    B, T, _ = u.shape
    z = u @ w_in
    za, zb = z[..., :A_IN], z[..., A_IN:]
    qa, ka, va = jnp.split(za, 3, axis=-1)
    qa = partial_rope(qa.reshape(B, T, 2 * A_HEADS, A_DC), pos).reshape(B, T, A_HEADS, 2, A_DC)
    ka = partial_rope(ka.reshape(B, T, 2 * A_HEADS, A_DC), pos).reshape(B, T, A_HEADS, 2, A_DC)
    va = va.reshape(B, T, A_HEADS, A_DV)
    lam = (jnp.exp(jnp.sum(lq1.astype(jnp.float32) * lk1.astype(jnp.float32)))
           - jnp.exp(jnp.sum(lq2.astype(jnp.float32) * lk2.astype(jnp.float32))) + lambda_init)
    ya = diff_attention(qa, ka, va, lam, subln_g, lambda_init)
    yb = rwkv7_time_mix(zb, mu, w0, w2, a0, a2, g2, k_k, k_a, r_k, lnx_g, lnx_b)
    return jnp.concatenate([ya.astype(u.dtype), yb.astype(u.dtype)], axis=-1) @ w_out

def mixer_c(u, pos, w_in, w_out, idx_k_g, idx_k_b, topk):
    B, T, _ = u.shape
    z = u @ w_in
    c1 = C_WIDTH
    c2 = c1 + C_KV_HEADS * C_HEAD_DIM
    c3 = c2 + C_KV_HEADS * C_HEAD_DIM
    c4 = c3 + IDX_HEADS * IDX_DIM
    c5 = c4 + IDX_DIM
    q, k, v, qi, ki, wi = jnp.split(z, [c1, c2, c3, c4, c5], axis=-1)
    q = partial_rope(q.reshape(B, T, C_HEADS, C_HEAD_DIM), pos)
    k = partial_rope(k.reshape(B, T, C_KV_HEADS, C_HEAD_DIM), pos)
    v = v.reshape(B, T, C_KV_HEADS, C_HEAD_DIM)
    qi = partial_rope(qi.reshape(B, T, IDX_HEADS, IDX_DIM), pos)
    ki = partial_rope(layer_norm(ki, idx_k_g, idx_k_b)[:, :, None, :], pos)[:, :, 0]
    wi = wi * ((IDX_HEADS * IDX_DIM) ** -0.5)
    nb = T // QBLK
    kpos = jnp.arange(T)
    scale = C_HEAD_DIM ** -0.5
    gather = jax.vmap(lambda src, ix: src[ix])

    def block(args):
        qb, qib, wib, start = args
        qpos = start + jnp.arange(QBLK)
        causal = kpos[None, :] <= qpos[:, None]
        isc = jax.nn.relu(jnp.einsum('bqhd,bsd->bqhs', qib, ki))
        score = jnp.einsum('bqhs,bqh->bqs', isc, wib).astype(jnp.float32)
        score = jnp.where(causal[None], score, -jnp.inf)
        _, sel = lax.top_k(score, topk)
        valid = sel <= qpos[None, :, None]
        ks = gather(k, sel)
        vs = gather(v, sel)
        qg = qb.reshape(B, QBLK, C_KV_HEADS, C_REP, C_HEAD_DIM)
        s = jnp.einsum('bqgrd,bqkgd->bqgrk', qg, ks).astype(jnp.float32) * scale
        s = jnp.where(valid[:, :, None, None, :], s, -jnp.inf)
        pr = jax.nn.softmax(s, axis=-1)
        o = jnp.einsum('bqgrk,bqkgd->bqgrd', pr.astype(vs.dtype), vs)
        return o.reshape(B, QBLK, C_WIDTH)

    o = lax.map(block, (to_blocks(q, nb), to_blocks(qi, nb), to_blocks(wi, nb), jnp.arange(nb) * QBLK))
    o = jnp.moveaxis(o, 0, 1).reshape(B, T, C_WIDTH)
    return o @ w_out

def sq_relu_mlp(u, w_up, w_down):
    return jnp.square(jax.nn.relu(u @ w_up)) @ w_down

def setup_inputs(seed: int = 0) -> dict:
    key = jax.random.key(seed)
    ks = iter(jax.random.split(key, 48))
    f32 = jnp.float32
    NE = (DEPTH + 1) // 2
    NO = DEPTH // 2

    def dense(shape, fan_in, scale=1.0):
        return jax.random.normal(next(ks), shape, f32) * (scale * fan_in ** -0.5)

    def gain(shape):
        return 1.0 + 0.05 * jax.random.normal(next(ks), shape, f32)

    def small(shape, s=0.02):
        return s * jax.random.normal(next(ks), shape, f32)

    x = jax.random.normal(next(ks), (BATCH, SEQ, D_MODEL), f32)
    p = jax.random.normal(next(ks), (DEPTH, BATCH, SEQ, PLE_DIM), f32)
    offsets = jax.random.randint(next(ks), (BATCH, 1), 0, 4096, dtype=jnp.int32)
    positions = offsets + jnp.arange(SEQ, dtype=jnp.int32)[None, :]
    return {
        'x': x,
        'p': p,
        'positions': positions,
        'mix_pre_g': gain((DEPTH, D_MODEL)),
        'mix_post_g': gain((DEPTH, D_MODEL)),
        'mlp_pre_g': gain((DEPTH, D_MODEL)),
        'mlp_post_g': gain((DEPTH, D_MODEL)),
        'w_mlp_up': dense((DEPTH, D_MODEL, D_FF), D_MODEL),
        'w_mlp_down': dense((DEPTH, D_FF, D_MODEL), D_FF),
        'w_ple_proj': dense((DEPTH, PLE_DIM, D_MODEL), PLE_DIM),
        'w_ple_gate': dense((DEPTH, D_MODEL, D_MODEL), D_MODEL),
        'ple_post_g': gain((DEPTH, D_MODEL)),
        'ab_w_in': dense((NE, D_MODEL, AB_IN), D_MODEL),
        'ab_w_out': dense((NE, A_WIDTH + B_WIDTH, D_MODEL), A_WIDTH + B_WIDTH),
        'diff_lq1': small((NE, A_DC), 0.1),
        'diff_lk1': small((NE, A_DC), 0.1),
        'diff_lq2': small((NE, A_DC), 0.1),
        'diff_lk2': small((NE, A_DC), 0.1),
        'diff_subln_g': gain((NE, A_DV)),
        'rwkv_mu': jax.random.uniform(next(ks), (NE, B_IN), f32, 0.0, 1.0),
        'rwkv_w0': jax.random.uniform(next(ks), (NE, B_WIDTH), f32, -5.0, 1.0),
        'rwkv_w2': dense((NE, DECAY_LORA, B_WIDTH), DECAY_LORA, 0.1),
        'rwkv_a0': small((NE, B_WIDTH), 0.1),
        'rwkv_a2': dense((NE, AAA_LORA, B_WIDTH), AAA_LORA, 0.1),
        'rwkv_g2': dense((NE, GATE_LORA, B_WIDTH), GATE_LORA),
        'rwkv_k_k': 0.85 + small((NE, B_WIDTH), 0.05),
        'rwkv_k_a': gain((NE, B_WIDTH)),
        'rwkv_r_k': small((NE, B_HEADS, B_HEAD), 0.1),
        'rwkv_lnx_g': gain((NE, B_WIDTH)),
        'rwkv_lnx_b': small((NE, B_WIDTH), 0.02),
        'c_w_in': dense((NO, D_MODEL, C_IN), D_MODEL),
        'c_w_out': dense((NO, C_WIDTH, D_MODEL), C_WIDTH),
        'idx_k_g': gain((NO, IDX_DIM)),
        'idx_k_b': small((NO, IDX_DIM), 0.02),
    }

def reference(x, p, positions, mix_pre_g, mix_post_g, mlp_pre_g, mlp_post_g, w_mlp_up, w_mlp_down,
              w_ple_proj, w_ple_gate, ple_post_g, ab_w_in, ab_w_out, diff_lq1, diff_lk1, diff_lq2,
              diff_lk2, diff_subln_g, rwkv_mu, rwkv_w0, rwkv_w2, rwkv_a0, rwkv_a2, rwkv_g2, rwkv_k_k,
              rwkv_k_a, rwkv_r_k, rwkv_lnx_g, rwkv_lnx_b, c_w_in, c_w_out, idx_k_g, idx_k_b):
    T = x.shape[1]
    topk = min(TOPK_MAX, T // 4)
    h = x
    for i in range(DEPTH):
        j = i // 2
        u = rms_norm(h, mix_pre_g[i])
        if i % 2 == 0:
            lambda_init = 0.8 - 0.6 * math.exp(-0.3 * i)
            m = mixer_ab(u, positions, ab_w_in[j], ab_w_out[j], diff_lq1[j], diff_lk1[j], diff_lq2[j],
                         diff_lk2[j], diff_subln_g[j], rwkv_mu[j], rwkv_w0[j], rwkv_w2[j], rwkv_a0[j],
                         rwkv_a2[j], rwkv_g2[j], rwkv_k_k[j], rwkv_k_a[j], rwkv_r_k[j], rwkv_lnx_g[j],
                         rwkv_lnx_b[j], lambda_init)
        else:
            m = mixer_c(u, positions, c_w_in[j], c_w_out[j], idx_k_g[j], idx_k_b[j], topk)
        h = h + rms_norm(m, mix_post_g[i])
        u = rms_norm(h, mlp_pre_g[i])
        h = h + rms_norm(sq_relu_mlp(u, w_mlp_up[i], w_mlp_down[i]), mlp_post_g[i])
        e = p[i] @ w_ple_proj[i]
        gate = jax.nn.sigmoid(h @ w_ple_gate[i])
        h = h + rms_norm(e * gate, ple_post_g[i])
    return h


_drawn_inputs = setup_inputs


def setup_inputs(seed=0):
    import zlib

    import numpy as np

    out = dict(_drawn_inputs(seed))
    spreads = {}
    factors = {'diff_lq1': 3.369, 'rwkv_w2': 4.784, 'idx_k_b': 2.881, 'rwkv_lnx_b': 2.952}
    for name, (base, spread) in spreads.items():
        noise = np.random.default_rng([zlib.crc32(name.encode()), seed]).standard_normal(out[name].shape)
        drawn = base * np.exp(spread * noise) if base else spread * noise
        out[name] = __import__('jax').numpy.asarray(drawn.astype(out[name].dtype))
    for name, factor in factors.items():
        out[name] = (out[name] * factor).astype(out[name].dtype)
    return out
```

```python
from contextlib import ExitStack, contextmanager
import math

import numpy as np
import concourse.bass as bass
from concourse import mybir

F32 = mybir.dt.float32
F32R = mybir.dt.float32r
BF16 = mybir.dt.bfloat16
I32 = mybir.dt.int32
ALU = mybir.AluOpType
ACT = mybir.ActivationFunctionType
AX = mybir.AxisListType

P = 128
T = 256
TT = T // P
D = 2048
KT = D // P
DFF = 4 * D
PLE = 256
AW = 1024
BW = 1024
A_HEADS, A_DV, A_DC = 8, 128, 64
B_HEADS, BH = 16, 64
LW, LA, LG = 96, 96, 256
B_IN = 3 * BW + LW + LA + LG
A_IN = 3 * AW
C_HEADS, C_KV, C_HD = 16, 4, 128
IDX_H, IDX_D = 16, 64
C_IN = C_HEADS * C_HD + 2 * C_KV * C_HD + IDX_H * IDX_D + IDX_D + IDX_H
TOPK = T // 4
THETA = 500000.0
LAMBDA_INIT = 0.8 - 0.6 * math.exp(0.0)
NORM_EPS, SUBLN_EPS, LNX_EPS, LN_EPS = 1e-6, 1e-5, 64e-5, 1e-6
CH = 64
NEG = -1e30
TAKEN = -3e38
W = 512
KB = 1024
C_W = C_IN // 9
FULL = ("ab", "mlp0", "ple0", "c", "mlp1", "ple1")


def plan_slabs(plan):
    base, s = {}, 0
    for st in plan:
        parts = {"ab": (("ab_in", 13), ("ab_out", 4)), "c": (("c_in", 9), ("c_out", 4))}.get(
            st, ((st, 32),) if st.startswith("mlp") else ((st, 4),))
        for name, n in parts:
            base[name] = s
            s += n
    return base


class Link:

    def __init__(self, eng, sem):
        self.eng, self.sem, self.n, self.extra = eng, sem, 0, 0

    def __call__(self, ins):
        ins.then_inc(self.sem, 1)
        self.n += 1
        self.eng.wait_ge(self.sem, self.extra + self.n)

    @contextmanager
    def loop(self, i, first, count, per):
        start = self.n
        self.extra = (i - first) * per
        yield
        assert self.n - start == per, (self.n - start, per)
        self.extra, self.n = 0, start + per * count


def build(nc, A, plan=FULL):
    base = plan_slabs(plan)
    ctx = ExitStack()
    sems = {}

    def sem(name):
        if name not in sems:
            sems[name] = ctx.enter_context(nc.semaphore(name))
        return sems[name]

    arena_bytes = 207 * KB + 768
    arena = ctx.enter_context(nc.sbuf_tensor("arena", [P, arena_bytes // 4], F32))
    origin = 16512

    def at(name, shape, dt, kb):
        size = int(np.prod(shape[1:])) * (2 if dt == BF16 else 4)
        assert kb * KB + size <= arena_bytes, name
        return nc.alloc_sbuf_tensor_at(name, shape, dt, offset=int(origin + kb * KB))

    psum = ctx.enter_context(nc.psum_tensor("psum", [P, 8 * 512], F32))
    bank = [psum[:, i * 512:(i + 1) * 512] for i in range(8)]

    h = at("h", [P, TT, D], F32, 0)
    uTh = at("uTh", [P, KT, T], F32R, 16)
    uTl = at("uTl", [P, KT, T], F32R, 32)
    raw = at("raw", [P, 4, 4, W], F32, 48)
    whi = at("whi", [P, 2, 4, W], F32R, 80)
    wlo = at("wlo", [P, 2, 4, W], F32R, 96)
    ident = at("ident", [P, P], F32, 112)
    m_su = at("m_su", [P, P], F32, 112.5)
    m_ui = at("m_ui", [P, P], F32, 113)
    m_l1t = at("m_l1t", [P, P], F32, 113.5)
    m_lv = at("m_lv", [P, 6, P], F32, 114)
    causal = at("causal", [P, T], F32, 117)
    junk = at("junk", [P, W], BF16, 118)
    cosT = at("cosT", [P, TT, 24], F32, 119)
    sinT = at("sinT", [P, TT, 24], F32, 119.1875)
    gpre = at("gpre", [P, 4, KT], F32, 119.375)
    nwt = at("nwt", [P, 2, 32], F32, 207.5)
    g_rows = at("g_rows", [4 * KT, P], F32, 118)
    ssq = at("ssq", [P, TT, 4], F32, 119.625)
    hss = at("hss", [P, TT, 4], F32, 119.65625)
    st2 = at("st2", [P, 8], F32, 119.6875)
    rstd_m = at("rstd_m", [P, TT], F32, 119.71875)
    rstd_h = at("rstd_h", [P, TT], F32, 119.75)
    lam = at("lam", [P, 4], F32, 119.78125)

    m = at("m", [P, TT, D], F32, 120)
    gpost = at("gpost", [P, D], F32, 136)
    hid = at("hid", [P, 2, TT, W], F32, 144)
    hTh = at("hTh", [P, KT, T], F32R, 152)
    hTl = at("hTl", [P, KT, T], F32R, 168)
    wple = at("wple", [P, 2, D], F32, 184)
    pT = at("pT", [P, 2, T], F32, 200)
    pin = at("pin", [P, TT, PLE], F32, 202)
    gate = at("gate", [P, TT, W], F32, 144)

    za = at("za", [P, TT, A_IN], F32, 120)
    zb = at("zb", [P, TT, B_IN], F32, 144)
    zprev = at("zprev", [P, 2, TT, W], F32, 171.5)
    mu = at("mu", [P, 2, W], F32, 179.5)
    qT = at("qT", [P, A_HEADS, T], F32, 16)
    kT = at("kT", [P, A_HEADS, T], F32, 24)
    sm = at("sm", [P, 2, 2, T], F32, 32)
    pe_ = at("pe_", [P, 2, 2, T], F32, 36)
    at_ = at("at_", [P, 2, T], F32, 40)
    atT = at("atT", [P, 2, 2, P], F32, 42)
    rt = at("rt", [P, 4, 512], F32, 171.5)
    subg = at("subg", [P, A_DV], F32, 47)
    lqk = at("lqk", [P, 4, A_DC], F32, 179.5)
    mx = at("mx", [P, 2, 8], F32, 46)
    s16 = at("s16", [P, TT, 16], F32, 46.125)
    s16b = at("s16b", [P, TT, 16], F32, 46.25)
    posi = at("posi", [P, TT], I32, 120)
    posf = at("posf", [P, TT], F32, 120.125)
    freq = at("freq", [P, 24], F32, 120.25)
    angle = at("angle", [P, 96], F32, 120.5)
    asq = at("asq", [P, TT, AW], F32, 171.5)
    r16 = at("r16", [P, 16], F32, 46.5)
    lw = at("lw", [P, TT, BW], F32, 171.5)
    av = at("av", [P, TT, BW], F32, 179.5)
    gv = at("gv", [P, TT, BW], F32, 187.5)
    kkv = at("kkv", [P, TT, BW], F32, 195.5)
    par = at("par", [P, BW], F32, 203.5)
    w2 = at("w2", [P, BW], F32, 16)
    a2 = at("a2", [P, BW], F32, 20)
    g2 = at("g2", [P, 2, BW], F32, 24)
    loraT = at("loraT", [P, 4, T], F32, 32)
    p_w0 = at("p_w0", [P, BW], F32, 36)
    p_a0 = at("p_a0", [P, BW], F32, 40)
    p_kk = at("p_kk", [P, BW], F32, 44)
    ex1 = at("ex1", [P, TT, BW], F32, 80)
    ex2 = at("ex2", [P, TT, BW], F32, 88)
    bon = at("bon", [P, TT, B_HEADS], F32, 118)
    nrm = at("nrm", [P, TT, B_HEADS], F32, 118.125)
    WL = at("WL", [P, 8, 4], F32, 118.25)
    XT = [at(f"{n}T", [P, 8, P], F32, 80 + 4 * i) for i, n in enumerate(("A", "B", "K", "R"))]
    tmp_set = [[at(f"{n}{s}", [P, 4, P], F32, 96 + 2 * i + 8 * s) for i, n in
                enumerate(("MT", "Ti", "Y1", "Lm"))] for s in range(2)]
    NT = at("NT", [P, 16, P], F32, 16)
    PT = at("PT", [P, 16, P], F32, 24)
    QT = at("QT", [P, 16, P], F32, 32)
    TTi = at("TTi", [P, 16, P], F32, 40)
    Xs = at("Xs", [P, BW], F32, 171.5)
    Us = at("Us", [P, BW], F32, 175.5)
    ST = at("ST", [P, 8, P], F32, 203.5)

    GAIN = {"ab_in": 0, "c_in": 1, "mlp0": 2, "mlp1": 3}

    def w_chunks(w, Q):
        v = w.rearrange("(Q q k p) n -> Q q p k n", q=4, k=4, p=P)
        return [v[Q, q] for q in range(4)]

    order = []
    for st_ in plan:
        order += {"ab": ["ab_in", "ab_out"], "c": ["c_in", "c_out"]}.get(st_, [st_])
    width = lambda st: C_W if st == "c_in" else W
    nxt = {a: (order[i + 1] if i + 1 < len(order) else None) for i, a in enumerate(order)}
    prv = {a: (order[i - 1] if i else None) for i, a in enumerate(order)}
    read_out = {"ab_in": ("ev_ab_in", 1, 12), "ab_out": ("m_sq", 2, 3), "c_in": ("ev_c_in", 1, 8),
                "c_out": ("m_sq", 2, 3), "mlp0": ("ev_dn", 1, 15), "mlp1": ("ev_dn", 1, 15),
                "ple0": ("ev_ple", 1, 3), "ple1": ("ev_ple", 1, 3)}

    counts = {"m_sq": lambda st: 32 if st.startswith("mlp") else 0 if st.endswith("_in") else 8,
              "h_ready": lambda st: 0 if st == order[0] or st.endswith("_out") else 8,
              "gpost": lambda st: 0 if st.endswith("_in") else 16,
              "ev_ab_in": lambda st: 0, "ev_c_in": lambda st: 0,
              "h_sq": lambda st: 8 if st in GAIN else 0, "rstd": lambda st: 1 if st in GAIN else 0}
    for kind in ("xT", "xT_hi", "xT_lo"):
        counts[kind] = lambda st: 8
    for kind in ("sq_done", "hT", "hT_hi", "hT_lo", "ev_up", "ev_dn"):
        counts[kind] = lambda st: 16 if st.startswith("mlp") else 0
    for kind, n_ in (("gated", 4), ("emb", 4), ("ev_ple", 4), ("ple_in", 32), ("pT_mm", 1), ("pT", 1)):
        counts[kind] = lambda st, n_=n_: n_ if st.startswith("ple") else 0

    def mark(kind, st, v):
        before = order[:order.index(st)] if st in order else order
        return sem(kind), sum(counts[kind](a) for a in before) + v

    landed = [sem(f"landed{q}") for q in range(4)]
    hi_ready, lo_ready = sem("hi_ready"), sem("lo_ready")
    mm_used = sem("mm_used")

    def load_slab(sp, s, w, col, n, first=False):
        for q in range(4):
            if not first:
                sp.wait_ge(lo_ready, 4 * s - 3 + q)
            sp.dma_start(raw[:, q, :, 0:n], w[q][:, :, bass.ds(col, n)]).then_inc(landed[q], 16)

    def split_hi(act, s, q, n=W, fresh=False):
        act.wait_ge(landed[q], 16 * (s + 1))
        if not fresh:
            act.wait_ge(mm_used, 4 * s + q - 1)
        act.activation(whi[:, q % 2, :, 0:n], raw[:, q, :, 0:n], ACT.Copy).then_inc(hi_ready, 1)

    def split_lo(dve, s, q, n=W):
        dve.wait_ge(hi_ready, 4 * s + q + 1)
        dve.tensor_tensor(wlo[:, q % 2, :, 0:n], raw[:, q, :, 0:n], whi[:, q % 2, :, 0:n].bitcast(F32),
                          ALU.subtract).then_inc(lo_ready, 1)

    def mm_slab(pe, s, par_, n=W, free=None, before=None, lhs=(uTh, uTl)):
        if free:
            pe.wait_ge(*free)
        for q in range(4):
            if before:
                before(q)
            pe.wait_ge(lo_ready, 4 * s + q + 1)
            for k in range(4):
                for tt in range(TT):
                    o = bank[2 * par_ + tt][:, 0:n]
                    xh = lhs[0][:, 4 * q + k, tt * P:(tt + 1) * P]
                    xl = lhs[1][:, 4 * q + k, tt * P:(tt + 1) * P]
                    hi, lo = whi[:, q % 2, k, 0:n], wlo[:, q % 2, k, 0:n]
                    pe.matmul(o, xh, hi, start=(q == 0 and k == 0), stop=False)
                    pe.matmul(o, xh, lo, start=False, stop=False)
                    last = pe.matmul(o, xl, hi, start=False, stop=(q == 3 and k == 3))
            last.then_inc(mm_used, 1)

    def T_pe(pe, st, src, ready, b):
        for pr in range(2):
            g = 2 * b + pr
            if g >= 4:
                pe.wait_ge(*mark("xT_lo", st, g - 3))
            if g == 3 and st == order[0]:
                pe.wait_ge(sem("gpre_ready"), 1)
            if g == 3 and st.startswith("ple"):
                pe.wait_ge(*mark("pT", st, 1))
            for kk in range(2):
                for tt in range(TT):
                    if pr == 0 and kk == 0:
                        pe.wait_ge(*ready(tt, b))
                    c = (2 * pr + kk) * P
                    last = pe.transpose(bank[4 + g % 4][:, (2 * kk + tt) * P:(2 * kk + tt + 1) * P],
                                        src(tt, b)[:, c:c + P], ident[:])
            last.then_inc(sem("xT"), 1)

    def T_act(act, st, b, gain=None):
        for pr in range(2):
            g = 2 * b + pr
            act.wait_ge(*mark("xT", st, g + 1))
            for kk in range(2):
                k = 2 * g + kk
                sc = 1.0 if gain is None else gpre[:, gain, k:k + 1]
                last = act.activation(uTh[:, k, :], bank[4 + g % 4][:, kk * T:(kk + 1) * T], ACT.Copy, scale=sc)
            last.then_inc(sem("xT_hi"), 1)

    def T_dve(dve, st, b, gain=None):
        for pr in range(2):
            g = 2 * b + pr
            dve.wait_ge(*mark("xT_hi", st, g + 1))
            for kk in range(2):
                k = 2 * g + kk
                x = bank[4 + g % 4][:, kk * T:(kk + 1) * T]
                if gain is None:
                    last = dve.tensor_tensor(uTl[:, k, :], x, uTh[:, k, :].bitcast(F32), ALU.subtract)
                else:
                    last = dve.scalar_tensor_tensor(out=uTl[:, k, :], in0=x, scalar=gpre[:, gain, k:k + 1],
                                                    in1=uTh[:, k, :].bitcast(F32), op0=ALU.mult,
                                                    op1=ALU.subtract)
            last.then_inc(sem("xT_lo"), 1)

    def pe_first(pe, st, s, par_, src, ready, n=W, free=None):
        T_pe(pe, st, src, ready, 0)

        def before(q):
            if q < 3:
                T_pe(pe, st, src, ready, q + 1)
            pe.wait_ge(*mark("xT_lo", st, 2 * q + 2))
        mm_slab(pe, s, par_, n, free, before)

    def act_first(act, st, s, n, gain, squares=None, fresh=False):
        for b in range(4):
            if squares:
                squares(b)
            T_act(act, st, b, gain)
            if b >= 2:
                split_hi(act, s, b, n)

    def dve_first(dve, st, s, n, gain):
        for b in range(4):
            T_dve(dve, st, b, gain)
            if b >= 2:
                split_lo(dve, s, b, n)

    last_junk = [None]

    def square(act, x, total, signal, i, prev=None):
        prev = prev or last_junk[0]
        if prev:
            act.wait_ge(*prev)
        last_junk[0] = (signal, i)
        return act.activation(junk[:], x, ACT.Square, accum_out=total).then_inc(signal, 1)

    def h_src(tt, b):
        return h[:, tt, b * W:(b + 1) * W]

    def h_squares(act, st):
        def squares(b):
            for tt in range(TT):
                act.wait_ge(*h_ready(st)(tt, b))
                square(act, h_src(tt, b), hss[:, tt, b:b + 1], *mark("h_sq", st, 2 * b + tt + 1))
        return squares

    def h_ready(st):
        return lambda tt, b: (sem("x_in"), 16) if st == order[0] else mark("h_ready", st, 2 * b + tt + 1)

    def rsqrt(dve, link, x):
        n = x.free_size()
        y, t = nwt[:, 0, 0:n], nwt[:, 1, 0:n]
        link(dve.tensor_scalar(y.bitcast(I32), x.bitcast(I32), 1, None, ALU.logical_shift_right))
        link(dve.tensor_scalar(y.bitcast(I32), y.bitcast(I32), -1.0, float(0x5F3759DF), ALU.mult, ALU.add))
        for i in range(3):
            link(dve.tensor_tensor(t, y, y, ALU.mult))
            link(dve.scalar_tensor_tensor(out=t, in0=t, scalar=-0.5, in1=x, op0=ALU.mult, op1=ALU.mult))
            last = dve.scalar_tensor_tensor(out=y if i < 2 else x, in0=t, scalar=1.5, in1=y, op0=ALU.add,
                                            op1=ALU.mult)
            if i < 2:
                link(last)
        return last

    def rstd_from(dve, link, src, out_, n, eps):
        link(dve.tensor_reduce(out_, src, AX.X, ALU.add))
        link(dve.tensor_scalar(out_, out_, 1.0 / n, eps, ALU.mult, ALU.add))
        return rsqrt(dve, link, out_)

    def h_update(dve, link, st, prev, b):
        if b == 0:
            dve.wait_ge(*mark("m_sq", prev, m_sq_all[prev]))
            link(rstd_from(dve, link, ssq[:], rstd_m[:], D, NORM_EPS))
            dve.wait_ge(*mark("gpost", prev, 16))
        for tt in range(TT):
            mb = m[:, tt, b * W:(b + 1) * W]
            link(dve.scalar_tensor_tensor(out=mb, in0=mb, scalar=rstd_m[:, tt:tt + 1],
                                          in1=gpost[:, b * W:(b + 1) * W], op0=ALU.mult, op1=ALU.mult))
            dve.tensor_tensor(h_src(tt, b), h_src(tt, b), mb, ALU.add).then_inc(sem("h_ready"), 1)

    m_sq_all = {"ab_out": 8, "c_out": 8, "mlp0": 32, "mlp1": 32, "ple0": 8, "ple1": 8}

    def h_first(dve, link, st, s, n, gain, prev):
        for b in range(4):
            if prev:
                h_update(dve, link, st, prev, b)
            if b:
                T_dve(dve, st, b - 1, gain)
            if b == 3:
                split_lo(dve, s, 2, n)
        T_dve(dve, st, 3, gain)
        split_lo(dve, s, 3, n)
        if gain is not None:
            dve.wait_ge(*mark("h_sq", st, 8))
            rstd_from(dve, link, hss[:], rstd_h[:], D, NORM_EPS).then_inc(sem("rstd"), 1)

    def prologue(fn, eng, st):
        if prv[st] is None or prv[st].endswith("_in"):
            s, n = base[st], width(st)
            if fn is split_hi:
                fn(eng, s, 0, n, fresh=(s == 0))
                fn(eng, s, 1, n, fresh=(s == 0))
            else:
                fn(eng, s, 0, n)
                fn(eng, s, 1, n)

    def free_of(st, i):
        if i >= 2:
            return mark(read_out[st][0], st, read_out[st][1] * (i - 1))
        if prv[st] is None:
            return None
        name, by, v = read_out[prv[st]]
        return mark(name, prv[st], by * (v + i))

    N_CONSTS = 7
    HALF_A, HALF_C = A_DC // 8, C_HD // 8
    chain = sem("pool_chain")

    def pool_setup(pool):
        n = [0]

        def link(ins):
            ins.then_inc(chain, 1)
            n[0] += 1
            pool.wait_ge(chain, n[0])

        def keep(ap, pattern, cm, base_, op=ALU.is_ge, fill=0.0):
            return pool.affine_select(out=ap, in_=ap, compare_op=op, fill=fill, base=base_, pattern=pattern,
                                      channel_multiplier=cm)
        for i, g in enumerate((A["mix_pre_g"][0], A["mix_pre_g"][1], A["mlp_pre_g"][0], A["mlp_pre_g"][1])):
            pool.dma_start(g_rows[KT * i:KT * (i + 1), :], g.rearrange("(k p) -> k p", p=P)).then_inc(sem("gpre_in"), 16)
        link(pool.memset(ident[:], 0.0))
        keep(ident[:], [[-1, P]], 1, 0, ALU.not_equal, 1.0).then_inc(sem("consts"), 1)
        link(pool.memset(m_su[:], 1.0))
        v = m_su[:].rearrange("p (j c) -> p j c", c=CH)
        link(keep(v, [[-CH, 2], [0, CH]], 1, 0))
        keep(v, [[CH, 2], [1, CH]], -1, -1).then_inc(sem("consts"), 1)
        link(pool.memset(m_ui[:], 1.0))
        v = m_ui[:].rearrange("p (j c) -> p j c", c=CH)
        link(keep(v, [[-CH, 2], [0, CH]], 1, 0))
        keep(v, [[CH, 2], [1, CH]], -1, 0).then_inc(sem("consts"), 1)
        link(pool.memset(m_l1t[:], 0.0))
        v = m_l1t[:].rearrange("p (j c) -> p j c", c=2)[:, :, 0:1]
        keep(v, [[-2, P // 2], [0, 1]], 1, -1, ALU.not_equal, 1.0).then_inc(sem("consts"), 1)
        link(pool.memset(m_lv[:], 0.0))
        for i in range(6):
            b = 1 << i
            v = m_lv[:, i, :].rearrange("p (j c) -> p j c", c=2 * b)[:, :, b:2 * b]
            link(pool.memset(v, 1.0))
            link(keep(v, [[-2 * b, P // (2 * b)], [0, b]], 1, 0))
            link(keep(v, [[2 * b, P // (2 * b)], [0, b]], -1, b - 1))
        pool.memset(st2[:, 6:7], 0.0).then_inc(sem("consts"), 1)
        link(pool.memset(causal[:], 0.0))
        keep(causal[:, P:T], [[-1, P]], 1, 0, ALU.is_ge, NEG).then_inc(sem("consts"), 1)
        pool.memset(st2[:, 7:8], 0.0).then_inc(sem("consts"), 1)
        for half, f0 in ((HALF_A, 0), (HALF_C, HALF_A)):
            for j in range(half):
                v = np.float32(THETA) ** (-(np.float32(j) * np.float32(2.0) / np.float32(2 * half)))
                pool.memset(freq[:, f0 + j:f0 + j + 1], float(np.float32(v))).then_inc(sem("freqs"), 1)
        with nc.allow_non_contiguous_dma(reason="256 positions"):
            pool.dma_start(posi[:], A["positions"][0].rearrange("(t p) -> p t", p=P)).then_inc(sem("pos_in"), 16)

    def act_setup(act):
        act.wait_ge(sem("gpre_T"), 1)
        act.activation(gpre[:], bank[7][:, 0:4 * KT], ACT.Copy).then_inc(sem("gpre_ready"), 1)
        act.wait_ge(sem("gpre_ready"), 1)

    def dve_setup(dve, link):
        dve.wait_ge(sem("gpre_ready"), 1)

    def step(fn, eng, s, st, nn, done, n=None, mid=None, skip=False):
        n = n or width(st)
        if not skip:
            fn(eng, s, 2, n)
            fn(eng, s, 3, n)
        if mid:
            mid()
        if nn:
            fn(eng, s + 1, 0, nn)
            fn(eng, s + 1, 1, nn)
        if done:
            done()

    def next_width(st):
        return width(nxt[st]) if nxt[st] and not st.endswith("_in") else None

    def T_mlp_pe(pe, l, Q, j):
        pe.wait_ge(*mark("sq_done", f"mlp{l}", 4 * Q + j + 1))
        if j >= 2:
            pe.wait_ge(*mark("hT_lo", f"mlp{l}", 4 * Q + j - 1))
        for pr in range(2):
            for kk in range(2):
                for tt in range(TT):
                    last = pe.transpose(bank[4 + 2 * (j % 2) + pr][:, (2 * kk + tt) * P:(2 * kk + tt + 1) * P],
                                        hid[:, j % 2, tt, (2 * pr + kk) * P:(2 * pr + kk + 1) * P], ident[:])
        last.then_inc(sem("hT"), 1)

    def T_mlp_split(eng, l, Q, j, high):
        eng.wait_ge(*mark("hT" if high else "hT_hi", f"mlp{l}", 4 * Q + j + 1))
        for pr in range(2):
            k = 4 * j + 2 * pr
            x = bank[4 + 2 * (j % 2) + pr][:]
            if high:
                last = eng.activation(hTh[:, k:k + 2, :], x, ACT.Copy)
            else:
                last = eng.tensor_tensor(hTl[:, k:k + 2, :], x, hTh[:, k:k + 2, :].bitcast(F32), ALU.subtract)
        last.then_inc(sem("hT_hi" if high else "hT_lo"), 1)

    def mlp_pe(pe, l, Q):
        st = f"mlp{l}"
        s = base[st] + 8 * Q
        par_ = lambda r: (base[st] + r) % 2
        up = lambda v: mark("ev_up", st, v)
        dn = lambda v: mark("ev_dn", st, v)
        first = isinstance(Q, int)
        if first:
            pe_first(pe, st, s, par_(0), h_src, h_ready(st), W, free_of(st, 0))
            mm_slab(pe, s + 1, par_(1), W, free_of(st, 1))
        else:
            mm_slab(pe, s, par_(0), W, dn(4 * Q - 1))
            mm_slab(pe, s + 1, par_(1), W, dn(4 * Q))
        for j in (2, 3):
            T_mlp_pe(pe, l, Q, j - 2)
            mm_slab(pe, s + j, par_(j), W, up(4 * Q + j - 1))
        T_mlp_pe(pe, l, Q, 2)

        def before(q):
            if q == 3:
                T_mlp_pe(pe, l, Q, 3)
            pe.wait_ge(*mark("hT_lo", f"mlp{l}", 4 * Q + q + 1))
        mm_slab(pe, s + 4, par_(4), W, up(4 * Q + 3), before, (hTh, hTl))
        mm_slab(pe, s + 5, par_(5), W, up(4 * Q + 4), None, (hTh, hTl))
        mm_slab(pe, s + 6, par_(6), W, dn(4 * Q + 1), None, (hTh, hTl))
        mm_slab(pe, s + 7, par_(7), W, dn(4 * Q + 2), None, (hTh, hTl))

    def mlp_act(act, l, Q):
        st = f"mlp{l}"
        first = isinstance(Q, int)
        for r in range(8):
            s, j, par_ = base[st] + 8 * Q + r, r % 4, (base[st] + r) % 2

            def relu():
                act.wait_ge(mm_used, 4 * s + 4)
                if first and r == 0:
                    act.wait_ge(*mark("rstd", st, 1))
                for tt in range(TT):
                    last = act.activation(hid[:, j % 2, tt, :], bank[2 * par_ + tt][:], ACT.Relu,
                                          scale=rstd_h[:, tt:tt + 1])
                last.then_inc(sem("ev_up"), 1)
                if j:
                    T_mlp_split(act, l, Q, j - 1, True)

            def squares():
                act.wait_ge(*mark("ev_dn", f"mlp{l}", 4 * Q + j + 1))
                for tt in range(TT):
                    n = 8 * Q + 2 * j + tt
                    square(act, m[:, tt, j * W:(j + 1) * W], ssq[:, tt, j:j + 1], *mark("m_sq", st, n + 1),
                           None if first and j + tt == 0 else mark("m_sq", st, n))
            step(split_hi, act, s, st, W,
                 squares if r >= 4 else relu, skip=first and r == 0,
                 mid=(lambda: T_mlp_split(act, l, Q, 3, True)) if r == 4 else None)

    def mlp_dve(dve, l, Q):
        st = f"mlp{l}"
        first = isinstance(Q, int)
        for r in range(8):
            s, j, par_ = base[st] + 8 * Q + r, r % 4, (base[st] + r) % 2

            def square():
                dve.wait_ge(*mark("ev_up", f"mlp{l}", 4 * Q + j + 1))
                x = hid[:, j % 2, :, :]
                dve.tensor_tensor(x, x, x, ALU.mult).then_inc(sem("sq_done"), 1)
                if j:
                    T_mlp_split(dve, l, Q, j - 1, False)

            def add():
                dve.wait_ge(mm_used, 4 * s + 4)
                for tt in range(TT):
                    x, y = bank[2 * par_ + tt][:], m[:, tt, j * W:(j + 1) * W]
                    last = dve.tensor_copy(y, x) if first else dve.tensor_tensor(y, y, x, ALU.add)
                last.then_inc(sem("ev_dn"), 1)
            step(split_lo, dve, s, st, W, add if r >= 4 else square, skip=first and r == 0,
                 mid=(lambda: T_mlp_split(dve, l, Q, 3, False)) if r == 4 else None)

    def ple_pe(pe, l):
        st = f"ple{l}"
        pe.wait_ge(*mark("ple_in", f"ple{l}", 32))
        if not prv[st]:
            pe.wait_ge(sem("gpre_ready"), 1)
        for k in range(2):
            for tt in range(TT):
                last = pe.transpose(bank[7][:, (2 * k + tt) * P:(2 * k + tt + 1) * P],
                                    pin[:, tt, k * P:(k + 1) * P], ident[:])
        last.then_inc(sem("pT_mm"), 1)
        for j in range(4):
            s = base[st] + j
            if j == 0:
                pe_first(pe, st, s, s % 2, h_src, h_ready(st), W, free_of(st, 0))
            else:
                mm_slab(pe, s, s % 2, W, free_of(st, j))
                pe.wait_ge(*mark("gated", f"ple{l}", j))
            for tt in range(TT):
                for k in range(2):
                    last = pe.matmul(bank[6 + tt][:], pT[:, k, tt * P:(tt + 1) * P],
                                     wple[:, k, j * W:(j + 1) * W], start=(k == 0), stop=(k == 1))
            last.then_inc(sem("emb"), 1)

    def ple_act(act, l):
        st = f"ple{l}"
        act.wait_ge(*mark("pT_mm", st, 1))
        act.activation(pT[:], bank[7][:], ACT.Copy).then_inc(sem("pT"), 1)
        act_first(act, st, base[st], W, None)
        for j in range(4):
            s = base[st] + j

            def sigmoid():
                act.wait_ge(mm_used, 4 * s + 4)
                for tt in range(TT):
                    last = act.activation(gate[:, tt, :], bank[2 * (s % 2) + tt][:], ACT.Sigmoid)
                last.then_inc(sem("ev_ple"), 1)
                act.wait_ge(*mark("gated", f"ple{l}", j + 1))
                for tt in range(TT):
                    square(act, m[:, tt, j * W:(j + 1) * W], ssq[:, tt, j:j + 1], *mark("m_sq", st, 2 * j + tt + 1))
            step(split_hi, act, s, st, W if j < 3 else next_width(st), sigmoid, skip=(j == 0))

    def ple_dve(dve, link, l):
        st = f"ple{l}"
        h_first(dve, link, st, base[st], W, None, prv[st])
        for j in range(4):
            s = base[st] + j

            def gated():
                dve.wait_ge(*mark("ev_ple", f"ple{l}", j + 1))
                dve.wait_ge(*mark("emb", f"ple{l}", j + 1))
                for tt in range(TT):
                    last = dve.tensor_tensor(m[:, tt, j * W:(j + 1) * W], gate[:, tt, :], bank[6 + tt][:],
                                             ALU.mult)
                last.then_inc(sem("gated"), 1)
            step(split_lo, dve, s, st, W if j < 3 else next_width(st), gated, skip=(j == 0))

    def out_act(act, st, fresh=False):
        if st == "ab_out":
            act.wait_ge(sem("yb_done"), 1)
        prologue(split_hi, act, st)
        act_first(act, st, base[st], W, None)
        for j in range(4):
            s = base[st] + j

            def keep():
                act.wait_ge(mm_used, 4 * s + 4)
                if j == 0:
                    act.wait_ge(*mark("xT", st, 8))
                for tt in range(TT):
                    act.activation(m[:, tt, j * W:(j + 1) * W], bank[2 * (s % 2) + tt][:], ACT.Copy)
                for tt in range(TT):
                    square(act, bank[2 * (s % 2) + tt][:], ssq[:, tt, j:j + 1], *mark("m_sq", st, 2 * j + tt + 1))
            step(split_hi, act, s, st, W if j < 3 else next_width(st), keep, skip=(j == 0))

    def out_dve(dve, st):
        prologue(split_lo, dve, st)
        dve_first(dve, st, base[st], W, None)
        for j in range(4):
            step(split_lo, dve, base[st] + j, st, W if j < 3 else next_width(st), None, skip=(j == 0))

    def out_pe(pe, st, src, ready):
        if st == "ab_out":
            pe.wait_ge(sem("y_out0"), 4)
            pe.wait_ge(sem("y_out1"), 4)
        for j in range(4):
            s = base[st] + j
            if j == 0:
                pe_first(pe, st, s, s % 2, src, ready, W, free_of(st, 0))
            else:
                mm_slab(pe, s, s % 2, W, free_of(st, j))

    def tr_pe(pe, name, groups, banks, first_waits=()):
        for w in first_waits:
            pe.wait_ge(*w)
        for g, items in enumerate(groups):
            if g >= len(banks):
                o = g - len(banks)
                pe.wait_ge(sem(f"{name}_out{o % 2}"), o // 2 + 1)
            for i, x in enumerate(items):
                rows = x.shape[1]
                last = pe.transpose(bank[banks[g % len(banks)]][0:rows, i * P:(i + 1) * P], x, ident[:])
            last.then_inc(sem(f"{name}_tr"), 1)

    def tr_out(eng, name, outs, banks, me):
        for g, (o, rows, c0, c1) in enumerate(outs):
            if g % 2 == me:
                eng.wait_ge(sem(f"{name}_tr"), g + 1)
                x = bank[banks[g % len(banks)]][0:rows, c0:c1]
                ins = eng.activation(o, x, ACT.Copy) if me == 0 else eng.tensor_copy(o, x)
                ins.then_inc(sem(f"{name}_out{me}"), 1)

    def tr_all(eng, name, n):
        for me in range(2):
            if (n + 1 - me) // 2:
                eng.wait_ge(sem(f"{name}_out{me}"), (n + 1 - me) // 2)

    def trig_act(act):
        act.wait_ge(sem("angles"), 2)
        act.activation(sinT[:], sinT[:], ACT.Sin).then_inc(sem("trig"), 1)
        act.activation(cosT[:], cosT[:], ACT.Sin).then_inc(sem("trig"), 1)

    def trig_dve(dve, link):
        ang, kq = angle[:, 0:48].rearrange("p (t f) -> p t f", t=TT), angle[:, 48:96].rearrange("p (t f) -> p t f", t=TT)
        dve.wait_ge(sem("pos_in"), 16)
        dve.wait_ge(sem("freqs"), 24)
        link(dve.tensor_copy(posf[:], posi[:]))
        for tt in range(TT):
            link(dve.tensor_scalar(ang[:, tt, :], freq[:], posf[:, tt:tt + 1], None, ALU.mult))
        magic = 1.5 * 2.0 ** 23
        link(dve.tensor_scalar(kq, ang, 1.0 / (2 * math.pi), magic, ALU.mult, ALU.add))
        link(dve.tensor_scalar(kq, kq, -magic, None, ALU.add))
        c1 = 6.28125
        c2 = float(np.float32(round((2 * math.pi - c1) * 2 ** 21) / 2 ** 21))
        c3 = 2 * math.pi - c1 - c2
        for c in (c1, c2, c3):
            link(dve.scalar_tensor_tensor(out=ang, in0=kq, scalar=-c, in1=ang, op0=ALU.mult, op1=ALU.add))
        lim = 3.1415925
        link(dve.tensor_scalar(ang, ang, lim, -lim, ALU.min, ALU.max))
        dve.tensor_copy(sinT[:], ang).then_inc(sem("angles"), 1)
        link(dve.scalar_tensor_tensor(out=kq, in0=ang, scalar=-1.0, in1=ang, op0=ALU.mult, op1=ALU.max))
        dve.tensor_scalar(cosT[:], kq, -1.0, math.pi / 2, ALU.mult, ALU.add).then_inc(sem("angles"), 1)

    def rope(dve, link, x, tt, f0, half, tmp):
        n = x.shape[1]
        c = cosT[:, tt, f0:f0 + half].unsqueeze(1).broadcast_to([P, n, half])
        s = sinT[:, tt, f0:f0 + half].unsqueeze(1).broadcast_to([P, n, half])
        x1, x2 = x[:, :, 0:half], x[:, :, half:2 * half]
        t = [tmp[:, i, 0:n * half].rearrange("p (a b) -> p a b", b=half) for i in range(4)]
        link(dve.tensor_tensor(t[0], x1, c, ALU.mult))
        link(dve.tensor_tensor(t[1], x2, s, ALU.mult))
        link(dve.tensor_tensor(t[2], x2, c, ALU.mult))
        link(dve.tensor_tensor(t[3], x1, s, ALU.mult))
        link(dve.tensor_tensor(x1, t[0], t[1], ALU.subtract))
        return dve.tensor_tensor(x2, t[2], t[3], ALU.add)

    def ab_in_pe(pe):
        st, b = "ab_in", base["ab_in"]
        ev = sem("ev_ab_in")
        pe_first(pe, st, b, b % 2, h_src, h_ready(st), W, free_of(st, 0))
        mm_slab(pe, b + 1, (b + 1) % 2, W, free_of(st, 1))
        with pe.Fori(1, 3) as i:
            for j in range(2):
                mm_slab(pe, b + 2 * i + j, (b + j) % 2, W, (ev, 2 * i + j - 1))
        mm_slab(pe, b + 6, b % 2, B_IN - 6 * W, (ev, 5))
        with pe.Fori(0, 3) as i:
            for j in range(2):
                mm_slab(pe, b + 7 + 2 * i + j, (b + 7 + j) % 2, W, (ev, 6 + 2 * i + j))

    def ab_in_act(act):
        st, b = "ab_in", base["ab_in"]
        prologue(split_hi, act, st)
        act_first(act, st, b, W, GAIN[st], h_squares(act, st))
        trig_act(act)

        def keep(s, par_, dst, col, n):
            def f():
                act.wait_ge(mm_used, 4 * s + 4)
                for tt in range(TT):
                    last = act.activation(dst[:, tt, bass.ds(col, n)], bank[2 * par_ + tt][:, 0:n], ACT.Copy,
                                          scale=rstd_h[:, tt:tt + 1])
                last.then_inc(sem("ev_ab_in"), 1)
            return f
        act.wait_ge(*mark("rstd", st, 1))
        step(split_hi, act, b, st, W, keep(b, b % 2, zb, 0, W), skip=True)
        with act.Fori(0, 2) as i:
            for j in (1, 2):
                s = b + 2 * i + j
                step(split_hi, act, s, st, W, keep(s, (b + j) % 2, zb, (2 * i + j) * W, W))
        nl = B_IN - 6 * W
        step(split_hi, act, b + 5, st, nl, keep(b + 5, (b + 5) % 2, zb, 5 * W, W))
        step(split_hi, act, b + 6, st, W, keep(b + 6, b % 2, zb, 6 * W, nl), n=nl)
        with act.Fori(0, 2) as i:
            for j in (7, 8):
                s = b + 2 * i + j
                step(split_hi, act, s, st, W, keep(s, (b + j) % 2, za, (2 * i + j - 7) * W, W))
        step(split_hi, act, b + 11, st, W, keep(b + 11, (b + 11) % 2, za, 4 * W, W))
        step(split_hi, act, b + 12, st, None, keep(b + 12, (b + 12) % 2, za, 5 * W, W))

    def ab_in_pool(pool):

        def block_(i, slot, n, first):
            pool.wait_ge(sem("ev_ab_in"), i + 1)
            if not first:
                pool.wait_ge(sem("mixed"), i - 1)
            done = sem(f"shifted{slot}")
            c = bass.ds(i * W, n)
            pool.dma_start(mu[:, slot, 0:n], A["rwkv_mu"][0, c].partition_broadcast(P)).then_inc(done, 16)
            pool.memset(zprev[0:1, slot, 0, :], 0.0).then_inc(sem("zero_row"), 1)
            pool.dma_start(zprev[1:P, slot, :, 0:n], zb[0:P - 1, :, c]).then_inc(done, 16)
            pool.dma_start(zprev[0:1, slot, 1:2, 0:n], zb[P - 1:P, 0:1, c]).then_inc(done, 16)
        block_(0, 0, W, True)
        block_(1, 1, W, True)
        with pool.Fori(1, 3) as i:
            for j in range(2):
                block_(2 * i + j, j, W, False)
        block_(6, 0, B_IN - 6 * W, False)

    def ab_in_dve(dve, link):
        st, b = "ab_in", base["ab_in"]
        trig_dve(dve, link)
        prologue(split_lo, dve, st)
        h_first(dve, link, st, b, W, GAIN[st], prv[st])

        def mix(i, slot, n, k):
            def f():
                dve.wait_ge(sem(f"shifted{slot}"), 48 * k)
                dve.wait_ge(sem("zero_row"), i + 1)
                z, d = zb[:, :, bass.ds(i * W, n)], zprev[:, slot, :, 0:n]
                link(dve.tensor_tensor(d, d, z, ALU.subtract))
                link(dve.tensor_tensor(d, d, mu[:, slot, 0:n].unsqueeze(1).broadcast_to([P, TT, n]), ALU.mult))
                dve.tensor_tensor(z, z, d, ALU.add).then_inc(sem("mixed"), 1)
            return f
        nl = B_IN - 6 * W
        step(split_lo, dve, b, st, W, None, skip=True)
        with dve.Fori(0, 2) as i, link.loop(i, 0, 2, 4):
            for j in range(2):
                step(split_lo, dve, b + 2 * i + j + 1, st, W, mix(2 * i + j, j, W, i + 1))
        step(split_lo, dve, b + 5, st, nl, mix(4, 0, W, 3))
        step(split_lo, dve, b + 6, st, W, mix(5, 1, W, 3), n=nl)
        step(split_lo, dve, b + 7, st, W, mix(6, 0, nl, 4))
        with dve.Fori(8, 12) as i:
            step(split_lo, dve, b + i, st, W, None)
        step(split_lo, dve, b + 12, st, None, None)

    units = [(hd, tt) for tt in range(TT) for hd in range(A_HEADS)]
    qk_groups = [[za[:, tt, w * AW + hd * P:w * AW + (hd + 1) * P] for hd in (2 * g, 2 * g + 1) for tt in range(TT)]
                 for w in range(2) for g in range(4)]
    qk_outs = [((qT, kT)[w][:, 2 * g:2 * g + 2, :], P, 0, 512) for w in range(2) for g in range(4)]
    QB = (4, 5, 6, 7)

    def ab_attn_pool(pool):
        pool.wait_ge(mm_used, 4 * (base["ab_in"] + 13))
        pool.dma_start(subg[:], A["diff_subln_g"][0].partition_broadcast(P)).then_inc(sem("attn_in"), 16)
        for i, n in enumerate(("diff_lq1", "diff_lk1", "diff_lq2", "diff_lk2")):
            if i == 0:
                pool.wait_ge(sem("mixed"), 7)
            pool.dma_start(lqk[:, i, :], A[n][0].partition_broadcast(P)).then_inc(sem("attn_in"), 16)

    def ab_attn_pe(pe):
        tr_pe(pe, "qk", qk_groups, QB, [(sem("roped"), 1)])
        tr_all(pe, "qk", 8)
        n = len(units)
        for i in range(n + 2):
            if i < n:
                hd, tt = units[i]
                nk = (tt + 1) * P
                if i >= 2:
                    pe.wait_ge(sem("a_masked"), i - 1)
                for c in range(2):
                    r = slice(c * A_DC, (c + 1) * A_DC)
                    last = pe.matmul(bank[2 * (i % 2) + c][:, 0:nk], qT[r, hd, tt * P:(tt + 1) * P],
                                     kT[r, hd, 0:nk], start=True, stop=True)
                last.then_inc(sem("a_scores"), 1)
            if 0 <= i - 1 < n:
                hd, tt = units[i - 1]
                pe.wait_ge(sem("a_weights"), i)
                if i - 1 >= 2:
                    pe.wait_ge(sem("a_wT"), i - 2)
                for kb in range(tt + 1):
                    last = pe.transpose(bank[4 + (i - 1) % 2][:, kb * P:(kb + 1) * P],
                                        at_[:, (i - 1) % 2, kb * P:(kb + 1) * P], ident[:])
                last.then_inc(sem("a_wT_tr"), 1)
            if 0 <= i - 2 < n:
                hd, tt = units[i - 2]
                pe.wait_ge(sem("a_wT"), i - 1)
                if i - 2 >= 2:
                    pe.wait_ge(sem("a_y"), i - 3)
                for kb in range(tt + 1):
                    last = pe.matmul(bank[6 + i % 2][:, 0:P], atT[:, i % 2, kb, :],
                                     za[:, kb, 2 * AW + hd * P:2 * AW + (hd + 1) * P],
                                     start=(kb == 0), stop=(kb == tt))
                last.then_inc(sem("a_pv"), 1)

    def ab_attn_act(act):
        act.wait_ge(sem("lam_sums"), 1)
        act.activation(lam[:, 0:2], lam[:, 0:2], ACT.Exp).then_inc(sem("lam_exp"), 1)
        tr_out(act, "qk", qk_outs, QB, 0)
        n = len(units)
        for i in range(n + 2):
            if i < n:
                hd, tt = units[i]
                nk = (tt + 1) * P
                act.wait_ge(sem("a_max"), i + 1)
                for c in range(2):
                    act.activation(pe_[:, i % 2, c, 0:nk], sm[:, i % 2, c, 0:nk], ACT.Exp,
                                   bias=mx[:, i % 2, 2 + c:3 + c],
                                   accum_out=mx[:, i % 2, 4 + c:5 + c]).then_inc(sem("a_exp"), 1)
            if 0 <= i - 1 < n:
                hd, tt = units[i - 1]
                act.wait_ge(sem("a_wT_tr"), i)
                if i - 1 >= 2:
                    act.wait_ge(sem("a_pv"), i - 2)
                act.activation(atT[:, (i - 1) % 2, 0:tt + 1, :], bank[4 + (i - 1) % 2][:, 0:(tt + 1) * P],
                               ACT.Copy).then_inc(sem("a_wT"), 1)
            if 0 <= i - 2 < n:
                hd, tt = units[i - 2]
                act.wait_ge(sem("a_pv"), i - 1)
                act.activation(za[:, tt, hd * P:(hd + 1) * P], bank[6 + i % 2][:, 0:P],
                               ACT.Copy).then_inc(sem("a_y"), 1)

    def ab_attn_dve(dve, link):
        dve.wait_ge(sem("attn_in"), 80)
        for i in range(2):
            link(dve.tensor_tensor(lqk[:, 2 * i, :], lqk[:, 2 * i, :], lqk[:, 2 * i + 1, :], ALU.mult))
            last = dve.tensor_reduce(lam[:, i:i + 1], lqk[:, 2 * i, :], AX.X, ALU.add)
            if i == 0:
                link(last)
        last.then_inc(sem("lam_sums"), 1)
        dve.wait_ge(sem("ev_ab_in"), 13)
        dve.wait_ge(sem("trig"), 2)
        for tt in range(TT):
            x = za[:, tt, 0:2 * AW].rearrange("p (h d) -> p h d", d=A_DC)
            last = rope(dve, link, x, tt, 0, HALF_A, rt)
            if tt == 0:
                link(last)
        last.then_inc(sem("roped"), 1)
        tr_out(dve, "qk", qk_outs, QB, 1)
        dve.wait_ge(sem("lam_exp"), 1)
        link(dve.tensor_tensor(lam[:, 2:3], lam[:, 1:2], lam[:, 0:1], ALU.subtract))
        link(dve.tensor_scalar(lam[:, 2:3], lam[:, 2:3], -LAMBDA_INIT, None, ALU.add))
        n = len(units)
        for i in range(n + 1):
            if i < n:
                hd, tt = units[i]
                nk = (tt + 1) * P
                dve.wait_ge(sem("a_scores"), i + 1)
                cb = causal[:, T - nk:T].unsqueeze(1).broadcast_to([P, 2, nk])
                b0 = 1024 * (i % 2)
                x = psum[:, b0:b0 + 1024].rearrange("p (c k) -> p c k", c=2)[:, :, 0:nk]
                y = sm[:, i % 2, :, 0:nk]
                ins = dve.scalar_tensor_tensor(out=y, in0=x, scalar=A_DC ** -0.5, in1=cb, op0=ALU.mult, op1=ALU.add)
                ins.then_inc(sem("a_masked"), 1)
                dve.wait_ge(sem("a_masked"), i + 1)
                link(dve.tensor_reduce(mx[:, i % 2, 0:2], y, AX.X, ALU.max))
                dve.tensor_scalar(mx[:, i % 2, 2:4], mx[:, i % 2, 0:2], -1.0, None,
                                  ALU.mult).then_inc(sem("a_max"), 1)
            if i >= 1:
                u = i - 1
                hd, tt = units[u]
                nk = (tt + 1) * P
                dve.wait_ge(sem("a_exp"), 2 * u + 2)
                rl = mx[:, u % 2, 6:8]
                link(dve.reciprocal(rl, mx[:, u % 2, 4:6]))
                link(dve.tensor_scalar(rl[:, 1:2], rl[:, 1:2], lam[:, 2:3], None, ALU.mult))
                if u >= 2:
                    dve.wait_ge(sem("a_wT_tr"), u - 1)
                link(dve.tensor_scalar(at_[:, u % 2, 0:nk], pe_[:, u % 2, 0, 0:nk], rl[:, 0:1], None, ALU.mult))
                dve.scalar_tensor_tensor(out=at_[:, u % 2, 0:nk], in0=pe_[:, u % 2, 1, 0:nk], scalar=rl[:, 1:2],
                                         in1=at_[:, u % 2, 0:nk], op0=ALU.mult,
                                         op1=ALU.add).then_inc(sem("a_weights"), 1)
        dve.wait_ge(sem("a_y"), n)
        y = za[:, :, 0:AW].rearrange("p t (h d) -> p t h d", d=A_DV)
        y2 = asq[:].rearrange("p t (h d) -> p t h d", d=A_DV)
        r = s16[:, :, 0:A_HEADS]
        link(dve.tensor_tensor(asq[:], za[:, :, 0:AW], za[:, :, 0:AW], ALU.mult))
        link(dve.tensor_reduce(r16[:].rearrange("p (t h) -> p t h", t=TT), y2, AX.X, ALU.add))
        link(dve.tensor_scalar(r16[:], r16[:], 1.0 / A_DV, SUBLN_EPS, ALU.mult, ALU.add))
        link(rsqrt(dve, link, r16[:]))
        link(dve.tensor_scalar(r16[:], r16[:], 1.0 - LAMBDA_INIT, None, ALU.mult))
        for tt in range(TT):
            yt = y[:, tt]
            link(dve.tensor_tensor(yt, yt, r16[:, tt * 8:tt * 8 + 8].unsqueeze(2).broadcast_to([P, 8, A_DV]), ALU.mult))
            last = dve.tensor_tensor(yt, yt, subg[:].unsqueeze(1).broadcast_to([P, 8, A_DV]), ALU.mult)
        last.then_inc(sem("ya_done"), 1)
    t1 = at("t1", [P, TT, BW], F32, 96)
    rv, kv, vv = (zb[:, :, i * BW:(i + 1) * BW] for i in range(3))
    heads4 = lambda x: x.rearrange("p t (h c) -> p t h c", c=BH)
    over_t = lambda x: x[:].unsqueeze(1).broadcast_to([P, TT, BW])
    over_c = lambda x: x[:].unsqueeze(3).broadcast_to([P, TT, B_HEADS, BH])
    jobs = [(w, tt, hf) for w in range(3) for tt in range(TT) for hf in range(2)]
    lnx_g = at("lnx_g", [P, BW], F32, 195.5)
    lnx_b = at("lnx_b", [P, BW], F32, 199.5)
    XB = (4, 5, 6, 7)
    x_src = (kkv[:], av[:], kv, rv)

    def x_groups(tt):
        return [[x_src[i][:, tt, (4 * g + p) * P:(4 * g + p + 1) * P] for p in range(4)]
                for i in range(4) for g in range(2)]
    x_outs = [(XT[i][:, 4 * g:4 * g + 4, :], P, 0, 512) for i in range(4) for g in range(2)]
    slot_of = lambda hd: ((hd // 8) * 2 + hd % 2) * 4 + (hd // 2) % 4
    DV, DL = 14, 9

    def rwkv_pool(pool):
        pool.wait_ge(sem("ya_done"), 1)
        done = sem("lora_in")
        pool.dma_start(w2[0:LW, :], A["rwkv_w2"][0]).then_inc(done, 16)
        pool.dma_start(a2[0:LA, :], A["rwkv_a2"][0]).then_inc(done, 16)
        pool.dma_start(g2[:], A["rwkv_g2"][0].rearrange("(k p) n -> p k n", p=P)).then_inc(done, 16)
        for dst, n in ((p_w0, "rwkv_w0"), (p_a0, "rwkv_a0"), (p_kk, "rwkv_k_k"), (par, "rwkv_k_a")):
            pool.dma_start(dst[:], A[n][0].partition_broadcast(P)).then_inc(done, 16)
        pool.wait_ge(sem("rw_sum"), 4)
        pool.dma_start(p_w0[:], A["rwkv_r_k"][0].rearrange("h c -> (h c)").partition_broadcast(P))\
            .then_inc(sem("rk_in"), 16)
        pool.wait_ge(sem("rw_b"), 1)
        pool.memset(ST[:], 0.0).then_inc(sem("st_zero"), 1)
        for tt in range(TT):
            for gp in range(2):
                rd = 2 * tt + gp
                bc = lambda x: x.unsqueeze(1).broadcast_to([P, 4, P])
                for s in range(2):
                    g = 2 * gp + s
                    MT, Ti, Y1, Lm = tmp_set[s]
                    pool.wait_ge(sem(f"dv{s}"), DV * rd + 1)
                    T_ = TTi[:, 4 * g:4 * g + 4, :]
                    pool.tensor_tensor(T_, MT[:], bc(m_lv[:, 0, :]), ALU.mult).then_inc(sem("tt_m"), 1)
                    pool.wait_ge(sem("tt_m"), 2 * rd + s + 1)
                    pool.tensor_tensor(T_, T_, bc(ident[:]), ALU.add).then_inc(sem(f"lm{s}"), 1)
                for li in range(1, 6):
                    for s in range(2):
                        MT, Ti, Y1, Lm = tmp_set[s]
                        if li > 1:
                            pool.wait_ge(sem(f"y1_{s}"), 5 * rd + li - 1)
                        pool.tensor_tensor(Lm[:], MT[:], bc(m_lv[:, li, :]), ALU.mult).then_inc(sem(f"lm{s}"), 1)
            if tt == 1:
                tr_all(pool, "x1", 8)
                pool.dma_start(lnx_g[:], A["rwkv_lnx_g"][0].partition_broadcast(P)).then_inc(sem("lnx_in"), 16)
                pool.dma_start(lnx_b[:], A["rwkv_lnx_b"][0].partition_broadcast(P)).then_inc(sem("lnx_in"), 16)

    def rwkv_pe(pe):
        pe.wait_ge(sem("lora_act"), 2)
        pe.wait_ge(sem("a_y"), 16)
        cuts = (0, LW, LW + LA, LW + LA + P, LW + LA + 2 * P)
        for tt in range(TT):
            for j in range(4):
                x = zb[:, tt, 3 * BW + cuts[j]:3 * BW + cuts[j + 1]]
                last = pe.transpose(bank[tt][0:cuts[j + 1] - cuts[j], j * P:(j + 1) * P], x, ident[:])
            last.then_inc(sem("lora_tr"), 1)
        pe.wait_ge(sem("lora_T"), 2)
        pe.wait_ge(sem("lora_in"), 112)
        for n, (w, tt, hf) in enumerate(jobs):
            if n >= 4:
                pe.wait_ge(sem("rw_sum"), n - 3)
            o, c, t = bank[2 + n % 4][:], slice(hf * 512, hf * 512 + 512), slice(tt * P, (tt + 1) * P)
            if w < 2:
                last = pe.matmul(o, loraT[0:LW, w, t], (w2, a2)[w][0:LW, c], start=True, stop=True)
            else:
                pe.matmul(o, loraT[:, 2, t], g2[:, 0, c], start=True, stop=False)
                last = pe.matmul(o, loraT[:, 3, t], g2[:, 1, c], start=False, stop=True)
            last.then_inc(sem("lora_mm"), 1)
        pe.wait_ge(sem("rw_g"), 4)
        pe.wait_ge(sem("rw_lw"), 1)
        for tt in range(TT):
            for hf in range(2):
                pe.matmul(bank[2 * tt + hf][:], m_ui[:], lw[:, tt, hf * 512:(hf + 1) * 512], start=True, stop=True)
        for p in range(8):
            for tt in range(TT):
                last = pe.matmul(bank[6][:, 4 * p + 2 * tt:4 * p + 2 * tt + 2], lw[:, tt, p * P:(p + 1) * P],
                                 m_ui[:, CH - 1:P:CH], start=True, stop=True)
        last.then_inc(sem("cum"), 1)
        for tt in range(TT):
            c0 = 2 * tt
            if tt == 0:
                w = [(sem("rw_x"), 4), (sem("ex"), 3), (sem("rw_prev"), 1)]
            else:
                w = [(sem("y_out0"), 2), (sem("y_out1"), 2), (sem("st_upd"), 2)]
            tr_pe(pe, f"x{tt}", x_groups(tt), XB, w)
            tr_all(pe, f"x{tt}", 8)
            AT, BT, KT_, RT = XT
            for gp in range(2):
                rd = 2 * tt + gp
                if gp == 1:
                    for s in range(2):
                        pe.wait_ge(sem(f"dv{s}"), DV * rd)
                        pe.wait_ge(sem(f"y1c{s}"), 5 * rd)
                plan_ = ((BT, AT, 0), (AT, BT, 1), (KT_, AT, 2), (BT, RT, 3))
                for s in range(2):
                    r = slice(64 * s, 64 * s + 64)
                    for l_, r_, bk in plan_:
                        for i in range(4):
                            last = pe.matmul(bank[4 * s + bk][:, i * P:(i + 1) * P], l_[r, 4 * gp + i, :],
                                             r_[r, 4 * gp + i, :], start=True, stop=True)
                        last.then_inc(sem(f"mats{s}"), 1)
                for s in range(2):
                    r = slice(64 * s, 64 * s + 64)
                    pe.wait_ge(sem(f"dv{s}"), DV * rd + 2)
                    for i in range(4):
                        last = pe.matmul(bank[4 * s + 1][:, i * P:(i + 1) * P], KT_[r, 4 * gp + i, :],
                                         RT[r, 4 * gp + i, :], start=True, stop=True)
                    last.then_inc(sem(f"mats{s}"), 1)
                for li in range(1, 6):
                    for s in range(2):
                        MT, Ti, Y1, Lm = tmp_set[s]
                        pe.wait_ge(sem(f"lm{s}"), 6 * rd + 1 + li)
                        if li > 1:
                            pe.wait_ge(sem(f"dv{s}"), DV * rd + 5 + 2 * (li - 1))
                        for i in range(4):
                            last = pe.matmul(bank[4 * s][:, i * P:(i + 1) * P], Lm[:, i, :], Ti[:, i, :],
                                             start=True, stop=True)
                        last.then_inc(sem(f"y1_{s}"), 1)
                    for s in range(2):
                        g = 2 * gp + s
                        MT, Ti, Y1, Lm = tmp_set[s]
                        pe.wait_ge(sem(f"y1c{s}"), 5 * rd + li)
                        if li == 1:
                            pe.wait_ge(sem(f"dv{s}"), DV * rd + 4)
                        if li < 5:
                            for i in range(4):
                                last = pe.matmul(bank[4 * s + 2][:, i * P:(i + 1) * P], TTi[:, 4 * g + i, :],
                                                 Y1[:, i, :], start=True, stop=True)
                            last.then_inc(sem(f"dl{s}"), 1)
                        for i in range(4):
                            last = pe.matmul(bank[4 * s + 3][:, i * P:(i + 1) * P], Y1[:, i, :],
                                             TTi[:, 4 * g + i, :], start=True, stop=True)
                        last.then_inc(sem(f"dl{s}"), 1)
            for s in range(2):
                pe.wait_ge(sem(f"dv{s}"), DV * (2 * tt + 2))
                pe.wait_ge(sem(f"y1c{s}"), 5 * (2 * tt + 2))
            pe.wait_ge(sem("st_zero"), 1)
            for half in range(2):
                c = 2 * tt + half
                if c:
                    pe.wait_ge(sem("st_upd"), c)
                    pe.wait_ge(sem("u_out1"), c)
                for p in range(8):
                    o = bank[p // 4][:, (p % 4) * P:(p % 4 + 1) * P]
                    pe.matmul(o, AT[:, p, :], ST[:, p, :], start=True, stop=False)
                    for e in range(2):
                        hd = 2 * p + e
                        last = pe.matmul(o[:, e * BH:(e + 1) * BH], NT[:, slot_of(hd), :],
                                         vv[:, tt, hd * BH:(hd + 1) * BH], start=False, stop=(e == 1))
                    if p % 4 == 3:
                        last.then_inc(sem("x_mm"), 1)
                for hd in range(16):
                    if hd % 8 == 0:
                        pe.wait_ge(sem(f"x_out{hd // 8}"), c + 1)
                    last = pe.matmul(bank[2 + hd // 8][:, (hd % 8) * BH:(hd % 8 + 1) * BH], TTi[:, slot_of(hd), :],
                                     Xs[:, hd * BH:(hd + 1) * BH], start=True, stop=True)
                    if hd % 8 == 7:
                        last.then_inc(sem("u_mm"), 1)
                if c < 3:
                    rows = slice(64 * half, 64 * half + 64)
                    for p in range(8):
                        if p % 4 == 0:
                            pe.wait_ge(sem(f"u_out{p // 4}"), c + 1)
                        o, cc = bank[6 + p // 4][:, (p % 4) * P:(p % 4 + 1) * P], slice(p * P, (p + 1) * P)
                        pe.matmul(o, av[rows, tt, cc], Us[rows, cc], start=True, stop=False)
                        last = pe.matmul(o, kv[rows, tt, cc], vv[rows, tt, cc], start=False, stop=True)
                    last.then_inc(sem("s_mm"), 1)
                else:
                    for e in range(2):
                        pe.wait_ge(sem(f"u_out{e}"), c + 1)
                if half:
                    pe.wait_ge(sem("y_out0"), c)
                    pe.wait_ge(sem("y_out1"), c)
                for p in range(8):
                    o = bank[4 + p // 4][:, (p % 4) * P:(p % 4 + 1) * P]
                    pe.matmul(o, RT[:, p, :], ST[:, p, :], start=True, stop=False)
                    for e in range(2):
                        hd = 2 * p + e
                        oh, cc = o[:, e * BH:(e + 1) * BH], slice(hd * BH, (hd + 1) * BH)
                        pe.matmul(oh, PT[:, slot_of(hd), :], Us[:, cc], start=False, stop=False)
                        last = pe.matmul(oh, QT[:, slot_of(hd), :], vv[:, tt, cc], start=False, stop=(e == 1))
                    if p % 4 == 3:
                        last.then_inc(sem("y_mm"), 1)

    def rwkv_act(act):
        act.wait_ge(sem("mixed"), 7)
        x = zb[:, :, 3 * BW:3 * BW + LW]
        act.activation(x, x, ACT.Tanh).then_inc(sem("lora_act"), 1)
        x = zb[:, :, 3 * BW + LW + LA:B_IN]
        act.activation(x, x, ACT.Sigmoid).then_inc(sem("lora_act"), 1)
        for tt in range(TT):
            act.wait_ge(sem("lora_tr"), tt + 1)
            if tt == 0:
                act.wait_ge(sem("ya_done"), 1)
            t = slice(tt * P, (tt + 1) * P)
            b2 = bank[tt].rearrange("p (j t) -> p j t", j=4)
            act.activation(loraT[0:LW, 0:2, t], b2[0:LW, 0:2, :], ACT.Copy)
            act.activation(loraT[:, 2:4, t], b2[:, 2:4, :], ACT.Copy).then_inc(sem("lora_T"), 1)
        for w, x in enumerate((lw, av)):
            act.wait_ge(sem("rw_sum"), 4 * w + 4)
            act.activation(x[:], x[:], ACT.Sigmoid).then_inc(sem("rw_sig"), 1)
        for n in range(8, 12):
            _, tt, hf = jobs[n]
            act.wait_ge(sem("lora_mm"), n + 1)
            act.activation(gv[:, tt, hf * 512:(hf + 1) * 512], bank[2 + n % 4][:], ACT.Copy).then_inc(sem("rw_g"), 1)
        act.wait_ge(sem("cum"), 1)
        act.activation(ex1[:], psum[:, 0:4 * 512], ACT.Exp).then_inc(sem("ex"), 1)
        act.activation(ex2[:], psum[:, 0:4 * 512], ACT.Exp, scale=-1.0).then_inc(sem("ex"), 1)
        act.activation(WL[:], bank[6][:, 0:32], ACT.Exp).then_inc(sem("ex"), 1)
        act.wait_ge(sem("rw_prev"), 1)
        act.activation(lw[:], lw[:], ACT.Exp).then_inc(sem("ex"), 1)
        for tt in range(TT):
            tr_out(act, f"x{tt}", x_outs, XB, 0)
            for gp in range(2):
                rd = 2 * tt + gp
                for li in range(1, 6):
                    for s in range(2):
                        act.wait_ge(sem(f"y1_{s}"), 5 * rd + li)
                        act.activation(tmp_set[s][2][:], bank[4 * s][:], ACT.Copy).then_inc(sem(f"y1c{s}"), 1)
            for half in range(2):
                c = 2 * tt + half
                rows = slice(64 * half, 64 * half + 64)
                act.wait_ge(sem("x_mm"), 2 * c + 1)
                act.activation(Xs[:, 0:512], bank[0], ACT.Copy).then_inc(sem("x_out0"), 1)
                act.wait_ge(sem("u_mm"), 2 * c + 1)
                if c:
                    act.wait_ge(sem("y_mm"), 2 * c)
                act.activation(Us[:, 0:512], bank[2], ACT.Copy).then_inc(sem("u_out0"), 1)
                act.wait_ge(sem("y_mm"), 2 * c + 1)
                act.activation(zb[rows, tt, 0:512], bank[4][rows, :], ACT.Copy).then_inc(sem("y_out0"), 1)

    def rwkv_dve(dve, link):
        for n in range(8):
            w, tt, hf = jobs[n]
            c = slice(hf * 512, (hf + 1) * 512)
            dve.wait_ge(sem("lora_mm"), n + 1)
            dve.tensor_tensor((lw, av)[w][:, tt, c], bank[2 + n % 4][:], (p_w0, p_a0)[w][:, c],
                              ALU.add).then_inc(sem("rw_sum"), 1)
        dve.wait_ge(sem("rw_sig"), 1)
        dve.tensor_scalar(lw[:], lw[:], -math.exp(-0.5), None, ALU.mult).then_inc(sem("rw_lw"), 1)
        link(dve.tensor_tensor(kkv[:], kv, over_t(p_kk), ALU.mult))
        link(dve.tensor_tensor(t1[:], kkv[:], kkv[:], ALU.mult))
        n32 = nrm[:].rearrange("p t h -> p (t h)")
        link(dve.tensor_reduce(nrm[:], heads4(t1[:]), AX.X, ALU.add))
        link(dve.tensor_scalar(n32, n32, 1e-24, None, ALU.max))
        link(rsqrt(dve, link, n32))
        link(dve.tensor_tensor(heads4(kkv[:]), heads4(kkv[:]), over_c(nrm), ALU.mult))
        dve.wait_ge(sem("rw_sig"), 2)
        link(dve.tensor_scalar(t1[:], av[:], -1.0, None, ALU.add))
        link(dve.tensor_tensor(t1[:], t1[:], over_t(par), ALU.mult))
        link(dve.scalar_tensor_tensor(out=kv, in0=t1[:], scalar=1.0, in1=kv, op0=ALU.add, op1=ALU.mult))
        dve.tensor_tensor(av[:], kkv[:], av[:], ALU.mult).then_inc(sem("rw_b"), 1)
        dve.wait_ge(sem("rw_b"), 1)
        link(dve.tensor_tensor(t1[:], rv, kv, ALU.mult))
        dve.wait_ge(sem("rk_in"), 16)
        link(dve.tensor_tensor(t1[:], t1[:], over_t(p_w0), ALU.mult))
        link(dve.tensor_reduce(bon[:], heads4(t1[:]), AX.X, ALU.add))
        dve.wait_ge(sem("ex"), 3)
        dve.tensor_tensor(lw[:], psum[:, 0:2048].rearrange("p (t n) -> p t n", t=TT), lw[:],
                          ALU.subtract).then_inc(sem("rw_prev"), 1)
        dve.tensor_tensor(rv, rv, ex1[:], ALU.mult).then_inc(sem("rw_x"), 1)
        dve.tensor_tensor(kv, kv, ex2[:], ALU.mult).then_inc(sem("rw_x"), 1)
        dve.tensor_tensor(av[:], av[:], ex2[:], ALU.mult).then_inc(sem("rw_x"), 1)
        dve.wait_ge(sem("ex"), 4)
        dve.scalar_tensor_tensor(out=kkv[:], in0=kkv[:], scalar=-1.0, in1=lw[:], op0=ALU.mult,
                                 op1=ALU.mult).then_inc(sem("rw_x"), 1)
        for tt in range(TT):
            if tt == 0:
                dve.wait_ge(sem("rw_x"), 4)
            tr_out(dve, f"x{tt}", x_outs, XB, 1)
            for gp in range(2):
                rd = 2 * tt + gp
                bc = lambda x: x.unsqueeze(1).broadcast_to([P, 4, P])
                b4 = lambda i: bank[i].rearrange("p (i t) -> p i t", i=4)
                for s in range(2):
                    MT, Ti, Y1, Lm = tmp_set[s]
                    dv = sem(f"dv{s}")
                    dve.wait_ge(sem(f"mats{s}"), 5 * rd + 1)
                    if rd:
                        dve.wait_ge(sem(f"lm{s}"), 6 * rd)
                    dve.tensor_tensor(MT[:], b4(4 * s), bc(m_su[:]), ALU.mult).then_inc(dv, 1)
                    dve.wait_ge(sem(f"mats{s}"), 5 * rd + 2)
                    link(dve.tensor_tensor(Ti[:], b4(4 * s + 1), bc(m_l1t[:]), ALU.mult))
                    dve.tensor_tensor(Ti[:], Ti[:], bc(ident[:]), ALU.add).then_inc(dv, 1)
                for s in range(2):
                    g = 2 * gp + s
                    dv = sem(f"dv{s}")
                    sl = slice(4 * g, 4 * g + 4)
                    dve.wait_ge(sem(f"mats{s}"), 5 * rd + 4)
                    dve.tensor_tensor(NT[:, sl, :], b4(4 * s + 2), bc(m_su[:]), ALU.mult).then_inc(dv, 1)
                    dve.tensor_tensor(PT[:, sl, :], b4(4 * s + 3), bc(m_ui[:]), ALU.mult).then_inc(dv, 1)
                    dve.wait_ge(sem(f"mats{s}"), 5 * rd + 5)
                    dve.tensor_tensor(QT[:, sl, :], b4(4 * s + 1), bc(m_ui[:]), ALU.mult).then_inc(dv, 1)
                for li in range(1, 6):
                    for s in range(2):
                        g = 2 * gp + s
                        MT, Ti, Y1, Lm = tmp_set[s]
                        dv, T_ = sem(f"dv{s}"), TTi[:, 4 * g:4 * g + 4, :]
                        if li < 5:
                            dve.wait_ge(sem(f"dl{s}"), DL * rd + 2 * li)
                            dve.tensor_tensor(Ti[:], Ti[:], b4(4 * s + 2), ALU.add).then_inc(dv, 1)
                        else:
                            dve.wait_ge(sem(f"dl{s}"), DL * rd + 9)
                        dve.tensor_tensor(T_, T_, b4(4 * s + 3), ALU.add).then_inc(dv, 1)
            for half in range(2):
                c = 2 * tt + half
                rows = slice(64 * half, 64 * half + 64)
                dve.wait_ge(sem("x_mm"), 2 * c + 2)
                dve.tensor_copy(Xs[:, 512:1024], bank[1]).then_inc(sem("x_out1"), 1)
                dve.wait_ge(sem("u_mm"), 2 * c + 2)
                if c:
                    dve.wait_ge(sem("y_mm"), 2 * c)
                dve.tensor_copy(Us[:, 512:1024], bank[3]).then_inc(sem("u_out1"), 1)
                if c < 3:
                    dve.wait_ge(sem("s_mm"), c + 1)
                    dve.wait_ge(sem("y_mm"), 2 * c + 2)
                    dve.tensor_copy(zb[rows, tt, 512:1024], bank[5][rows, :]).then_inc(sem("y_out1"), 1)
                    for e in range(2):
                        r = slice(64 * e, 64 * e + 64)
                        s2 = ST[r, :, r]
                        x2 = psum[r, 6 * 512:8 * 512].rearrange("p (a t) -> p a t", a=8)[:, :, r]
                        link(dve.tensor_tensor(s2, s2, x2, ALU.add))
                        last = dve.tensor_tensor(s2, s2, WL[r, :, c:c + 1].broadcast_to([64, 8, 64]), ALU.mult)
                    last.then_inc(sem("st_upd"), 1)
                else:
                    dve.wait_ge(sem("y_mm"), 2 * c + 2)
                    dve.tensor_copy(zb[rows, tt, 512:1024], bank[5][rows, :]).then_inc(sem("y_out1"), 1)
        dve.wait_ge(sem("y_out0"), 4)
        dve.wait_ge(sem("y_out1"), 4)
        y4 = heads4(rv)
        link(dve.tensor_reduce(nrm[:], y4, AX.X, ALU.add))
        link(dve.tensor_scalar(n32, n32, -1.0 / BH, None, ALU.mult))
        link(dve.tensor_tensor(y4, y4, over_c(nrm), ALU.add))
        link(dve.tensor_tensor(t1[:], rv, rv, ALU.mult))
        link(dve.tensor_reduce(nrm[:], heads4(t1[:]), AX.X, ALU.add))
        link(dve.tensor_scalar(n32, n32, 1.0 / BH, LNX_EPS, ALU.mult, ALU.add))
        link(rsqrt(dve, link, n32))
        link(dve.tensor_tensor(y4, y4, over_c(nrm), ALU.mult))
        dve.wait_ge(sem("lnx_in"), 32)
        link(dve.tensor_tensor(rv, rv, over_t(lnx_g), ALU.mult))
        link(dve.tensor_tensor(rv, rv, over_t(lnx_b), ALU.add))
        link(dve.tensor_tensor(heads4(t1[:]), heads4(vv), over_c(bon), ALU.mult))
        link(dve.tensor_tensor(rv, rv, t1[:], ALU.add))
        dve.tensor_tensor(za[:, :, AW:2 * AW], rv, gv[:], ALU.mult).then_inc(sem("yb_done"), 1)

    C1, C2 = C_HEADS * C_HD, C_HEADS * C_HD + C_KV * C_HD
    C3 = C2 + C_KV * C_HD
    C4 = C3 + IDX_H * IDX_D
    C5 = C4 + IDX_D
    zc = at("zc", [P, TT, C_IN], F32, 120)
    qTc = at("qTc", [P, C_HEADS, T], F32, 153)
    kTc = at("kTc", [P, C_KV, T], F32, 169)
    qiT = at("qiT", [P, IDX_H // 2, T], F32, 173)
    kiT = at("kiT", [P, T], F32, 181)
    score = at("score", [P, TT, T], F32, 182)
    mb = at("mb", [P, TT, T], F32, 184)
    rl_ = at("rl_", [P, 2, 2, T], F32, 186)
    smc = at("smc", [P, 2, 2, T], F32, 190)
    pc = at("pc", [P, 2, 2, T], F32, 194)
    pcT = at("pcT", [P, 2, 4, P], F32, 198)
    kid = at("kid", [P, TT, P], F32, 202)
    rtc = at("rtc", [P, 4, 256], F32, 203)
    mxc = at("mxc", [P, 2, 8], F32, 16)
    m8 = at("m8", [P, 8], F32, 16.25)
    lns = at("lns", [P, 4], F32, 16.5)
    ikg = at("ikg", [P, 2, IDX_D], F32, 17)
    wis = at("wis", [P, TT, IDX_H], F32, 18)
    ki2 = at("ki2", [P, TT, IDX_D], F32, 19)
    qi_groups = [[zc[:, tt, C3 + hp * P:C3 + (hp + 1) * P] for hp in (2 * g, 2 * g + 1) for tt in range(TT)]
                 for g in range(4)] + [[kid[:, tt, :] for tt in range(TT)]]
    qi_outs = [(qiT[:, 2 * g:2 * g + 2, :], P, 0, 512) for g in range(4)] + [(kiT[:], P, 0, 256)]
    c_groups = [[zc[:, tt, hd * P:(hd + 1) * P] for hd in (2 * g, 2 * g + 1) for tt in range(TT)] for g in range(10)]
    c_outs = [(qTc[:, 2 * g:2 * g + 2, :], P, 0, 512) for g in range(8)] + \
             [(kTc[:, 2 * g:2 * g + 2, :], P, 0, 512) for g in range(2)]
    c_units = [(tt, hp) for tt in range(TT) for hp in range(8)]
    nu = len(c_units)

    def c_in_pe(pe):
        st, b = "c_in", base["c_in"]
        ev = sem("ev_c_in")
        pe_first(pe, st, b, b % 2, h_src, h_ready(st), C_W, free_of(st, 0))
        mm_slab(pe, b + 1, (b + 1) % 2, C_W, free_of(st, 1))
        with pe.Fori(1, 4) as i:
            for j in range(2):
                mm_slab(pe, b + 2 * i + j, (b + j) % 2, C_W, (ev, 2 * i + j - 1))
        mm_slab(pe, b + 8, b % 2, C_W, (ev, 7))

    def c_in_act(act):
        st, b = "c_in", base["c_in"]
        prologue(split_hi, act, st)
        act_first(act, st, b, C_W, GAIN[st], h_squares(act, st))

        def keep(i, par_):
            def f():
                act.wait_ge(mm_used, 4 * (b + i) + 4)
                for tt in range(TT):
                    last = act.activation(zc[:, tt, bass.ds(i * C_W, C_W)], bank[2 * par_ + tt][:, 0:C_W], ACT.Copy,
                                          scale=rstd_h[:, tt:tt + 1])
                last.then_inc(sem("ev_c_in"), 1)
            return f
        act.wait_ge(*mark("rstd", st, 1))
        step(split_hi, act, b, st, C_W, keep(0, b % 2), skip=True)
        step(split_hi, act, b + 1, st, C_W, keep(1, (b + 1) % 2))
        with act.Fori(1, 4) as i:
            for j in range(2):
                step(split_hi, act, b + 2 * i + j, st, C_W, keep(2 * i + j, (b + j) % 2))
        step(split_hi, act, b + 8, st, None, keep(8, b % 2))

    def c_in_dve(dve, link):
        st, b = "c_in", base["c_in"]
        prologue(split_lo, dve, st)
        h_first(dve, link, st, b, C_W, GAIN[st], prv[st])
        step(split_lo, dve, b, st, C_W, None, skip=True)
        with dve.Fori(1, 8) as i:
            step(split_lo, dve, b + i, st, C_W, None)
        step(split_lo, dve, b + 8, st, None, None)

    def c_pool(pool):
        pool.wait_ge(mm_used, 4 * (base["c_in"] + 9))
        for i, n in enumerate(("idx_k_g", "idx_k_b")):
            pool.dma_start(ikg[:, i, :], A[n][0].partition_broadcast(P)).then_inc(sem("ikg_in"), 16)

    def c_pe(pe):
        tr_pe(pe, "qi", qi_groups, QB, [(sem("qi_roped"), 1)])
        tr_all(pe, "qi", 5)
        for i, (tt, hp) in enumerate(c_units):
            nk = (tt + 1) * P
            if i >= 2:
                pe.wait_ge(sem("i_relu"), i - 1)
            for j in range(2):
                r = slice(64 * j, 64 * j + 64)
                last = pe.matmul(bank[2 * (i % 2) + j][:, 0:nk], qiT[r, hp, tt * P:(tt + 1) * P], kiT[r, 0:nk],
                                 start=True, stop=True)
            last.then_inc(sem("i_mm"), 1)
        tr_pe(pe, "qc", c_groups, QB, [(sem("qc_roped"), 1)])
        tr_all(pe, "qc", 10)
        pe.wait_ge(sem("i_relu"), nu)
        for i in range(nu + 2):
            if i < nu:
                tt, hp = c_units[i]
                nk = (tt + 1) * P
                if i >= 2:
                    pe.wait_ge(sem("c_masked"), i - 1)
                for j in range(2):
                    last = pe.matmul(bank[2 * (i % 2) + j][:, 0:nk], qTc[:, 2 * hp + j, tt * P:(tt + 1) * P],
                                     kTc[:, hp // 2, 0:nk], start=True, stop=True)
                last.then_inc(sem("c_scores"), 1)
            if 0 <= i - 1 < nu:
                u = i - 1
                tt, hp = c_units[u]
                pe.wait_ge(sem("c_exp"), 2 * u + 2)
                if u >= 2:
                    pe.wait_ge(sem("c_wT"), u - 1)
                for j in range(2):
                    for kb in range(tt + 1):
                        q = j * (tt + 1) + kb
                        last = pe.transpose(bank[4 + u % 2][:, q * P:(q + 1) * P], pc[:, u % 2, j, kb * P:(kb + 1) * P],
                                            ident[:])
                last.then_inc(sem("c_tr"), 1)
            if 0 <= i - 2 < nu:
                u = i - 2
                tt, hp = c_units[u]
                pe.wait_ge(sem("c_wT"), u + 1)
                if u >= 2:
                    pe.wait_ge(sem("c_y"), u - 1)
                for j in range(2):
                    for kb in range(tt + 1):
                        last = pe.matmul(bank[6 + u % 2][:, j * P:(j + 1) * P], pcT[:, u % 2, j * (tt + 1) + kb, :],
                                         zc[:, kb, C2 + (hp // 2) * P:C2 + (hp // 2 + 1) * P],
                                         start=(kb == 0), stop=(kb == tt))
                last.then_inc(sem("c_pv"), 1)

    def c_act(act):
        tr_out(act, "qi", qi_outs, QB, 0)
        for i, (tt, hp) in enumerate(c_units):
            nk = (tt + 1) * P
            act.wait_ge(sem("i_mm"), i + 1)
            if i >= 2:
                act.wait_ge(sem("i_added"), 2 * (i - 1))
            x = psum[:, 1024 * (i % 2):1024 * (i % 2) + 1024].rearrange("p (c k) -> p c k", c=2)[:, :, 0:nk]
            act.activation(rl_[:, i % 2, :, 0:nk], x, ACT.Relu).then_inc(sem("i_relu"), 1)
        tr_out(act, "qc", c_outs, QB, 0)
        for i in range(nu + 2):
            if i < nu:
                tt, hp = c_units[i]
                nk = (tt + 1) * P
                act.wait_ge(sem("c_max"), i + 1)
                for j in range(2):
                    act.activation(pc[:, i % 2, j, 0:nk], smc[:, i % 2, j, 0:nk], ACT.Exp,
                                   bias=mxc[:, i % 2, 2 + j:3 + j],
                                   accum_out=mxc[:, i % 2, 4 + j:5 + j]).then_inc(sem("c_exp"), 1)
            if 0 <= i - 2 < nu:
                u = i - 2
                tt, hp = c_units[u]
                act.wait_ge(sem("c_pv"), u + 1)
                act.wait_ge(sem("c_rl"), u + 1)
                for j in range(2):
                    hd = 2 * hp + j
                    last = act.activation(zc[:, tt, hd * P:(hd + 1) * P], bank[6 + u % 2][:, j * P:(j + 1) * P],
                                          ACT.Copy, scale=rlc[:, u % 4, j:j + 1])
                last.then_inc(sem("c_y"), 1)

    rlc = at("rlc", [P, 4, 2], F32, 16.75)

    def c_dve(dve, link):
        dve.wait_ge(sem("ev_c_in"), 9)
        dve.wait_ge(mm_used, 4 * (base["c_in"] + 9))
        dve.wait_ge(sem("trig"), 2)
        x = zc[:, :, C4:C5]
        over64 = lambda v: v.unsqueeze(2).broadcast_to([P, TT, IDX_D])
        mean, var = lns[:, 0:2], lns[:, 2:4]
        link(dve.tensor_reduce(mean, x, AX.X, ALU.add))
        link(dve.tensor_scalar(mean, mean, -1.0 / IDX_D, None, ALU.mult))
        link(dve.tensor_tensor(x, x, over64(mean), ALU.add))
        link(dve.tensor_tensor(ki2[:], x, x, ALU.mult))
        link(dve.tensor_reduce(var, ki2[:], AX.X, ALU.add))
        link(dve.tensor_scalar(var, var, 1.0 / IDX_D, LN_EPS, ALU.mult, ALU.add))
        link(rsqrt(dve, link, var))
        link(dve.tensor_tensor(x, x, over64(var), ALU.mult))
        dve.wait_ge(sem("ikg_in"), 32)
        link(dve.tensor_tensor(x, x, ikg[:, 0, :].unsqueeze(1).broadcast_to([P, TT, IDX_D]), ALU.mult))
        link(dve.tensor_tensor(x, x, ikg[:, 1, :].unsqueeze(1).broadcast_to([P, TT, IDX_D]), ALU.add))
        link(dve.tensor_scalar(wis[:], zc[:, :, C5:C_IN], float((IDX_H * IDX_D) ** -0.5), None, ALU.mult))
        for tt in range(TT):
            link(rope(dve, link, zc[:, tt, C4:C5].unsqueeze(1), tt, 0, HALF_A, rtc))
            link(rope(dve, link, zc[:, tt, C3:C4].rearrange("p (h d) -> p h d", d=IDX_D), tt, 0, HALF_A, rtc))
            for j in range(2):
                last = dve.tensor_copy(kid[:, tt, j * 64:(j + 1) * 64], zc[:, tt, C4:C5])
        last.then_inc(sem("qi_roped"), 1)
        tr_out(dve, "qi", qi_outs, QB, 1)
        for tt in range(TT):
            link(rope(dve, link, zc[:, tt, 0:C1].rearrange("p (h d) -> p h d", d=C_HD), tt, HALF_A, HALF_C, rtc))
            last = rope(dve, link, zc[:, tt, C1:C2].rearrange("p (h d) -> p h d", d=C_HD), tt, HALF_A, HALF_C, rtc)
            if tt == 0:
                link(last)
        last.then_inc(sem("qc_roped"), 1)
        added = sem("i_added")
        for i, (tt, hp) in enumerate(c_units):
            nk = (tt + 1) * P
            dve.wait_ge(sem("i_relu"), i + 1)
            for j in range(2):
                w_, sc, x = wis[:, tt, 2 * hp + j:2 * hp + j + 1], score[:, tt, 0:nk], rl_[:, i % 2, j, 0:nk]
                if hp + j == 0:
                    dve.tensor_scalar(sc, x, w_, None, ALU.mult).then_inc(added, 1)
                else:
                    dve.scalar_tensor_tensor(out=sc, in0=x, scalar=w_, in1=sc, op0=ALU.mult,
                                             op1=ALU.add).then_inc(added, 1)
                dve.wait_ge(added, 2 * i + j + 1)
        tr_out(dve, "qc", c_outs, QB, 1)
        for tt in range(TT):
            nk = (tt + 1) * P
            sc, ca = score[:, tt, 0:nk], causal[:, T - nk:T]
            link(dve.tensor_tensor(sc, sc, ca, ALU.add))
            for _ in range(TOPK // 8):
                link(dve.max(m8[:], sc))
                link(dve.match_replace(sc, m8[:], sc, TAKEN))
            link(dve.tensor_scalar(mb[:, tt, 0:nk], sc, TAKEN / 2, NEG, ALU.is_gt, ALU.mult))
            link(dve.tensor_tensor(mb[:, tt, 0:nk], mb[:, tt, 0:nk], ca, ALU.add))
        for i in range(nu + 1):
            if i < nu:
                tt, hp = c_units[i]
                nk = (tt + 1) * P
                dve.wait_ge(sem("c_scores"), i + 1)
                if i >= 2:
                    dve.wait_ge(sem("c_exp"), 2 * (i - 1))
                x = psum[:, 1024 * (i % 2):1024 * (i % 2) + 1024].rearrange("p (c k) -> p c k", c=2)[:, :, 0:nk]
                y = smc[:, i % 2, :, 0:nk]
                dve.scalar_tensor_tensor(out=y, in0=x, scalar=C_HD ** -0.5,
                                         in1=mb[:, tt, 0:nk].unsqueeze(1).broadcast_to([P, 2, nk]), op0=ALU.mult,
                                         op1=ALU.add).then_inc(sem("c_masked"), 1)
                dve.wait_ge(sem("c_masked"), i + 1)
                link(dve.tensor_reduce(mxc[:, i % 2, 0:2], y, AX.X, ALU.max))
                dve.tensor_scalar(mxc[:, i % 2, 2:4], mxc[:, i % 2, 0:2], -1.0, None,
                                  ALU.mult).then_inc(sem("c_max"), 1)
            if i >= 1:
                u = i - 1
                tt, hp = c_units[u]
                dve.wait_ge(sem("c_exp"), 2 * u + 2)
                if u >= 4:
                    dve.wait_ge(sem("c_y"), u - 3)
                dve.reciprocal(rlc[:, u % 4, :], mxc[:, u % 2, 4:6]).then_inc(sem("c_rl"), 1)
                dve.wait_ge(sem("c_tr"), u + 1)
                if u >= 2:
                    dve.wait_ge(sem("c_pv"), u - 1)
                nq = 2 * (tt + 1)
                dve.tensor_copy(pcT[:, u % 2, 0:nq, :], bank[4 + u % 2][:, 0:nq * P]).then_inc(sem("c_wT"), 1)

    def y_src(st):
        y = za if st == "ab_out" else zc
        return lambda tt, b: y[:, tt, b * W:(b + 1) * W]

    def y_ready(st):
        if st == "ab_out":
            return lambda tt, b: (sem("ya_done" if b < 2 else "yb_done"), 1)
        return lambda tt, b: (sem("c_y"), nu)

    mats = {"ab_in": A["ab_w_in"][0], "ab_out": A["ab_w_out"][0], "c_in": A["c_w_in"][0], "c_out": A["c_w_out"][0]}
    end = order[-1]
    block = ctx.enter_context(nc.Block())

    @block.sync
    def _(sp):
        sp.dma_start(h[:], A["x"][0].rearrange("(t p) d -> p t d", p=P)).then_inc(sem("x_in"), 16)
        for st in order:
            b = base[st]
            if st.startswith("mlp"):
                l = int(st[-1])
                up = A["w_mlp_up"][l]
                down = A["w_mlp_down"][l]

                def quarter(Q, first):
                    for j in range(4):
                        load_slab(sp, b + 8 * Q + j, w_chunks(up, 0), Q * 4 * W + j * W, W, first and j == 0)
                    for j in range(4):
                        load_slab(sp, b + 8 * Q + 4 + j, w_chunks(down, Q), j * W, W)
                quarter(0, b == 0)
                with sp.Fori(1, 4) as Q:
                    quarter(Q, False)
            elif st.startswith("ple"):
                for j in range(4):
                    load_slab(sp, b + j, w_chunks(A["w_ple_gate"][int(st[-1])], 0), j * W, W, b + j == 0)
            elif st == "ab_in":
                w = w_chunks(mats[st], 0)
                load_slab(sp, b, w, A_IN, W, b == 0)
                with sp.Fori(1, 6) as i:
                    load_slab(sp, b + i, w, A_IN + i * W, W)
                load_slab(sp, b + 6, w, A_IN + 6 * W, B_IN - 6 * W)
                with sp.Fori(0, 6) as i:
                    load_slab(sp, b + 7 + i, w, i * W, W)
            elif st == "c_in":
                w = w_chunks(mats[st], 0)
                load_slab(sp, b, w, 0, C_W, b == 0)
                with sp.Fori(1, 9) as i:
                    load_slab(sp, b + i, w, i * C_W, C_W)
            else:
                for j in range(4):
                    load_slab(sp, b + j, w_chunks(mats[st], 0), j * W, W)
        for tt in range(TT):
            sp.wait_ge(*mark("h_ready", "end", 8))
            sp.dma_start(A["out"][0][tt * P:(tt + 1) * P, :], h[:, tt, :]).then_inc(sem("stored"), 16)
        sp.wait_ge(sem("stored"), 32)

    @block.gpsimd
    def _(pool):
        pool_setup(pool)
        for st in order:
            if st == "ab_in":
                ab_in_pool(pool)
                ab_attn_pool(pool)
                rwkv_pool(pool)
            if st == "c_in":
                c_pool(pool)
            if st.startswith("ple"):
                l = int(st[-1])
                if prv[st]:
                    pool.wait_ge(*mark("xT_lo", prv[st], 8))
                pool.dma_start(wple[:], A["w_ple_proj"][l].rearrange("(k p) n -> p k n", p=P))\
                    .then_inc(sem("ple_in"), 16)
                pool.dma_start(pin[:], A["p"][l, 0].rearrange("(t p) n -> p t n", p=P))\
                    .then_inc(sem("ple_in"), 16)
            if not st.endswith("_in"):
                g = {"ab_out": A["mix_post_g"][0], "c_out": A["mix_post_g"][1], "mlp0": A["mlp_post_g"][0],
                     "mlp1": A["mlp_post_g"][1], "ple0": A["ple_post_g"][0], "ple1": A["ple_post_g"][1]}[st]
                pool.wait_ge(*mark("xT_lo", st, 8))
                pool.dma_start(gpost[:], g.partition_broadcast(P)).then_inc(sem("gpost"), 16)

    @block.scalar
    def _(act):
        act_setup(act)
        for st in order:
            if st.startswith("mlp"):
                l = int(st[-1])
                prologue(split_hi, act, st)
                act_first(act, st, base[st], W, GAIN[st], h_squares(act, st))
                mlp_act(act, l, 0)
                with act.Fori(1, 4) as Q:
                    mlp_act(act, l, Q)
                last_junk[0] = mark("m_sq", st, 32)
            elif st.startswith("ple"):
                prologue(split_hi, act, st)
                ple_act(act, int(st[-1]))
            elif st == "ab_in":
                ab_in_act(act)
                ab_attn_act(act)
                rwkv_act(act)
            elif st == "c_in":
                c_in_act(act)
                c_act(act)
            else:
                out_act(act, st)

    @block.vector
    def _(dve):
        link = Link(dve, sem("dve_chain"))
        dve_setup(dve, link)
        for st in order:
            if st.startswith("mlp"):
                l = int(st[-1])
                prologue(split_lo, dve, st)
                h_first(dve, link, st, base[st], W, GAIN[st], prv[st])
                mlp_dve(dve, l, 0)
                with dve.Fori(1, 4) as Q:
                    mlp_dve(dve, l, Q)
            elif st.startswith("ple"):
                prologue(split_lo, dve, st)
                ple_dve(dve, link, int(st[-1]))
            elif st == "ab_in":
                ab_in_dve(dve, link)
                ab_attn_dve(dve, link)
                rwkv_dve(dve, link)
            elif st == "c_in":
                c_in_dve(dve, link)
                c_dve(dve, link)
            else:
                out_dve(dve, st)
        for b in range(4):
            h_update(dve, link, "end", end, b)

    @block.tensor
    def _(pe):
        pe.wait_ge(sem("consts"), N_CONSTS)
        pe.wait_ge(sem("gpre_in"), 64)
        pe.transpose(bank[7][:, 0:4 * KT], g_rows[:], ident[0:4 * KT, 0:4 * KT]).then_inc(sem("gpre_T"), 1)
        for st in order:
            if st.startswith("mlp"):
                l = int(st[-1])
                mlp_pe(pe, l, 0)
                with pe.Fori(1, 4) as Q:
                    mlp_pe(pe, l, Q)
            elif st.startswith("ple"):
                ple_pe(pe, int(st[-1]))
            elif st == "ab_in":
                ab_in_pe(pe)
                ab_attn_pe(pe)
                rwkv_pe(pe)
            elif st == "c_in":
                c_in_pe(pe)
                c_pe(pe)
            else:
                out_pe(pe, st, y_src(st), y_ready(st))

    ctx.close()


def kernel(**inputs):
    from concourse import bacc
    from concourse.bass_utils import run_bass_kernel_spmd

    nc = bacc.Bacc("TRN2", target_bir_lowering=False, num_devices=1)
    arrays, A = {}, {}
    for name, a in inputs.items():
        a = np.ascontiguousarray(a)
        arrays[f"in_{name}"] = a
        A[name] = nc.dram_tensor(f"in_{name}", a.shape, mybir.dt.from_np(a.dtype), kind="ExternalInput").ap()
    A["out"] = nc.dram_tensor("out_0", (1, T, D), F32, kind="ExternalOutput").ap()
    build(nc, A)
    r = run_bass_kernel_spmd(nc, [arrays], core_ids=[0])
    return r.results[0]["out_0"]
```

```python
from contextlib import ExitStack, contextmanager
import math

import numpy as np
import concourse.bass as bass
from concourse import mybir

F32 = mybir.dt.float32
F32R = mybir.dt.float32r
BF16 = mybir.dt.bfloat16
I32 = mybir.dt.int32
ALU = mybir.AluOpType
ACT = mybir.ActivationFunctionType
AX = mybir.AxisListType

P = 128
T = 256
TT = T // P
D = 2048
KT = D // P
DFF = 4 * D
PLE = 256
AW = 1024
BW = 1024
A_HEADS, A_DV, A_DC = 8, 128, 64
B_HEADS, BH = 16, 64
LW, LA, LG = 96, 96, 256
B_IN = 3 * BW + LW + LA + LG
A_IN = 3 * AW
C_HEADS, C_KV, C_HD = 16, 4, 128
IDX_H, IDX_D = 16, 64
C_IN = C_HEADS * C_HD + 2 * C_KV * C_HD + IDX_H * IDX_D + IDX_D + IDX_H
TOPK = T // 4
THETA = 500000.0
LAMBDA_INIT = 0.8 - 0.6 * math.exp(0.0)
NORM_EPS, SUBLN_EPS, LNX_EPS, LN_EPS = 1e-6, 1e-5, 64e-5, 1e-6
CH = 64
NEG = -1e30
TAKEN = -3e38
W = 512
KB = 1024
C_W = C_IN // 9
FULL = ("ab", "mlp0", "ple0", "c", "mlp1", "ple1")


def plan_slabs(plan):
    base, s = {}, 0
    for st in plan:
        parts = {"ab": (("ab_in", 13), ("ab_out", 4)), "c": (("c_in", 9), ("c_out", 4))}.get(
            st, ((st, 32),) if st.startswith("mlp") else ((st, 4),))
        for name, n in parts:
            base[name] = s
            s += n
    return base


class Link:

    def __init__(self, eng, sem):
        self.eng, self.sem, self.n, self.extra = eng, sem, 0, 0

    def __call__(self, ins):
        ins.then_inc(self.sem, 1)
        self.n += 1
        self.eng.wait_ge(self.sem, self.extra + self.n)

    @contextmanager
    def loop(self, i, first, count, per):
        start = self.n
        self.extra = (i - first) * per
        yield
        assert self.n - start == per, (self.n - start, per)
        self.extra, self.n = 0, start + per * count


def build(nc, A, plan=FULL):
    base = plan_slabs(plan)
    ctx = ExitStack()
    sems = {}

    def sem(name):
        if name not in sems:
            sems[name] = ctx.enter_context(nc.semaphore(name))
        return sems[name]

    arena_bytes = 207 * KB + 768
    arena = ctx.enter_context(nc.sbuf_tensor("arena", [P, arena_bytes // 4], F32))
    origin = 16512

    def at(name, shape, dt, kb):
        size = int(np.prod(shape[1:])) * (2 if dt == BF16 else 4)
        assert kb * KB + size <= arena_bytes, name
        return nc.alloc_sbuf_tensor_at(name, shape, dt, offset=int(origin + kb * KB))

    psum = ctx.enter_context(nc.psum_tensor("psum", [P, 8 * 512], F32))
    bank = [psum[:, i * 512:(i + 1) * 512] for i in range(8)]

    h = at("h", [P, TT, D], F32, 0)
    uTh = at("uTh", [P, KT, T], F32R, 16)
    uTl = at("uTl", [P, KT, T], F32R, 32)
    raw = at("raw", [P, 4, 4, W], F32, 48)
    whi = at("whi", [P, 2, 4, W], F32R, 80)
    wlo = at("wlo", [P, 2, 4, W], F32R, 96)
    ident = at("ident", [P, P], F32, 112)
    m_su = at("m_su", [P, P], F32, 112.5)
    m_ui = at("m_ui", [P, P], F32, 113)
    m_l1 = at("m_l1", [P, P], F32, 113.5)
    m_lvt = at("m_lvt", [P, 6, P], F32, 114)
    causal = at("causal", [P, T], F32, 117)
    junk = at("junk", [P, W], BF16, 118)
    cosT = at("cosT", [P, TT, 24], F32, 119)
    sinT = at("sinT", [P, TT, 24], F32, 119.1875)
    gpre = at("gpre", [P, 4, KT], F32, 119.375)
    nwt = at("nwt", [P, 2, 32], F32, 207.5)
    g_rows = at("g_rows", [4 * KT, P], F32, 118)
    ssq = at("ssq", [P, TT, 4], F32, 119.625)
    hss = at("hss", [P, TT, 4], F32, 119.65625)
    st2 = at("st2", [P, 8], F32, 119.6875)
    rstd_m = at("rstd_m", [P, TT], F32, 119.71875)
    rstd_h = at("rstd_h", [P, TT], F32, 119.75)
    lam = at("lam", [P, 4], F32, 119.78125)
    first_half = at("first_half", [P, 6], F32, 119.8125)

    m = at("m", [P, TT, D], F32, 120)
    gpost = at("gpost", [P, D], F32, 136)
    hid = at("hid", [P, 2, TT, W], F32, 144)
    hTh = at("hTh", [P, KT, T], F32R, 152)
    hTl = at("hTl", [P, KT, T], F32R, 168)
    wple = at("wple", [P, 2, D], F32, 184)
    pT = at("pT", [P, 2, T], F32, 200)
    pin = at("pin", [P, TT, PLE], F32, 202)
    gate = at("gate", [P, TT, W], F32, 144)

    za = at("za", [P, TT, A_IN], F32, 120)
    zb = at("zb", [P, TT, B_IN], F32, 144)
    zprev = at("zprev", [P, 2, TT, W], F32, 171.5)
    mu = at("mu", [P, 2, W], F32, 179.5)
    qkT = at("qkT", [P, 2, T], F32, 183.5)
    sm = at("sm", [P, 2, 3 * P], F32, 185.5)
    pe_ = at("pe_", [P, 2, 3 * P], F32, 188.5)
    at_ = at("at_", [P, 3 * P], F32, 191.5)
    atT = at("atT", [P, 3, P], F32, 193)
    cau3 = at("cau3", [P, 3 * P], F32, 194.5)
    rt = at("rt", [P, 4, 64], F32, 196)
    lqk = at("lqk", [P, 4, A_DC], F32, 197)
    mx = at("mx", [P, 4, 4], F32, 198)
    subg = at("subg", [P, A_DV], F32, 118.5)
    r16 = at("r16", [P, 16], F32, 118.4375)
    asq = at("asq", [P, TT, AW], F32, 104)
    posi = at("posi", [P, TT], I32, 120)
    posf = at("posf", [P, TT], F32, 120.125)
    freq = at("freq", [P, 24], F32, 120.25)
    angle = at("angle", [P, 96], F32, 120.5)
    lw = at("lw", [P, TT, BW], F32, 171.5)
    av = at("av", [P, TT, BW], F32, 179.5)
    gv = at("gv", [P, TT, BW], F32, 187.5)
    kkv = at("kkv", [P, TT, BW], F32, 195.5)
    w2 = at("w2", [P, BW], F32, 48)
    a2 = at("a2", [P, BW], F32, 52)
    g2 = at("g2", [P, 2, BW], F32, 56)
    p_w0 = at("p_w0", [P, BW], F32, 64)
    p_a0 = at("p_a0", [P, BW], F32, 68)
    p_kk = at("p_kk", [P, BW], F32, 72)
    p_ka = at("p_ka", [P, BW], F32, 76)
    lnx_g = at("lnx_g", [P, BW], F32, 48)
    lnx_b = at("lnx_b", [P, BW], F32, 52)
    p_rk = at("p_rk", [P, BW], F32, 56)
    loraT = at("loraT", [P, 4, T], F32, 203.5)
    ex1 = at("ex1", [P, TT, BW], F32, 80)
    ex2 = at("ex2", [P, TT, BW], F32, 88)
    bon = at("bon", [P, TT, B_HEADS], F32, 118)
    nrm = at("nrm", [P, TT, B_HEADS], F32, 118.125)
    WL = at("WL", [P, 8, 4], F32, 118.25)
    XT = [[at(f"{n}T{tt}", [P, 8, P], F32, (80 + 4 * i, (124, 128, 136, 140)[i])[tt])
           for i, n in enumerate(("A", "B", "K", "R"))] for tt in range(TT)]
    tmp_set = [[at(f"{n}{s}", [P, 4, P], F32, 96 + 2 * i + 8 * s) for i, n in
                enumerate(("MT", "Ti", "Y1"))] for s in range(2)]
    NT = at("NT", [P, 16, P], F32, 16)
    PT = at("PT", [P, 16, P], F32, 24)
    QT = at("QT", [P, 16, P], F32, 32)
    TTi = at("TTi", [P, 16, P], F32, 40)
    Xs = at("Xs", [P, BW], F32, 171.5)
    Us = at("Us", [P, BW], F32, 175.5)
    ST = at("ST", [P, 8, P], F32, 203.5)

    GAIN = {"ab_in": 0, "c_in": 1, "mlp0": 2, "mlp1": 3}

    def w_chunks(w, Q):
        v = w.rearrange("(Q q k p) n -> Q q p k n", q=4, k=4, p=P)
        return [v[Q, q] for q in range(4)]

    order = []
    for st_ in plan:
        order += {"ab": ["ab_in", "ab_out"], "c": ["c_in", "c_out"]}.get(st_, [st_])
    width = lambda st: C_W if st == "c_in" else W
    nxt = {a: (order[i + 1] if i + 1 < len(order) else None) for i, a in enumerate(order)}
    prv = {a: (order[i - 1] if i else None) for i, a in enumerate(order)}
    read_out = {"ab_in": ("ev_ab_in", 1, 12), "ab_out": ("m_sq", 2, 3), "c_in": ("ev_c_in", 1, 8),
                "c_out": ("m_sq", 2, 3), "mlp0": ("ev_dn", 1, 15), "mlp1": ("ev_dn", 1, 15),
                "ple0": ("ev_ple", 1, 3), "ple1": ("ev_ple", 1, 3)}

    counts = {"m_sq": lambda st: 32 if st.startswith("mlp") else 0 if st.endswith("_in") else 8,
              "h_ready": lambda st: 0 if st == order[0] or st.endswith("_out") else 8,
              "gpost": lambda st: 0 if st.endswith("_in") else 16,
              "ev_ab_in": lambda st: 0, "ev_c_in": lambda st: 0,
              "h_sq": lambda st: 8 if st in GAIN else 0, "rstd": lambda st: 1 if st in GAIN else 0}
    for kind in ("xT", "xT_hi", "xT_lo"):
        counts[kind] = lambda st: 8
    for kind in ("sq_done", "hT", "hT_hi", "hT_lo", "ev_up", "ev_dn"):
        counts[kind] = lambda st: 16 if st.startswith("mlp") else 0
    for kind, n_ in (("gated", 4), ("emb", 4), ("ev_ple", 4), ("ple_in", 32), ("pT_mm", 1), ("pT", 1)):
        counts[kind] = lambda st, n_=n_: n_ if st.startswith("ple") else 0

    def mark(kind, st, v):
        before = order[:order.index(st)] if st in order else order
        return sem(kind), sum(counts[kind](a) for a in before) + v

    landed = [sem(f"landed{q}") for q in range(4)]
    hi_ready, lo_ready = sem("hi_ready"), sem("lo_ready")
    mm_used = sem("mm_used")

    def load_slab(sp, s, w, col, n, first=False):
        for q in range(4):
            if not first:
                sp.wait_ge(lo_ready, 4 * s - 3 + q)
            sp.dma_start(raw[:, q, :, 0:n], w[q][:, :, bass.ds(col, n)]).then_inc(landed[q], 16)

    def split_hi(act, s, q, n=W, fresh=False):
        act.wait_ge(landed[q], 16 * (s + 1))
        if not fresh:
            act.wait_ge(mm_used, 4 * s + q - 1)
        act.activation(whi[:, q % 2, :, 0:n], raw[:, q, :, 0:n], ACT.Copy).then_inc(hi_ready, 1)

    def split_lo(dve, s, q, n=W):
        dve.wait_ge(hi_ready, 4 * s + q + 1)
        dve.tensor_tensor(wlo[:, q % 2, :, 0:n], raw[:, q, :, 0:n], whi[:, q % 2, :, 0:n].bitcast(F32),
                          ALU.subtract).then_inc(lo_ready, 1)

    def mm_slab(pe, s, par_, n=W, free=None, before=None, lhs=(uTh, uTl)):
        if free:
            pe.wait_ge(*free)
        for q in range(4):
            if before:
                before(q)
            pe.wait_ge(lo_ready, 4 * s + q + 1)
            for k in range(4):
                for tt in range(TT):
                    o = bank[2 * par_ + tt][:, 0:n]
                    xh = lhs[0][:, 4 * q + k, tt * P:(tt + 1) * P]
                    xl = lhs[1][:, 4 * q + k, tt * P:(tt + 1) * P]
                    hi, lo = whi[:, q % 2, k, 0:n], wlo[:, q % 2, k, 0:n]
                    pe.matmul(o, xh, hi, start=(q == 0 and k == 0), stop=False)
                    pe.matmul(o, xh, lo, start=False, stop=False)
                    last = pe.matmul(o, xl, hi, start=False, stop=(q == 3 and k == 3))
            last.then_inc(mm_used, 1)

    def T_pe(pe, st, src, ready, b):
        for pr in range(2):
            g = 2 * b + pr
            if g >= 4:
                pe.wait_ge(*mark("xT_lo", st, g - 3))
            if g == 3 and st == order[0]:
                pe.wait_ge(sem("gpre_ready"), 1)
            if g == 3 and st.startswith("ple"):
                pe.wait_ge(*mark("pT", st, 1))
            for kk in range(2):
                for tt in range(TT):
                    if pr == 0 and kk == 0:
                        pe.wait_ge(*ready(tt, b))
                    c = (2 * pr + kk) * P
                    last = pe.transpose(bank[4 + g % 4][:, (2 * kk + tt) * P:(2 * kk + tt + 1) * P],
                                        src(tt, b)[:, c:c + P], ident[:])
            last.then_inc(sem("xT"), 1)

    def T_act(act, st, b, gain=None):
        for pr in range(2):
            g = 2 * b + pr
            act.wait_ge(*mark("xT", st, g + 1))
            for kk in range(2):
                k = 2 * g + kk
                sc = 1.0 if gain is None else gpre[:, gain, k:k + 1]
                last = act.activation(uTh[:, k, :], bank[4 + g % 4][:, kk * T:(kk + 1) * T], ACT.Copy, scale=sc)
            last.then_inc(sem("xT_hi"), 1)

    def T_dve(dve, st, b, gain=None):
        for pr in range(2):
            g = 2 * b + pr
            dve.wait_ge(*mark("xT_hi", st, g + 1))
            for kk in range(2):
                k = 2 * g + kk
                x = bank[4 + g % 4][:, kk * T:(kk + 1) * T]
                if gain is None:
                    last = dve.tensor_tensor(uTl[:, k, :], x, uTh[:, k, :].bitcast(F32), ALU.subtract)
                else:
                    last = dve.scalar_tensor_tensor(out=uTl[:, k, :], in0=x, scalar=gpre[:, gain, k:k + 1],
                                                    in1=uTh[:, k, :].bitcast(F32), op0=ALU.mult,
                                                    op1=ALU.subtract)
            last.then_inc(sem("xT_lo"), 1)

    def pe_first(pe, st, s, par_, src, ready, n=W, free=None):
        T_pe(pe, st, src, ready, 0)

        def before(q):
            if q < 3:
                T_pe(pe, st, src, ready, q + 1)
            pe.wait_ge(*mark("xT_lo", st, 2 * q + 2))
        mm_slab(pe, s, par_, n, free, before)

    def act_first(act, st, s, n, gain, squares=None, fresh=False):
        for b in range(4):
            if squares:
                squares(b)
            T_act(act, st, b, gain)
            if b >= 2:
                split_hi(act, s, b, n)

    def dve_first(dve, st, s, n, gain):
        for b in range(4):
            T_dve(dve, st, b, gain)
            if b >= 2:
                split_lo(dve, s, b, n)

    last_junk = [None]

    def square(act, x, total, signal, i, prev=None):
        prev = prev or last_junk[0]
        if prev:
            act.wait_ge(*prev)
        last_junk[0] = (signal, i)
        return act.activation(junk[:], x, ACT.Square, accum_out=total).then_inc(signal, 1)

    def h_src(tt, b):
        return h[:, tt, b * W:(b + 1) * W]

    def h_squares(act, st):
        def squares(b):
            for tt in range(TT):
                act.wait_ge(*h_ready(st)(tt, b))
                square(act, h_src(tt, b), hss[:, tt, b:b + 1], *mark("h_sq", st, 2 * b + tt + 1))
        return squares

    def h_ready(st):
        return lambda tt, b: (sem("x_in"), 16) if st == order[0] else mark("h_ready", st, 2 * b + tt + 1)

    def rsqrt(dve, link, x):
        n = x.free_size()
        y, t = nwt[:, 0, 0:n], nwt[:, 1, 0:n]
        link(dve.tensor_scalar(y.bitcast(I32), x.bitcast(I32), 1, None, ALU.logical_shift_right))
        link(dve.tensor_scalar(y.bitcast(I32), y.bitcast(I32), -1.0, float(0x5F3759DF), ALU.mult, ALU.add))
        for i in range(3):
            link(dve.tensor_tensor(t, y, y, ALU.mult))
            link(dve.scalar_tensor_tensor(out=t, in0=t, scalar=-0.5, in1=x, op0=ALU.mult, op1=ALU.mult))
            last = dve.scalar_tensor_tensor(out=y if i < 2 else x, in0=t, scalar=1.5, in1=y, op0=ALU.add,
                                            op1=ALU.mult)
            if i < 2:
                link(last)
        return last

    def rstd_from(dve, link, src, out_, n, eps):
        link(dve.tensor_reduce(out_, src, AX.X, ALU.add))
        link(dve.tensor_scalar(out_, out_, 1.0 / n, eps, ALU.mult, ALU.add))
        return rsqrt(dve, link, out_)

    def h_update(dve, link, st, prev, b):
        if b == 0:
            dve.wait_ge(*mark("m_sq", prev, m_sq_all[prev]))
            link(rstd_from(dve, link, ssq[:], rstd_m[:], D, NORM_EPS))
            dve.wait_ge(*mark("gpost", prev, 16))
        for tt in range(TT):
            mb = m[:, tt, b * W:(b + 1) * W]
            link(dve.scalar_tensor_tensor(out=mb, in0=mb, scalar=rstd_m[:, tt:tt + 1],
                                          in1=gpost[:, b * W:(b + 1) * W], op0=ALU.mult, op1=ALU.mult))
            dve.tensor_tensor(h_src(tt, b), h_src(tt, b), mb, ALU.add).then_inc(sem("h_ready"), 1)

    m_sq_all = {"ab_out": 8, "c_out": 8, "mlp0": 32, "mlp1": 32, "ple0": 8, "ple1": 8}

    def h_first(dve, link, st, s, n, gain, prev):
        for b in range(4):
            if prev:
                h_update(dve, link, st, prev, b)
            if b:
                T_dve(dve, st, b - 1, gain)
            if b == 3:
                split_lo(dve, s, 2, n)
        T_dve(dve, st, 3, gain)
        split_lo(dve, s, 3, n)
        if gain is not None:
            dve.wait_ge(*mark("h_sq", st, 8))
            rstd_from(dve, link, hss[:], rstd_h[:], D, NORM_EPS).then_inc(sem("rstd"), 1)

    def prologue(fn, eng, st):
        if prv[st] is None or prv[st].endswith("_in"):
            s, n = base[st], width(st)
            if fn is split_hi:
                fn(eng, s, 0, n, fresh=(s == 0))
                fn(eng, s, 1, n, fresh=(s == 0))
            else:
                fn(eng, s, 0, n)
                fn(eng, s, 1, n)

    def free_of(st, i):
        if i >= 2:
            return mark(read_out[st][0], st, read_out[st][1] * (i - 1))
        if prv[st] is None:
            return None
        name, by, v = read_out[prv[st]]
        return mark(name, prv[st], by * (v + i))

    N_CONSTS = 7
    HALF_A, HALF_C = A_DC // 8, C_HD // 8
    chain = sem("pool_chain")

    def pool_setup(pool):
        n = [0]

        def link(ins):
            ins.then_inc(chain, 1)
            n[0] += 1
            pool.wait_ge(chain, n[0])

        def keep(ap, pattern, cm, base_, op=ALU.is_ge, fill=0.0):
            return pool.affine_select(out=ap, in_=ap, compare_op=op, fill=fill, base=base_, pattern=pattern,
                                      channel_multiplier=cm)
        for i, g in enumerate((A["mix_pre_g"][0], A["mix_pre_g"][1], A["mlp_pre_g"][0], A["mlp_pre_g"][1])):
            pool.dma_start(g_rows[KT * i:KT * (i + 1), :], g.rearrange("(k p) -> k p", p=P)).then_inc(sem("gpre_in"), 16)
        link(pool.memset(ident[:], 0.0))
        keep(ident[:], [[-1, P]], 1, 0, ALU.not_equal, 1.0).then_inc(sem("consts"), 1)
        link(pool.memset(m_su[:], 1.0))
        v = m_su[:].rearrange("p (j c) -> p j c", c=CH)
        link(keep(v, [[-CH, 2], [0, CH]], 1, 0))
        keep(v, [[CH, 2], [1, CH]], -1, -1).then_inc(sem("consts"), 1)
        link(pool.memset(m_ui[:], 1.0))
        v = m_ui[:].rearrange("p (j c) -> p j c", c=CH)
        link(keep(v, [[-CH, 2], [0, CH]], 1, 0))
        keep(v, [[CH, 2], [1, CH]], -1, 0).then_inc(sem("consts"), 1)
        link(pool.memset(m_l1[:], 0.0))
        v = m_l1[:].rearrange("p (j c) -> p j c", c=2)[:, :, 1:2]
        keep(v, [[-2, P // 2], [0, 1]], 1, 0, ALU.not_equal, 1.0).then_inc(sem("consts"), 1)
        link(pool.memset(m_lvt[:], 0.0))
        for i in range(6):
            b = 1 << i
            v = m_lvt[:, i, :].rearrange("p (j c) -> p j c", c=2 * b)[:, :, 0:b]
            link(pool.memset(v, 1.0))
            link(keep(v, [[-2 * b, P // (2 * b)], [0, b]], 1, -b))
            link(keep(v, [[2 * b, P // (2 * b)], [0, b]], -1, 2 * b - 1))
        pool.memset(st2[:, 6:7], 0.0).then_inc(sem("consts"), 1)
        link(pool.memset(causal[:], 0.0))
        keep(causal[:, P:T], [[-1, P]], 1, 0, ALU.is_ge, NEG).then_inc(sem("consts"), 1)
        pool.memset(st2[:, 7:8], 0.0).then_inc(sem("consts"), 1)
        for half, f0 in ((HALF_A, 0), (HALF_C, HALF_A)):
            for j in range(half):
                v = np.float32(THETA) ** (-(np.float32(j) * np.float32(2.0) / np.float32(2 * half)))
                pool.memset(freq[:, f0 + j:f0 + j + 1], float(np.float32(v))).then_inc(sem("freqs"), 1)
        with nc.allow_non_contiguous_dma(reason="256 positions"):
            pool.dma_start(posi[:], A["positions"][0].rearrange("(t p) -> p t", p=P)).then_inc(sem("pos_in"), 16)

    def act_setup(act):
        act.wait_ge(sem("gpre_T"), 1)
        act.activation(gpre[:], bank[7][:, 0:4 * KT], ACT.Copy).then_inc(sem("gpre_ready"), 1)
        act.wait_ge(sem("gpre_ready"), 1)

    def dve_setup(dve, link):
        dve.wait_ge(sem("consts"), N_CONSTS)
        link(dve.tensor_reduce(first_half[:], m_lvt[:], AX.X, ALU.max))
        link(dve.tensor_scalar(first_half[:], first_half[:], -1.0, 1.0, ALU.mult, ALU.add))
        dve.wait_ge(sem("gpre_ready"), 1)

    def step(fn, eng, s, st, nn, done, n=None, mid=None, skip=False):
        n = n or width(st)
        if not skip:
            fn(eng, s, 2, n)
            fn(eng, s, 3, n)
        if mid:
            mid()
        if nn:
            fn(eng, s + 1, 0, nn)
            fn(eng, s + 1, 1, nn)
        if done:
            done()

    def next_width(st):
        return width(nxt[st]) if nxt[st] and not st.endswith("_in") else None

    def T_mlp_pe(pe, l, Q, j):
        pe.wait_ge(*mark("sq_done", f"mlp{l}", 4 * Q + j + 1))
        if j >= 2:
            pe.wait_ge(*mark("hT_lo", f"mlp{l}", 4 * Q + j - 1))
        for pr in range(2):
            for kk in range(2):
                for tt in range(TT):
                    last = pe.transpose(bank[4 + 2 * (j % 2) + pr][:, (2 * kk + tt) * P:(2 * kk + tt + 1) * P],
                                        hid[:, j % 2, tt, (2 * pr + kk) * P:(2 * pr + kk + 1) * P], ident[:])
        last.then_inc(sem("hT"), 1)

    def T_mlp_split(eng, l, Q, j, high):
        eng.wait_ge(*mark("hT" if high else "hT_hi", f"mlp{l}", 4 * Q + j + 1))
        for pr in range(2):
            k = 4 * j + 2 * pr
            x = bank[4 + 2 * (j % 2) + pr][:]
            if high:
                last = eng.activation(hTh[:, k:k + 2, :], x, ACT.Copy)
            else:
                last = eng.tensor_tensor(hTl[:, k:k + 2, :], x, hTh[:, k:k + 2, :].bitcast(F32), ALU.subtract)
        last.then_inc(sem("hT_hi" if high else "hT_lo"), 1)

    def mlp_pe(pe, l, Q):
        st = f"mlp{l}"
        s = base[st] + 8 * Q
        par_ = lambda r: (base[st] + r) % 2
        up = lambda v: mark("ev_up", st, v)
        dn = lambda v: mark("ev_dn", st, v)
        first = isinstance(Q, int)
        if first:
            pe_first(pe, st, s, par_(0), h_src, h_ready(st), W, free_of(st, 0))
            mm_slab(pe, s + 1, par_(1), W, free_of(st, 1))
        else:
            mm_slab(pe, s, par_(0), W, dn(4 * Q - 1))
            mm_slab(pe, s + 1, par_(1), W, dn(4 * Q))
        for j in (2, 3):
            T_mlp_pe(pe, l, Q, j - 2)
            mm_slab(pe, s + j, par_(j), W, up(4 * Q + j - 1))
        T_mlp_pe(pe, l, Q, 2)

        def before(q):
            if q == 3:
                T_mlp_pe(pe, l, Q, 3)
            pe.wait_ge(*mark("hT_lo", f"mlp{l}", 4 * Q + q + 1))
        mm_slab(pe, s + 4, par_(4), W, up(4 * Q + 3), before, (hTh, hTl))
        mm_slab(pe, s + 5, par_(5), W, up(4 * Q + 4), None, (hTh, hTl))
        mm_slab(pe, s + 6, par_(6), W, dn(4 * Q + 1), None, (hTh, hTl))
        mm_slab(pe, s + 7, par_(7), W, dn(4 * Q + 2), None, (hTh, hTl))

    def mlp_act(act, l, Q):
        st = f"mlp{l}"
        first = isinstance(Q, int)
        for r in range(8):
            s, j, par_ = base[st] + 8 * Q + r, r % 4, (base[st] + r) % 2

            def relu():
                act.wait_ge(mm_used, 4 * s + 4)
                if first and r == 0:
                    act.wait_ge(*mark("rstd", st, 1))
                for tt in range(TT):
                    last = act.activation(hid[:, j % 2, tt, :], bank[2 * par_ + tt][:], ACT.Relu,
                                          scale=rstd_h[:, tt:tt + 1])
                last.then_inc(sem("ev_up"), 1)
                if j:
                    T_mlp_split(act, l, Q, j - 1, True)

            def squares():
                act.wait_ge(*mark("ev_dn", f"mlp{l}", 4 * Q + j + 1))
                for tt in range(TT):
                    n = 8 * Q + 2 * j + tt
                    square(act, m[:, tt, j * W:(j + 1) * W], ssq[:, tt, j:j + 1], *mark("m_sq", st, n + 1),
                           None if first and j + tt == 0 else mark("m_sq", st, n))
            step(split_hi, act, s, st, W,
                 squares if r >= 4 else relu, skip=first and r == 0,
                 mid=(lambda: T_mlp_split(act, l, Q, 3, True)) if r == 4 else None)

    def mlp_dve(dve, l, Q):
        st = f"mlp{l}"
        first = isinstance(Q, int)
        for r in range(8):
            s, j, par_ = base[st] + 8 * Q + r, r % 4, (base[st] + r) % 2

            def square():
                dve.wait_ge(*mark("ev_up", f"mlp{l}", 4 * Q + j + 1))
                x = hid[:, j % 2, :, :]
                dve.tensor_tensor(x, x, x, ALU.mult).then_inc(sem("sq_done"), 1)
                if j:
                    T_mlp_split(dve, l, Q, j - 1, False)

            def add():
                dve.wait_ge(mm_used, 4 * s + 4)
                for tt in range(TT):
                    x, y = bank[2 * par_ + tt][:], m[:, tt, j * W:(j + 1) * W]
                    last = dve.tensor_copy(y, x) if first else dve.tensor_tensor(y, y, x, ALU.add)
                last.then_inc(sem("ev_dn"), 1)
            step(split_lo, dve, s, st, W, add if r >= 4 else square, skip=first and r == 0,
                 mid=(lambda: T_mlp_split(dve, l, Q, 3, False)) if r == 4 else None)

    def ple_pe(pe, l):
        st = f"ple{l}"
        pe.wait_ge(*mark("ple_in", f"ple{l}", 32))
        if not prv[st]:
            pe.wait_ge(sem("gpre_ready"), 1)
        for k in range(2):
            for tt in range(TT):
                last = pe.transpose(bank[7][:, (2 * k + tt) * P:(2 * k + tt + 1) * P],
                                    pin[:, tt, k * P:(k + 1) * P], ident[:])
        last.then_inc(sem("pT_mm"), 1)
        for j in range(4):
            s = base[st] + j
            if j == 0:
                pe_first(pe, st, s, s % 2, h_src, h_ready(st), W, free_of(st, 0))
            else:
                mm_slab(pe, s, s % 2, W, free_of(st, j))
                pe.wait_ge(*mark("gated", f"ple{l}", j))
            for tt in range(TT):
                for k in range(2):
                    last = pe.matmul(bank[6 + tt][:], pT[:, k, tt * P:(tt + 1) * P],
                                     wple[:, k, j * W:(j + 1) * W], start=(k == 0), stop=(k == 1))
            last.then_inc(sem("emb"), 1)

    def ple_act(act, l):
        st = f"ple{l}"
        act.wait_ge(*mark("pT_mm", st, 1))
        act.activation(pT[:], bank[7][:], ACT.Copy).then_inc(sem("pT"), 1)
        act_first(act, st, base[st], W, None)
        for j in range(4):
            s = base[st] + j

            def sigmoid():
                act.wait_ge(mm_used, 4 * s + 4)
                for tt in range(TT):
                    last = act.activation(gate[:, tt, :], bank[2 * (s % 2) + tt][:], ACT.Sigmoid)
                last.then_inc(sem("ev_ple"), 1)
                act.wait_ge(*mark("gated", f"ple{l}", j + 1))
                for tt in range(TT):
                    square(act, m[:, tt, j * W:(j + 1) * W], ssq[:, tt, j:j + 1], *mark("m_sq", st, 2 * j + tt + 1))
            step(split_hi, act, s, st, W if j < 3 else next_width(st), sigmoid, skip=(j == 0))

    def ple_dve(dve, link, l):
        st = f"ple{l}"
        h_first(dve, link, st, base[st], W, None, prv[st])
        for j in range(4):
            s = base[st] + j

            def gated():
                dve.wait_ge(*mark("ev_ple", f"ple{l}", j + 1))
                dve.wait_ge(*mark("emb", f"ple{l}", j + 1))
                for tt in range(TT):
                    last = dve.tensor_tensor(m[:, tt, j * W:(j + 1) * W], gate[:, tt, :], bank[6 + tt][:],
                                             ALU.mult)
                last.then_inc(sem("gated"), 1)
            step(split_lo, dve, s, st, W if j < 3 else next_width(st), gated, skip=(j == 0))

    def out_act(act, st, fresh=False):
        if st == "ab_out":
            act.wait_ge(sem("y_mm"), 4)
        prologue(split_hi, act, st)
        act_first(act, st, base[st], W, None)
        for j in range(4):
            s = base[st] + j

            def keep():
                act.wait_ge(mm_used, 4 * s + 4)
                if j == 0:
                    act.wait_ge(*mark("xT", st, 8))
                for tt in range(TT):
                    act.activation(m[:, tt, j * W:(j + 1) * W], bank[2 * (s % 2) + tt][:], ACT.Copy)
                for tt in range(TT):
                    square(act, bank[2 * (s % 2) + tt][:], ssq[:, tt, j:j + 1], *mark("m_sq", st, 2 * j + tt + 1))
            step(split_hi, act, s, st, W if j < 3 else next_width(st), keep, skip=(j == 0))

    def out_dve(dve, st):
        prologue(split_lo, dve, st)
        dve_first(dve, st, base[st], W, None)
        for j in range(4):
            step(split_lo, dve, base[st] + j, st, W if j < 3 else next_width(st), None, skip=(j == 0))

    def out_pe(pe, st, src, ready):
        if st == "ab_out":
            pe.wait_ge(sem("y_out"), 4)
        for j in range(4):
            s = base[st] + j
            if j == 0:
                pe_first(pe, st, s, s % 2, src, ready, W, free_of(st, 0))
            else:
                mm_slab(pe, s, s % 2, W, free_of(st, j))

    QB = (4, 5, 6, 7)

    def tr_pe(pe, name, groups, banks, first_waits=()):
        for w in first_waits:
            pe.wait_ge(*w)
        for g, items in enumerate(groups):
            if g >= len(banks):
                o = g - len(banks)
                pe.wait_ge(sem(f"{name}_out{o % 2}"), o // 2 + 1)
            for i, x in enumerate(items):
                rows = x.shape[1]
                last = pe.transpose(bank[banks[g % len(banks)]][0:rows, i * P:(i + 1) * P], x, ident[:])
            last.then_inc(sem(f"{name}_tr"), 1)

    def tr_out(eng, name, outs, banks, me):
        for g, (o, rows, c0, c1) in enumerate(outs):
            if g % 2 == me:
                eng.wait_ge(sem(f"{name}_tr"), g + 1)
                x = bank[banks[g % len(banks)]][0:rows, c0:c1]
                ins = eng.activation(o, x, ACT.Copy) if me == 0 else eng.tensor_copy(o, x)
                ins.then_inc(sem(f"{name}_out{me}"), 1)

    def tr_all(eng, name, n):
        for me in range(2):
            if (n + 1 - me) // 2:
                eng.wait_ge(sem(f"{name}_out{me}"), (n + 1 - me) // 2)

    def trig_act(act):
        act.wait_ge(sem("angles"), 2)
        act.activation(sinT[:], sinT[:], ACT.Sin).then_inc(sem("trig"), 1)
        act.activation(cosT[:], cosT[:], ACT.Sin).then_inc(sem("trig"), 1)

    def trig_dve(dve, link):
        ang, kq = angle[:, 0:48].rearrange("p (t f) -> p t f", t=TT), angle[:, 48:96].rearrange("p (t f) -> p t f", t=TT)
        dve.wait_ge(sem("pos_in"), 16)
        dve.wait_ge(sem("freqs"), 24)
        link(dve.tensor_copy(posf[:], posi[:]))
        for tt in range(TT):
            link(dve.tensor_scalar(ang[:, tt, :], freq[:], posf[:, tt:tt + 1], None, ALU.mult))
        magic = 1.5 * 2.0 ** 23
        link(dve.tensor_scalar(kq, ang, 1.0 / (2 * math.pi), magic, ALU.mult, ALU.add))
        link(dve.tensor_scalar(kq, kq, -magic, None, ALU.add))
        c1 = 6.28125
        c2 = float(np.float32(round((2 * math.pi - c1) * 2 ** 21) / 2 ** 21))
        c3 = 2 * math.pi - c1 - c2
        for c in (c1, c2, c3):
            link(dve.scalar_tensor_tensor(out=ang, in0=kq, scalar=-c, in1=ang, op0=ALU.mult, op1=ALU.add))
        lim = 3.1415925
        link(dve.tensor_scalar(ang, ang, lim, -lim, ALU.min, ALU.max))
        dve.tensor_copy(sinT[:], ang).then_inc(sem("angles"), 1)
        link(dve.scalar_tensor_tensor(out=kq, in0=ang, scalar=-1.0, in1=ang, op0=ALU.mult, op1=ALU.max))
        dve.tensor_scalar(cosT[:], kq, -1.0, math.pi / 2, ALU.mult, ALU.add).then_inc(sem("angles"), 1)

    def rope(dve, link, x, tt, f0, half, tmp):
        n = x.shape[1]
        c = cosT[:, tt, f0:f0 + half].unsqueeze(1).broadcast_to([P, n, half])
        s = sinT[:, tt, f0:f0 + half].unsqueeze(1).broadcast_to([P, n, half])
        x1, x2 = x[:, :, 0:half], x[:, :, half:2 * half]
        t = [tmp[:, i, 0:n * half].rearrange("p (a b) -> p a b", b=half) for i in range(4)]
        link(dve.tensor_tensor(t[0], x1, c, ALU.mult))
        link(dve.tensor_tensor(t[1], x2, s, ALU.mult))
        link(dve.tensor_tensor(t[2], x2, c, ALU.mult))
        link(dve.tensor_tensor(t[3], x1, s, ALU.mult))
        link(dve.tensor_tensor(x1, t[0], t[1], ALU.subtract))
        return dve.tensor_tensor(x2, t[2], t[3], ALU.add)

    NL = B_IN - 6 * W
    ab_slabs = [(za, (w * AW + g * W), W) for g in range(2) for w in range(3)] + \
               [(zb, 6 * W, NL)] + [(zb, i * W, W) for i in (2, 3, 0, 1, 4, 5)]
    ab_cols = [c if dst is za else A_IN + c for dst, c, _ in ab_slabs]
    N_AB = len(ab_slabs)
    R0 = 6
    H0 = 4

    def ab_in_pe(pe):
        st, b = "ab_in", base["ab_in"]
        ev = sem("ev_ab_in")
        for i, (_, _, n) in enumerate(ab_slabs):
            if i == 0:
                pe_first(pe, st, b, b % 2, h_src, h_ready(st), W, free_of(st, 0))
                continue

            def before(q):
                hd = i - H0
                if q == 0 and 1 <= hd <= A_HEADS:
                    head_weights_pe(pe, hd - 1)
                if q == 0 and 0 <= hd < A_HEADS:
                    head_transposes_pe(pe, hd)
                if q == 1 and 1 <= hd <= A_HEADS:
                    head_values_pe(pe, hd - 1)
                if q == 2 and 0 <= hd < A_HEADS:
                    head_scores_pe(pe, hd)
                if q == 3 and i - 10 in range(TT):
                    lora_transposes_pe(pe, i - 10)
            mm_slab(pe, b + i, (b + i) % 2, n, (ev, i - 1) if i > 1 else free_of(st, 1), before)

    def ab_in_act(act):
        st, b = "ab_in", base["ab_in"]
        prologue(split_hi, act, st)
        act_first(act, st, b, W, GAIN[st], h_squares(act, st))
        trig_act(act)
        act.wait_ge(sem("lam_sums"), 1)
        act.activation(lam[:, 0:2], lam[:, 0:2], ACT.Exp).then_inc(sem("lam_exp"), 1)
        act.wait_ge(*mark("rstd", st, 1))
        for i, (dst, col, n) in enumerate(ab_slabs):
            s, hd = b + i, i - H0
            if i:
                split_hi(act, s, 2, n)
                if 1 <= hd <= A_HEADS:
                    head_out_act(act, hd - 1)
                split_hi(act, s, 3, n)
                if 0 <= hd < A_HEADS:
                    head_exp_act(act, hd)
            if i + 1 < N_AB:
                nn = ab_slabs[i + 1][2]
                split_hi(act, s + 1, 0, nn)
                if i - 10 in range(TT):
                    lora_out_act(act, i - 10)
                split_hi(act, s + 1, 1, nn)
            act.wait_ge(mm_used, 4 * s + 4)
            for tt in range(TT):
                last = act.activation(dst[:, tt, col:col + n], bank[2 * (s % 2) + tt][:, 0:n], ACT.Copy,
                                      scale=rstd_h[:, tt:tt + 1])
            last.then_inc(sem("ev_ab_in"), 1)
            if 0 <= hd < A_HEADS:
                head_weights_act(act, hd)
            if 0 <= hd + 1 < A_HEADS:
                head_transposes_act(act, hd + 1)
            if i == 8:
                act.wait_ge(sem("mixed"), 1)
                x = zb[:, :, 3 * BW:3 * BW + LW]
                act.activation(x, x, ACT.Tanh).then_inc(sem("lora_act"), 1)
                x = zb[:, :, 3 * BW + LW + LA:B_IN]
                act.activation(x, x, ACT.Sigmoid).then_inc(sem("lora_act"), 1)

    def ab_in_pool(pool):
        for i, n in enumerate(("diff_lq1", "diff_lk1", "diff_lq2", "diff_lk2")):
            pool.dma_start(lqk[:, i, :], A[n][0].partition_broadcast(P)).then_inc(sem("attn_in"), 16)
        pool.wait_ge(*mark("h_sq", "ab_in", 8))
        pool.dma_start(subg[:], A["diff_subln_g"][0].partition_broadcast(P)).then_inc(sem("subg_in"), 16)
        pool.wait_ge(sem("consts"), N_CONSTS)
        pool.tensor_copy(cau3[:, 0:P], causal[:, P:T]).then_inc(sem("mask_in"), 1)
        pool.tensor_copy(cau3[:, P:3 * P], causal[:]).then_inc(sem("mask_in"), 1)
        for i, (_, col, n) in enumerate(ab_slabs[R0:]):
            pool.wait_ge(sem("ev_ab_in"), R0 + i + 1)
            if i >= 2:
                pool.wait_ge(sem("mixed"), i - 1)
            slot, c = i % 2, slice(col, col + n)
            done = sem(f"shifted{slot}")
            pool.dma_start(mu[:, slot, 0:n], A["rwkv_mu"][0, c].partition_broadcast(P)).then_inc(done, 16)
            pool.memset(zprev[0:1, slot, 0, :], 0.0).then_inc(sem("zero_row"), 1)
            pool.dma_start(zprev[1:P, slot, :, 0:n], zb[0:P - 1, :, c]).then_inc(done, 16)
            pool.dma_start(zprev[0:1, slot, 1:2, 0:n], zb[P - 1:P, 0:1, c]).then_inc(done, 16)

    def mix_dve(dve, link, i):
        _, col, n = ab_slabs[R0 + i]
        slot = i % 2
        dve.wait_ge(sem(f"shifted{slot}"), 48 * (i // 2 + 1))
        dve.wait_ge(sem("zero_row"), i + 1)
        z, d = zb[:, :, col:col + n], zprev[:, slot, :, 0:n]
        link(dve.tensor_tensor(d, d, z, ALU.subtract))
        link(dve.tensor_tensor(d, d, mu[:, slot, 0:n].unsqueeze(1).broadcast_to([P, TT, n]), ALU.mult))
        dve.tensor_tensor(z, z, d, ALU.add).then_inc(sem("mixed"), 1)

    def rope_heads_dve(dve, link, g):
        dve.wait_ge(sem("ev_ab_in"), 3 * g + 2)
        dve.wait_ge(sem("trig"), 2)
        for w in range(2):
            for tt in range(TT):
                x = za[:, tt, w * AW + g * W:w * AW + (g + 1) * W].rearrange("p (h d) -> p h d", d=A_DC)
                last = rope(dve, link, x, tt, 0, HALF_A, rt)
                if (w, tt) != (1, 1):
                    link(last)
        last.then_inc(sem("roped"), 1)

    def ab_in_dve(dve, link):
        st, b = "ab_in", base["ab_in"]
        trig_dve(dve, link)
        dve.wait_ge(sem("attn_in"), 64)
        for i in range(2):
            link(dve.tensor_tensor(lqk[:, 2 * i, :], lqk[:, 2 * i, :], lqk[:, 2 * i + 1, :], ALU.mult))
            last = dve.tensor_reduce(lam[:, i:i + 1], lqk[:, 2 * i, :], AX.X, ALU.add)
            if i == 0:
                link(last)
        last.then_inc(sem("lam_sums"), 1)
        prologue(split_lo, dve, st)
        h_first(dve, link, st, b, W, GAIN[st], prv[st])
        dve.wait_ge(sem("lam_exp"), 1)
        link(dve.tensor_tensor(lam[:, 2:3], lam[:, 1:2], lam[:, 0:1], ALU.subtract))
        link(dve.tensor_scalar(lam[:, 2:3], lam[:, 2:3], -LAMBDA_INIT, None, ALU.add))
        dve.wait_ge(sem("mask_in"), 2)
        for i, (_, _, n) in enumerate(ab_slabs):
            s, hd = b + i, i - H0
            if i:
                split_lo(dve, s, 2, n)
                if 0 <= hd < A_HEADS:
                    head_mask_dve(dve, link, hd)
                split_lo(dve, s, 3, n)
                if 0 <= hd < A_HEADS:
                    head_weights_dve(dve, link, hd)
            if i + 1 < N_AB:
                nn = ab_slabs[i + 1][2]
                split_lo(dve, s + 1, 0, nn)
                split_lo(dve, s + 1, 1, nn)
            if i in (2, 5):
                rope_heads_dve(dve, link, i // 3)
            if i > R0:
                mix_dve(dve, link, i - R0 - 1)
        mix_dve(dve, link, N_AB - R0 - 1)

    PARTS3 = ((0, slice(0, P), 1), (1, slice(P, 3 * P), 2))

    def head_transposes_pe(pe, hd):
        pe.wait_ge(sem("roped"), hd // 4 + 1)
        if hd:
            pe.wait_ge(sem("qkT"), hd)
        for w in range(2):
            for tt in range(TT):
                last = pe.transpose(bank[4][:, (2 * w + tt) * P:(2 * w + tt + 1) * P],
                                    za[:, tt, w * AW + hd * P:w * AW + (hd + 1) * P], ident[:])
        last.then_inc(sem("qk_tr"), 1)

    def head_transposes_act(act, hd):
        act.wait_ge(sem("qk_tr"), hd + 1)
        act.activation(qkT[:], bank[4], ACT.Copy).then_inc(sem("qkT"), 1)

    def head_scores_pe(pe, hd):
        pe.wait_ge(sem("qkT"), hd + 1)
        if hd:
            pe.wait_ge(sem("a_masked"), hd)
            pe.wait_ge(sem("a_y"), hd)
        for tt, cols, _ in PARTS3:
            for c in range(2):
                r = slice(c * A_DC, (c + 1) * A_DC)
                last = pe.matmul(bank[5 + c][:, cols], qkT[r, 0, tt * P:(tt + 1) * P], qkT[r, 1, 0:(tt + 1) * P],
                                 start=True, stop=True)
        last.then_inc(sem("a_scores"), 1)

    def head_mask_dve(dve, link, hd):
        dve.wait_ge(sem("a_scores"), hd + 1)
        if hd:
            dve.wait_ge(sem("a_exp"), 4 * hd)
        x = psum[:, 5 * 512:7 * 512].rearrange("p (c k) -> p c k", c=2)[:, :, 0:3 * P]
        dve.scalar_tensor_tensor(out=sm[:], in0=x, scalar=A_DC ** -0.5,
                                 in1=cau3[:].unsqueeze(1).broadcast_to([P, 2, 3 * P]), op0=ALU.mult,
                                 op1=ALU.add).then_inc(sem("a_masked"), 1)
        dve.wait_ge(sem("a_masked"), hd + 1)
        for tt, cols, _ in PARTS3:
            last = dve.tensor_reduce(mx[:, 0, 2 * tt:2 * tt + 2], sm[:, :, cols], AX.X, ALU.max)
            link(last)
        dve.tensor_scalar(mx[:, 1, :], mx[:, 0, :], -1.0, None, ALU.mult).then_inc(sem("a_max"), 1)

    def head_exp_act(act, hd):
        act.wait_ge(sem("a_max"), hd + 1)
        if hd:
            act.wait_ge(sem("a_weights"), hd)
        for tt, cols, _ in PARTS3:
            for c in range(2):
                i = 2 * tt + c
                act.activation(pe_[:, c, cols], sm[:, c, cols], ACT.Exp, bias=mx[:, 1, i:i + 1],
                               accum_out=mx[:, 2, i:i + 1]).then_inc(sem("a_exp"), 1)

    def head_weights_dve(dve, link, hd):
        dve.wait_ge(sem("a_exp"), 4 * hd + 4)
        if hd:
            dve.wait_ge(sem("a_wT_tr"), hd)
        link(dve.reciprocal(mx[:, 3, :], mx[:, 2, :]))
        second = mx[:, 3, 1:4:2]
        link(dve.tensor_scalar(second, second, lam[:, 2:3], None, ALU.mult))
        for tt, cols, _ in PARTS3:
            link(dve.tensor_scalar(at_[:, cols], pe_[:, 0, cols], mx[:, 3, 2 * tt:2 * tt + 1], None, ALU.mult))
            last = dve.scalar_tensor_tensor(out=at_[:, cols], in0=pe_[:, 1, cols],
                                            scalar=mx[:, 3, 2 * tt + 1:2 * tt + 2], in1=at_[:, cols],
                                            op0=ALU.mult, op1=ALU.add)
            if tt == 0:
                link(last)
        last.then_inc(sem("a_weights"), 1)

    def head_weights_pe(pe, hd):
        pe.wait_ge(sem("a_weights"), hd + 1)
        if hd:
            pe.wait_ge(sem("a_wT"), hd)
        if hd + H0 - 10 in range(TT):
            pe.wait_ge(sem("lora_T"), hd + H0 - 9)
        for k in range(3):
            last = pe.transpose(bank[7][:, k * P:(k + 1) * P], at_[:, k * P:(k + 1) * P], ident[:])
        last.then_inc(sem("a_wT_tr"), 1)

    def head_weights_act(act, hd):
        act.wait_ge(sem("a_wT_tr"), hd + 1)
        act.activation(atT[:], bank[7][:, 0:3 * P], ACT.Copy).then_inc(sem("a_wT"), 1)

    def head_values_pe(pe, hd):
        pe.wait_ge(sem("a_wT"), hd + 1)
        for tt, _, n in PARTS3:
            for kb in range(n):
                last = pe.matmul(bank[5][:, tt * P:(tt + 1) * P], atT[:, tt + kb, :],
                                 za[:, kb, 2 * AW + hd * P:2 * AW + (hd + 1) * P], start=(kb == 0), stop=(kb == tt))
        last.then_inc(sem("a_pv"), 1)

    def head_out_act(act, hd):
        act.wait_ge(sem("a_pv"), hd + 1)
        act.activation(za[:, :, hd * P:(hd + 1) * P], bank[5][:, 0:T], ACT.Copy).then_inc(sem("a_y"), 1)

    y_heads = za[:, :, 0:AW].rearrange("p t (h d) -> p t h d", d=A_DV)

    def subln_dve(dve, link):
        dve.wait_ge(sem("a_sq"), 1)
        link(dve.tensor_reduce(r16[:].rearrange("p (t h) -> p t h", t=TT),
                               asq[:].rearrange("p t (h d) -> p t h d", d=A_DV), AX.X, ALU.add))
        link(dve.tensor_scalar(r16[:], r16[:], 1.0 / A_DV, SUBLN_EPS, ALU.mult, ALU.add))
        link(rsqrt(dve, link, r16[:]))
        dve.tensor_scalar(r16[:], r16[:], 1.0 - LAMBDA_INIT, None, ALU.mult).then_inc(sem("a_rms"), 1)

    def subln_square_pool(pool):
        pool.wait_ge(sem("a_y"), A_HEADS)
        pool.wait_ge(mm_used, 4 * (base["ab_in"] + N_AB))
        pool.tensor_tensor(asq[:], za[:, :, 0:AW], za[:, :, 0:AW], ALU.mult).then_inc(sem("a_sq"), 1)

    def subln_pool(pool):
        pool.wait_ge(sem("a_rms"), 1)
        pool.wait_ge(sem("subg_in"), 16)
        for tt in range(TT):
            pool.tensor_tensor(y_heads[:, tt], y_heads[:, tt],
                               r16[:, tt * 8:tt * 8 + 8].unsqueeze(2).broadcast_to([P, 8, A_DV]),
                               ALU.mult).then_inc(sem("ya_scaled"), 1)
            pool.wait_ge(sem("ya_scaled"), tt + 1)
            pool.tensor_tensor(y_heads[:, tt], y_heads[:, tt], subg[:].unsqueeze(1).broadcast_to([P, 8, A_DV]),
                               ALU.mult).then_inc(sem("ya_done"), 1)

    lora_cuts = (0, LW, LW + LA, LW + LA + P, LW + LA + 2 * P)

    def lora_transposes_pe(pe, tt):
        pe.wait_ge(sem("lora_act"), 2)
        pe.wait_ge(sem("a_wT"), 10 + tt - H0)
        for j in range(4):
            x = zb[:, tt, 3 * BW + lora_cuts[j]:3 * BW + lora_cuts[j + 1]]
            last = pe.transpose(bank[7][0:lora_cuts[j + 1] - lora_cuts[j], j * P:(j + 1) * P], x, ident[:])
        last.then_inc(sem("lora_tr"), 1)

    def lora_out_act(act, tt):
        act.wait_ge(sem("lora_tr"), tt + 1)
        t = slice(tt * P, (tt + 1) * P)
        b2 = bank[7].rearrange("p (j t) -> p j t", j=4)
        act.activation(loraT[0:LW, 0:2, t], b2[0:LW, 0:2, :], ACT.Copy)
        act.activation(loraT[:, 2:4, t], b2[:, 2:4, :], ACT.Copy).then_inc(sem("lora_T"), 1)

    t1 = at("t1", [P, TT, BW], F32, 96)
    rv, kv, vv = (zb[:, :, i * BW:(i + 1) * BW] for i in range(3))
    heads4 = lambda x: x.rearrange("p t (h c) -> p t h c", c=BH)
    over_t = lambda x: x[:].unsqueeze(1).broadcast_to([P, TT, BW])
    over_c = lambda x: x[:].unsqueeze(3).broadcast_to([P, TT, B_HEADS, BH])
    jobs = [(w, tt, hf) for w in range(3) for tt in range(TT) for hf in range(2)]
    g2v = at("g2v", [P, TT, BW], F32, 195.5)
    XB = (4, 5, 6, 7)
    x_src = (kkv[:], av[:], kv, rv)

    def x_groups(tt):
        return [[x_src[i][:, tt, (4 * g + p) * P:(4 * g + p + 1) * P] for p in range(4)]
                for i in range(4) for g in range(2)]
    x_outs = [[(XT[tt][i][:, 4 * g:4 * g + 4, :], P, 0, 512) for i in range(4) for g in range(2)] for tt in range(TT)]
    slot_of = lambda hd: ((hd // 8) * 2 + hd % 2) * 4 + (hd // 2) % 4
    def halves(x, b, k):
        return x.rearrange("p (j c) -> p j c", c=2 * b)[:, :, k * b:(k + 1) * b]

    flat = lambda x: x[:].rearrange("p i t -> p (i t)")
    DV, DL = 14, 9

    def rwkv_pool(pool):
        last_lo = 4 * (base["ab_in"] + N_AB - 1)
        done = sem("lora_in")
        pool.wait_ge(lo_ready, last_lo + 1)
        pool.dma_start(w2[0:LW, :], A["rwkv_w2"][0]).then_inc(done, 16)
        pool.dma_start(a2[0:LA, :], A["rwkv_a2"][0]).then_inc(done, 16)
        pool.wait_ge(lo_ready, last_lo + 2)
        pool.dma_start(g2[:], A["rwkv_g2"][0].rearrange("(k p) n -> p k n", p=P)).then_inc(done, 16)
        pool.wait_ge(lo_ready, last_lo + 4)
        for dst, n in ((p_w0, "rwkv_w0"), (p_a0, "rwkv_a0"), (p_kk, "rwkv_k_k"), (p_ka, "rwkv_k_a")):
            pool.dma_start(dst[:], A[n][0].partition_broadcast(P)).then_inc(done, 16)
        subln_square_pool(pool)
        pool.wait_ge(sem("lora_mm"), 12)
        pool.memset(ST[:], 0.0).then_inc(sem("st_zero"), 1)
        pool.dma_start(p_rk[:], A["rwkv_r_k"][0].rearrange("h c -> (h c)").partition_broadcast(P))\
            .then_inc(sem("rk_in"), 16)
        pool.dma_start(lnx_g[:], A["rwkv_lnx_g"][0].partition_broadcast(P)).then_inc(sem("lnx_in"), 16)
        pool.dma_start(lnx_b[:], A["rwkv_lnx_b"][0].partition_broadcast(P)).then_inc(sem("lnx_in"), 16)
        pool.wait_ge(sem("rw_prev"), 1)
        pool.wait_ge(sem("a_rms"), 1)
        for s in range(2):
            pool.memset(tmp_set[s][2][:], 0.0).then_inc(sem("y1_zero"), 1)
        pool.wait_ge(sem("rw_g"), 4)
        tr_all(pool, "x0", 8)
        tr_all(pool, "x1", 8)
        pool.wait_ge(sem("lnx_in"), 32)
        for tt in range(TT):
            for gp in range(2):
                rd = 2 * tt + gp
                bc = lambda x: x.unsqueeze(1).broadcast_to([P, 4, P])
                for s in range(2):
                    g = 2 * gp + s
                    MT, Ti, Y1 = tmp_set[s]
                    pool.wait_ge(sem(f"dv{s}"), DV * rd + 1)
                    T_ = TTi[:, 4 * g:4 * g + 4, :]
                    pool.tensor_tensor(T_, MT[:], bc(m_l1[:]), ALU.mult).then_inc(sem("tt_m"), 1)
                    pool.wait_ge(sem("tt_m"), 2 * rd + s + 1)
                    pool.tensor_tensor(T_, T_, bc(ident[:]), ALU.add).then_inc(sem(f"tt{s}"), 1)
                if tt == 0:
                    g = gv[:, gp, :]
                    o, v = g2v[:, gp, :], vv[:, gp, :].rearrange("p (h c) -> p h c", c=BH)
                    o3 = o.rearrange("p (h c) -> p h c", c=BH)
                    pool.tensor_tensor(o3, v, bon[:, gp, :].unsqueeze(2).broadcast_to([P, B_HEADS, BH]),
                                       ALU.mult).then_inc(sem("gated_y"), 1)
                    pool.wait_ge(sem("gated_y"), 4 * gp + 1)
                    pool.tensor_tensor(o, o, lnx_b[:], ALU.add).then_inc(sem("gated_y"), 1)
                    pool.wait_ge(sem("gated_y"), 4 * gp + 2)
                    pool.tensor_tensor(o, o, g, ALU.mult).then_inc(sem("gated_y"), 1)
                    pool.wait_ge(sem("gated_y"), 4 * gp + 3)
                    pool.tensor_tensor(g, g, lnx_g[:], ALU.mult).then_inc(sem("gated_y"), 1)
        subln_pool(pool)

    def rwkv_pe(pe):
        pe.wait_ge(sem("lora_T"), 2)
        pe.wait_ge(sem("ev_ab_in"), N_AB)
        pe.wait_ge(sem("a_y"), A_HEADS)
        pe.wait_ge(sem("lora_in"), 112)
        for n, (w, tt, hf) in enumerate(jobs):
            if n >= 4:
                pe.wait_ge(sem("rw_sum"), n - 3)
            o, c, t = bank[2 + n % 4][:], slice(hf * 512, hf * 512 + 512), slice(tt * P, (tt + 1) * P)
            if w < 2:
                last = pe.matmul(o, loraT[0:LW, w, t], (w2, a2)[w][0:LW, c], start=True, stop=True)
            else:
                pe.matmul(o, loraT[:, 2, t], g2[:, 0, c], start=True, stop=False)
                last = pe.matmul(o, loraT[:, 3, t], g2[:, 1, c], start=False, stop=True)
            last.then_inc(sem("lora_mm"), 1)
        pe.wait_ge(sem("rw_g"), 4)
        pe.wait_ge(sem("rw_lw"), 1)
        for tt in range(TT):
            for hf in range(2):
                pe.matmul(bank[2 * tt + hf][:], m_ui[:], lw[:, tt, hf * 512:(hf + 1) * 512], start=True, stop=True)
        for p in range(8):
            for tt in range(TT):
                last = pe.matmul(bank[6][:, 4 * p + 2 * tt:4 * p + 2 * tt + 2], lw[:, tt, p * P:(p + 1) * P],
                                 m_ui[:, CH - 1:P:CH], start=True, stop=True)
        last.then_inc(sem("cum"), 1)
        tr_pe(pe, "x0", x_groups(0), XB, [(sem("rw_x"), 4), (sem("ex"), 3), (sem("rw_prev"), 1)])
        tr_all(pe, "x0", 8)
        tr_pe(pe, "x1", x_groups(1), XB)
        tr_all(pe, "x1", 8)
        for tt in range(TT):
            AT, BT, KT_, RT = XT[tt]
            if tt == 1:
                pe.wait_ge(sem("y_out"), 2)
                pe.wait_ge(sem("st_upd"), 4)
            for gp in range(2):
                rd = 2 * tt + gp
                if gp == 1:
                    for s in range(2):
                        pe.wait_ge(sem(f"dv{s}"), DV * rd)
                        pe.wait_ge(sem(f"y1c{s}"), 5 * rd)
                plan_ = ((BT, AT, 0), (AT, BT, 1), (KT_, AT, 2), (BT, RT, 3))
                for s in range(2):
                    r = slice(64 * s, 64 * s + 64)
                    for l_, r_, bk in plan_:
                        for i in range(4):
                            last = pe.matmul(bank[4 * s + bk][:, i * P:(i + 1) * P], l_[r, 4 * gp + i, :],
                                             r_[r, 4 * gp + i, :], start=True, stop=True)
                        last.then_inc(sem(f"mats{s}"), 1)
                for s in range(2):
                    r = slice(64 * s, 64 * s + 64)
                    pe.wait_ge(sem(f"dv{s}"), DV * rd + 2)
                    for i in range(4):
                        last = pe.matmul(bank[4 * s + 1][:, i * P:(i + 1) * P], KT_[r, 4 * gp + i, :],
                                         RT[r, 4 * gp + i, :], start=True, stop=True)
                    last.then_inc(sem(f"mats{s}"), 1)
                for li in range(1, 6):
                    for s in range(2):
                        MT, Ti, Y1 = tmp_set[s]
                        pe.wait_ge(sem(f"dv{s}"), DV * rd + (2 if li == 1 else 5 + 2 * (li - 1)))
                        for i in range(4):
                            last = pe.matmul(bank[4 * s][:, i * P:(i + 1) * P], MT[:, i, :], Ti[:, i, :],
                                             start=True, stop=True)
                        last.then_inc(sem(f"y1_{s}"), 1)
                    for s in range(2):
                        g = 2 * gp + s
                        MT, Ti, Y1 = tmp_set[s]
                        pe.wait_ge(sem(f"y1c{s}"), 5 * rd + li)
                        if li == 1:
                            pe.wait_ge(sem(f"tt{s}"), rd + 1)
                            pe.wait_ge(sem(f"dv{s}"), DV * rd + 4)
                        if li < 5:
                            for i in range(4):
                                last = pe.matmul(bank[4 * s + 2][:, i * P:(i + 1) * P], TTi[:, 4 * g + i, :],
                                                 Y1[:, i, :], start=True, stop=True)
                            last.then_inc(sem(f"dl{s}"), 1)
                        for i in range(4):
                            last = pe.matmul(bank[4 * s + 3][:, i * P:(i + 1) * P], Y1[:, i, :],
                                             TTi[:, 4 * g + i, :], start=True, stop=True)
                        last.then_inc(sem(f"dl{s}"), 1)
            for s in range(2):
                pe.wait_ge(sem(f"dv{s}"), DV * (2 * tt + 2))
                pe.wait_ge(sem(f"y1c{s}"), 5 * (2 * tt + 2))
            pe.wait_ge(sem("st_zero"), 1)
            for half in range(2):
                c = 2 * tt + half
                rows = slice(64 * half, 64 * half + 64)
                pair = lambda b, p: bank[b + p // 4][:, (p % 4) * P:(p % 4 + 1) * P]
                head = lambda b, hd: bank[b + hd // 8][rows, (hd % 8) * BH:(hd % 8 + 1) * BH]
                if c:
                    pe.wait_ge(sem("x_out0"), c)
                    pe.wait_ge(sem("x_out1"), c)
                for hd in range(16):
                    pe.matmul(head(0, hd), NT[rows, slot_of(hd), rows], vv[rows, tt, hd * BH:(hd + 1) * BH], start=(hd % 8 == 0), stop=False)
                for p in range(8):
                    if c and p % 4 == 0:
                        pe.wait_ge(sem("st_upd"), 2 * c - 1 + p // 4)
                    last = pe.matmul(pair(0, p)[rows, :], AT[:, p, rows], ST[:, p, :], start=False, stop=(p % 4 == 3))
                    if p % 4 == 3:
                        last.then_inc(sem("x_mm"), 1)
                if c < 3:
                    for p in range(8):
                        cc = slice(p * P, (p + 1) * P)
                        pe.matmul(pair(6, p), ident[:], ST[:, p, :], start=(p % 4 == 0), stop=False)
                        pe.matmul(pair(6, p), kv[rows, tt, cc], vv[rows, tt, cc], start=False, stop=False)
                for hd in range(16):
                    if hd % 8 == 0:
                        pe.wait_ge(sem(f"x_out{hd // 8}"), c + 1)
                    last = pe.matmul(head(2, hd), TTi[rows, slot_of(hd), rows],
                                     Xs[rows, hd * BH:(hd + 1) * BH], start=True, stop=True)
                    if hd % 8 == 7:
                        last.then_inc(sem("u_mm"), 1)
                if c:
                    pe.wait_ge(sem("y_out"), c)
                for p in range(8):
                    pe.matmul(pair(4, p)[rows, :], RT[:, p, rows], ST[:, p, :], start=(p % 4 == 0), stop=False)
                    for hd in (2 * p, 2 * p + 1):
                        pe.matmul(head(4, hd), QT[rows, slot_of(hd), rows],
                                  vv[rows, tt, hd * BH:(hd + 1) * BH], start=False, stop=False)
                if c < 3:
                    for p in range(8):
                        if p % 4 == 0:
                            pe.wait_ge(sem(f"u_out{p // 4}"), c + 1)
                        cc = slice(p * P, (p + 1) * P)
                        last = pe.matmul(pair(6, p), av[rows, tt, cc], Us[rows, cc], start=False, stop=(p % 4 == 3))
                        if p % 4 == 3:
                            last.then_inc(sem("s_mm"), 1)
                else:
                    for e in range(2):
                        pe.wait_ge(sem(f"u_out{e}"), c + 1)
                for hd in range(16):
                    last = pe.matmul(head(4, hd), PT[rows, slot_of(hd), rows],
                                     Us[rows, hd * BH:(hd + 1) * BH], start=False, stop=(hd % 8 == 7))
                last.then_inc(sem("y_mm"), 1)

    def rwkv_act(act):
        for w, x in enumerate((lw, av)):
            act.wait_ge(sem("rw_sum"), 4 * w + 4)
            act.activation(x[:], x[:], ACT.Sigmoid).then_inc(sem("rw_sig"), 1)
        for n in range(8, 12):
            _, tt, hf = jobs[n]
            act.wait_ge(sem("lora_mm"), n + 1)
            act.activation(gv[:, tt, hf * 512:(hf + 1) * 512], bank[2 + n % 4][:], ACT.Copy).then_inc(sem("rw_g"), 1)
        act.wait_ge(sem("cum"), 1)
        act.activation(ex1[:], psum[:, 0:4 * 512], ACT.Exp).then_inc(sem("ex"), 1)
        act.activation(ex2[:], psum[:, 0:4 * 512], ACT.Exp, scale=-1.0).then_inc(sem("ex"), 1)
        act.activation(WL[:], bank[6][:, 0:32], ACT.Exp).then_inc(sem("ex"), 1)
        act.wait_ge(sem("rw_prev"), 1)
        act.activation(lw[:], lw[:], ACT.Exp).then_inc(sem("ex"), 1)
        tr_out(act, "x0", x_outs[0], XB, 0)
        tr_out(act, "x1", x_outs[1], XB, 0)
        for tt in range(TT):
            for half in range(2):
                c = 2 * tt + half
                rows = slice(64 * half, 64 * half + 64)
                act.wait_ge(sem("x_mm"), 2 * c + 1)
                act.activation(Xs[rows, 0:512], bank[0][rows, :], ACT.Copy).then_inc(sem("x_out0"), 1)
                act.wait_ge(sem("u_mm"), 2 * c + 1)
                act.activation(Us[rows, 0:512], bank[2][rows, :], ACT.Copy).then_inc(sem("u_out0"), 1)
                act.wait_ge(sem("y_mm"), c + 1)
                act.activation(zb[rows, tt, 0:BW], psum[rows, 4 * 512:6 * 512], ACT.Copy).then_inc(sem("y_out"), 1)

    def rwkv_dve(dve, link):
        dve.wait_ge(sem("mixed"), N_AB - R0)
        dve.wait_ge(sem("a_wT_tr"), A_HEADS)
        for n in range(8):
            w, tt, hf = jobs[n]
            c = slice(hf * 512, (hf + 1) * 512)
            dve.wait_ge(sem("lora_mm"), n + 1)
            dve.tensor_tensor((lw, av)[w][:, tt, c], bank[2 + n % 4][:], (p_w0, p_a0)[w][:, c],
                              ALU.add).then_inc(sem("rw_sum"), 1)
        dve.wait_ge(sem("rw_sig"), 1)
        dve.tensor_scalar(lw[:], lw[:], -math.exp(-0.5), None, ALU.mult).then_inc(sem("rw_lw"), 1)
        link(dve.tensor_tensor(kkv[:], kv, over_t(p_kk), ALU.mult))
        link(dve.tensor_tensor(t1[:], kkv[:], kkv[:], ALU.mult))
        n32 = nrm[:].rearrange("p t h -> p (t h)")
        link(dve.tensor_reduce(nrm[:], heads4(t1[:]), AX.X, ALU.add))
        link(dve.tensor_scalar(n32, n32, 1e-24, None, ALU.max))
        link(rsqrt(dve, link, n32))
        link(dve.tensor_tensor(heads4(kkv[:]), heads4(kkv[:]), over_c(nrm), ALU.mult))
        dve.wait_ge(sem("rw_sig"), 2)
        link(dve.tensor_scalar(t1[:], av[:], -1.0, None, ALU.add))
        link(dve.tensor_tensor(t1[:], t1[:], over_t(p_ka), ALU.mult))
        link(dve.scalar_tensor_tensor(out=kv, in0=t1[:], scalar=1.0, in1=kv, op0=ALU.add, op1=ALU.mult))
        dve.tensor_tensor(av[:], kkv[:], av[:], ALU.mult).then_inc(sem("rw_b"), 1)
        dve.wait_ge(sem("rw_b"), 1)
        link(dve.tensor_tensor(t1[:], rv, kv, ALU.mult))
        dve.wait_ge(sem("rk_in"), 16)
        link(dve.tensor_tensor(t1[:], t1[:], over_t(p_rk), ALU.mult))
        link(dve.tensor_reduce(bon[:], heads4(t1[:]), AX.X, ALU.add))
        dve.wait_ge(sem("ex"), 3)
        dve.tensor_tensor(lw[:], psum[:, 0:2048].rearrange("p (t n) -> p t n", t=TT), lw[:],
                          ALU.subtract).then_inc(sem("rw_prev"), 1)
        dve.tensor_tensor(rv, rv, ex1[:], ALU.mult).then_inc(sem("rw_x"), 1)
        dve.tensor_tensor(kv, kv, ex2[:], ALU.mult).then_inc(sem("rw_x"), 1)
        dve.tensor_tensor(av[:], av[:], ex2[:], ALU.mult).then_inc(sem("rw_x"), 1)
        dve.wait_ge(sem("ex"), 4)
        dve.scalar_tensor_tensor(out=kkv[:], in0=kkv[:], scalar=-1.0, in1=lw[:], op0=ALU.mult,
                                 op1=ALU.mult).then_inc(sem("rw_x"), 1)
        subln_dve(dve, link)
        dve.wait_ge(sem("rw_x"), 4)
        tr_out(dve, "x0", x_outs[0], XB, 1)
        tr_out(dve, "x1", x_outs[1], XB, 1)
        dve.wait_ge(sem("y1_zero"), 2)
        for tt in range(TT):
            for gp in range(2):
                rd = 2 * tt + gp
                bc = lambda x: x.unsqueeze(1).broadcast_to([P, 4, P])
                b4 = lambda i: bank[i].rearrange("p (i t) -> p i t", i=4)
                for s in range(2):
                    MT, Ti, Y1 = tmp_set[s]
                    dv = sem(f"dv{s}")
                    dve.wait_ge(sem(f"mats{s}"), 5 * rd + 1)
                    if rd:
                        dve.wait_ge(sem(f"tt{s}"), rd)
                    dve.tensor_tensor(MT[:], b4(4 * s), bc(m_su[:]), ALU.mult).then_inc(dv, 1)
                    dve.wait_ge(sem(f"mats{s}"), 5 * rd + 2)
                    link(dve.tensor_tensor(Ti[:], b4(4 * s + 1), bc(m_lvt[:, 0, :]), ALU.mult))
                    dve.tensor_tensor(Ti[:], Ti[:], bc(ident[:]), ALU.add).then_inc(dv, 1)
                for s in range(2):
                    g = 2 * gp + s
                    dv = sem(f"dv{s}")
                    sl = slice(4 * g, 4 * g + 4)
                    dve.wait_ge(sem(f"mats{s}"), 5 * rd + 4)
                    dve.tensor_tensor(NT[:, sl, :], b4(4 * s + 2), bc(m_su[:]), ALU.mult).then_inc(dv, 1)
                    dve.tensor_tensor(PT[:, sl, :], b4(4 * s + 3), bc(m_ui[:]), ALU.mult).then_inc(dv, 1)
                    dve.wait_ge(sem(f"mats{s}"), 5 * rd + 5)
                    dve.tensor_tensor(QT[:, sl, :], b4(4 * s + 1), bc(m_ui[:]), ALU.mult).then_inc(dv, 1)
                for li in range(1, 6):
                    for s in range(2):
                        dve.wait_ge(sem(f"y1_{s}"), 5 * rd + li)
                        quarters = lambda x: x.rearrange("p i (j c) -> p i j c", c=2 << li)[:, :, :, 0:1 << li]
                        dve.tensor_tensor(quarters(tmp_set[s][2][:]), quarters(b4(4 * s)),
                                          quarters(bc(m_lvt[:, li, :])), ALU.mult).then_inc(sem(f"y1c{s}"), 1)
                    for s in range(2):
                        g = 2 * gp + s
                        MT, Ti, Y1 = tmp_set[s]
                        dv, T_ = sem(f"dv{s}"), halves(TTi[:, 4 * g:4 * g + 4, :].rearrange("p i t -> p (i t)"), 1 << li, 1)
                        if li < 5:
                            dve.wait_ge(sem(f"dl{s}"), DL * rd + 2 * li)
                            x = halves(flat(Ti), 1 << li, 0)
                            dve.tensor_tensor(x, x, halves(bank[4 * s + 2], 1 << li, 0), ALU.add).then_inc(dv, 1)
                        else:
                            dve.wait_ge(sem(f"dl{s}"), DL * rd + 9)
                        dve.scalar_tensor_tensor(out=T_, in0=halves(bank[4 * s + 3], 1 << li, 1),
                                                 scalar=first_half[:, li:li + 1], in1=T_, op0=ALU.mult,
                                                 op1=ALU.add).then_inc(dv, 1)
            for half in range(2):
                c = 2 * tt + half
                rows = slice(64 * half, 64 * half + 64)
                dve.wait_ge(sem("x_mm"), 2 * c + 2)
                dve.tensor_copy(Xs[rows, 512:1024], bank[1][rows, :]).then_inc(sem("x_out1"), 1)
                dve.wait_ge(sem("u_mm"), 2 * c + 2)
                dve.tensor_copy(Us[rows, 512:1024], bank[3][rows, :]).then_inc(sem("u_out1"), 1)
                for g in range(2 if c < 3 else 0):
                    dve.wait_ge(sem("s_mm"), 2 * c + 1 + g)
                    for e in range(2):
                        hs = slice(64 * e, 64 * e + 64)
                        x2 = bank[6 + g][hs, :].rearrange("p (a t) -> p a t", a=4)[:, :, hs]
                        last = dve.tensor_tensor(ST[hs, 4 * g:4 * g + 4, hs], x2,
                                                 WL[hs, 4 * g:4 * g + 4, c:c + 1].broadcast_to([64, 4, 64]), ALU.mult)
                    last.then_inc(sem("st_upd"), 1)
        for tt in range(TT):
            dve.wait_ge(sem("y_out"), 2 * tt + 2)
            y, s = rv[:, tt, :], nrm[:, tt, :]
            y3, sq = y.rearrange("p (h c) -> p h c", c=BH), Xs[:].rearrange("p (h c) -> p h c", c=BH)
            over = s.unsqueeze(2).broadcast_to([P, B_HEADS, BH])
            link(dve.tensor_reduce(s, y3, AX.X, ALU.add))
            link(dve.tensor_scalar(s, s, -1.0 / BH, None, ALU.mult))
            link(dve.tensor_tensor(y3, y3, over, ALU.add))
            link(dve.tensor_tensor(sq, y3, y3, ALU.mult))
            link(dve.tensor_reduce(s, sq, AX.X, ALU.add))
            link(dve.tensor_scalar(s, s, 1.0 / BH, LNX_EPS, ALU.mult, ALU.add))
            link(rsqrt(dve, link, s))
            link(dve.tensor_tensor(y3, y3, over, ALU.mult))
            dve.wait_ge(sem("gated_y"), 4 * tt + 4)
            link(dve.tensor_tensor(y, y, gv[:, tt, :], ALU.mult))
            dve.tensor_tensor(y, y, g2v[:, tt, :], ALU.add).then_inc(sem("yb_done"), 1)

    C1, C2 = C_HEADS * C_HD, C_HEADS * C_HD + C_KV * C_HD
    C3 = C2 + C_KV * C_HD
    C4 = C3 + IDX_H * IDX_D
    C5 = C4 + IDX_D
    zc = at("zc", [P, TT, C_IN], F32, 120)
    qTc = at("qTc", [P, C_HEADS, T], F32, 153)
    kTc = at("kTc", [P, C_KV, T], F32, 169)
    qiT = at("qiT", [P, IDX_H // 2, T], F32, 173)
    kiT = at("kiT", [P, T], F32, 181)
    score = at("score", [P, TT, T], F32, 182)
    mb = at("mb", [P, TT, T], F32, 184)
    rl_ = at("rl_", [P, 2, 2, T], F32, 186)
    smc = at("smc", [P, 2, 2, T], F32, 190)
    pc = at("pc", [P, 2, 2, T], F32, 194)
    pcT = at("pcT", [P, 2, 4, P], F32, 198)
    kid = at("kid", [P, TT, P], F32, 202)
    rtc = at("rtc", [P, 4, 256], F32, 203)
    mxc = at("mxc", [P, 2, 8], F32, 16)
    m8 = at("m8", [P, 8], F32, 16.25)
    lns = at("lns", [P, 4], F32, 16.5)
    ikg = at("ikg", [P, 2, IDX_D], F32, 17)
    wis = at("wis", [P, TT, IDX_H], F32, 18)
    ki2 = at("ki2", [P, TT, IDX_D], F32, 19)
    qi_groups = [[zc[:, tt, C3 + hp * P:C3 + (hp + 1) * P] for hp in (2 * g, 2 * g + 1) for tt in range(TT)]
                 for g in range(4)] + [[kid[:, tt, :] for tt in range(TT)]]
    qi_outs = [(qiT[:, 2 * g:2 * g + 2, :], P, 0, 512) for g in range(4)] + [(kiT[:], P, 0, 256)]
    c_groups = [[zc[:, tt, hd * P:(hd + 1) * P] for hd in (2 * g, 2 * g + 1) for tt in range(TT)] for g in range(10)]
    c_outs = [(qTc[:, 2 * g:2 * g + 2, :], P, 0, 512) for g in range(8)] + \
             [(kTc[:, 2 * g:2 * g + 2, :], P, 0, 512) for g in range(2)]
    c_units = [(tt, hp) for tt in range(TT) for hp in range(8)]
    nu = len(c_units)

    def c_in_pe(pe):
        st, b = "c_in", base["c_in"]
        ev = sem("ev_c_in")
        pe_first(pe, st, b, b % 2, h_src, h_ready(st), C_W, free_of(st, 0))
        mm_slab(pe, b + 1, (b + 1) % 2, C_W, free_of(st, 1))
        with pe.Fori(1, 4) as i:
            for j in range(2):
                mm_slab(pe, b + 2 * i + j, (b + j) % 2, C_W, (ev, 2 * i + j - 1))
        mm_slab(pe, b + 8, b % 2, C_W, (ev, 7))

    def c_in_act(act):
        st, b = "c_in", base["c_in"]
        prologue(split_hi, act, st)
        act_first(act, st, b, C_W, GAIN[st], h_squares(act, st))

        def keep(i, par_):
            def f():
                act.wait_ge(mm_used, 4 * (b + i) + 4)
                for tt in range(TT):
                    last = act.activation(zc[:, tt, bass.ds(i * C_W, C_W)], bank[2 * par_ + tt][:, 0:C_W], ACT.Copy,
                                          scale=rstd_h[:, tt:tt + 1])
                last.then_inc(sem("ev_c_in"), 1)
            return f
        act.wait_ge(*mark("rstd", st, 1))
        step(split_hi, act, b, st, C_W, keep(0, b % 2), skip=True)
        step(split_hi, act, b + 1, st, C_W, keep(1, (b + 1) % 2))
        with act.Fori(1, 4) as i:
            for j in range(2):
                step(split_hi, act, b + 2 * i + j, st, C_W, keep(2 * i + j, (b + j) % 2))
        step(split_hi, act, b + 8, st, None, keep(8, b % 2))

    def c_in_dve(dve, link):
        st, b = "c_in", base["c_in"]
        prologue(split_lo, dve, st)
        h_first(dve, link, st, b, C_W, GAIN[st], prv[st])
        step(split_lo, dve, b, st, C_W, None, skip=True)
        with dve.Fori(1, 8) as i:
            step(split_lo, dve, b + i, st, C_W, None)
        step(split_lo, dve, b + 8, st, None, None)

    def c_pool(pool):
        pool.wait_ge(mm_used, 4 * (base["c_in"] + 9))
        for i, n in enumerate(("idx_k_g", "idx_k_b")):
            pool.dma_start(ikg[:, i, :], A[n][0].partition_broadcast(P)).then_inc(sem("ikg_in"), 16)

    def c_pe(pe):
        tr_pe(pe, "qi", qi_groups, QB, [(sem("qi_roped"), 1)])
        tr_all(pe, "qi", 5)
        for i, (tt, hp) in enumerate(c_units):
            nk = (tt + 1) * P
            if i >= 2:
                pe.wait_ge(sem("i_relu"), i - 1)
            for j in range(2):
                r = slice(64 * j, 64 * j + 64)
                last = pe.matmul(bank[2 * (i % 2) + j][:, 0:nk], qiT[r, hp, tt * P:(tt + 1) * P], kiT[r, 0:nk],
                                 start=True, stop=True)
            last.then_inc(sem("i_mm"), 1)
        tr_pe(pe, "qc", c_groups, QB, [(sem("qc_roped"), 1)])
        tr_all(pe, "qc", 10)
        pe.wait_ge(sem("i_relu"), nu)
        for i in range(nu + 2):
            if i < nu:
                tt, hp = c_units[i]
                nk = (tt + 1) * P
                if i >= 2:
                    pe.wait_ge(sem("c_masked"), i - 1)
                for j in range(2):
                    last = pe.matmul(bank[2 * (i % 2) + j][:, 0:nk], qTc[:, 2 * hp + j, tt * P:(tt + 1) * P],
                                     kTc[:, hp // 2, 0:nk], start=True, stop=True)
                last.then_inc(sem("c_scores"), 1)
            if 0 <= i - 1 < nu:
                u = i - 1
                tt, hp = c_units[u]
                pe.wait_ge(sem("c_exp"), 2 * u + 2)
                if u >= 2:
                    pe.wait_ge(sem("c_wT"), u - 1)
                for j in range(2):
                    for kb in range(tt + 1):
                        q = j * (tt + 1) + kb
                        last = pe.transpose(bank[4 + u % 2][:, q * P:(q + 1) * P], pc[:, u % 2, j, kb * P:(kb + 1) * P],
                                            ident[:])
                last.then_inc(sem("c_tr"), 1)
            if 0 <= i - 2 < nu:
                u = i - 2
                tt, hp = c_units[u]
                pe.wait_ge(sem("c_wT"), u + 1)
                if u >= 2:
                    pe.wait_ge(sem("c_y"), u - 1)
                for j in range(2):
                    for kb in range(tt + 1):
                        last = pe.matmul(bank[6 + u % 2][:, j * P:(j + 1) * P], pcT[:, u % 2, j * (tt + 1) + kb, :],
                                         zc[:, kb, C2 + (hp // 2) * P:C2 + (hp // 2 + 1) * P],
                                         start=(kb == 0), stop=(kb == tt))
                last.then_inc(sem("c_pv"), 1)

    def c_act(act):
        tr_out(act, "qi", qi_outs, QB, 0)
        for i, (tt, hp) in enumerate(c_units):
            nk = (tt + 1) * P
            act.wait_ge(sem("i_mm"), i + 1)
            if i >= 2:
                act.wait_ge(sem("i_added"), 2 * (i - 1))
            x = psum[:, 1024 * (i % 2):1024 * (i % 2) + 1024].rearrange("p (c k) -> p c k", c=2)[:, :, 0:nk]
            act.activation(rl_[:, i % 2, :, 0:nk], x, ACT.Relu).then_inc(sem("i_relu"), 1)
        tr_out(act, "qc", c_outs, QB, 0)
        for i in range(nu + 2):
            if i < nu:
                tt, hp = c_units[i]
                nk = (tt + 1) * P
                act.wait_ge(sem("c_max"), i + 1)
                for j in range(2):
                    act.activation(pc[:, i % 2, j, 0:nk], smc[:, i % 2, j, 0:nk], ACT.Exp,
                                   bias=mxc[:, i % 2, 2 + j:3 + j],
                                   accum_out=mxc[:, i % 2, 4 + j:5 + j]).then_inc(sem("c_exp"), 1)
            if 0 <= i - 2 < nu:
                u = i - 2
                tt, hp = c_units[u]
                act.wait_ge(sem("c_pv"), u + 1)
                act.wait_ge(sem("c_rl"), u + 1)
                for j in range(2):
                    hd = 2 * hp + j
                    last = act.activation(zc[:, tt, hd * P:(hd + 1) * P], bank[6 + u % 2][:, j * P:(j + 1) * P],
                                          ACT.Copy, scale=rlc[:, u % 4, j:j + 1])
                last.then_inc(sem("c_y"), 1)

    rlc = at("rlc", [P, 4, 2], F32, 16.75)

    def c_dve(dve, link):
        dve.wait_ge(sem("ev_c_in"), 9)
        dve.wait_ge(mm_used, 4 * (base["c_in"] + 9))
        dve.wait_ge(sem("trig"), 2)
        x = zc[:, :, C4:C5]
        over64 = lambda v: v.unsqueeze(2).broadcast_to([P, TT, IDX_D])
        mean, var = lns[:, 0:2], lns[:, 2:4]
        link(dve.tensor_reduce(mean, x, AX.X, ALU.add))
        link(dve.tensor_scalar(mean, mean, -1.0 / IDX_D, None, ALU.mult))
        link(dve.tensor_tensor(x, x, over64(mean), ALU.add))
        link(dve.tensor_tensor(ki2[:], x, x, ALU.mult))
        link(dve.tensor_reduce(var, ki2[:], AX.X, ALU.add))
        link(dve.tensor_scalar(var, var, 1.0 / IDX_D, LN_EPS, ALU.mult, ALU.add))
        link(rsqrt(dve, link, var))
        link(dve.tensor_tensor(x, x, over64(var), ALU.mult))
        dve.wait_ge(sem("ikg_in"), 32)
        link(dve.tensor_tensor(x, x, ikg[:, 0, :].unsqueeze(1).broadcast_to([P, TT, IDX_D]), ALU.mult))
        link(dve.tensor_tensor(x, x, ikg[:, 1, :].unsqueeze(1).broadcast_to([P, TT, IDX_D]), ALU.add))
        link(dve.tensor_scalar(wis[:], zc[:, :, C5:C_IN], float((IDX_H * IDX_D) ** -0.5), None, ALU.mult))
        for tt in range(TT):
            link(rope(dve, link, zc[:, tt, C4:C5].unsqueeze(1), tt, 0, HALF_A, rtc))
            link(rope(dve, link, zc[:, tt, C3:C4].rearrange("p (h d) -> p h d", d=IDX_D), tt, 0, HALF_A, rtc))
            for j in range(2):
                last = dve.tensor_copy(kid[:, tt, j * 64:(j + 1) * 64], zc[:, tt, C4:C5])
        last.then_inc(sem("qi_roped"), 1)
        tr_out(dve, "qi", qi_outs, QB, 1)
        for tt in range(TT):
            link(rope(dve, link, zc[:, tt, 0:C1].rearrange("p (h d) -> p h d", d=C_HD), tt, HALF_A, HALF_C, rtc))
            last = rope(dve, link, zc[:, tt, C1:C2].rearrange("p (h d) -> p h d", d=C_HD), tt, HALF_A, HALF_C, rtc)
            if tt == 0:
                link(last)
        last.then_inc(sem("qc_roped"), 1)
        added = sem("i_added")
        for i, (tt, hp) in enumerate(c_units):
            nk = (tt + 1) * P
            dve.wait_ge(sem("i_relu"), i + 1)
            for j in range(2):
                w_, sc, x = wis[:, tt, 2 * hp + j:2 * hp + j + 1], score[:, tt, 0:nk], rl_[:, i % 2, j, 0:nk]
                if hp + j == 0:
                    dve.tensor_scalar(sc, x, w_, None, ALU.mult).then_inc(added, 1)
                else:
                    dve.scalar_tensor_tensor(out=sc, in0=x, scalar=w_, in1=sc, op0=ALU.mult,
                                             op1=ALU.add).then_inc(added, 1)
                dve.wait_ge(added, 2 * i + j + 1)
        tr_out(dve, "qc", c_outs, QB, 1)
        for tt in range(TT):
            nk = (tt + 1) * P
            sc, ca = score[:, tt, 0:nk], causal[:, T - nk:T]
            link(dve.tensor_tensor(sc, sc, ca, ALU.add))
            for _ in range(TOPK // 8):
                link(dve.max(m8[:], sc))
                link(dve.match_replace(sc, m8[:], sc, TAKEN))
            link(dve.tensor_scalar(mb[:, tt, 0:nk], sc, TAKEN / 2, NEG, ALU.is_gt, ALU.mult))
            link(dve.tensor_tensor(mb[:, tt, 0:nk], mb[:, tt, 0:nk], ca, ALU.add))
        for i in range(nu + 1):
            if i < nu:
                tt, hp = c_units[i]
                nk = (tt + 1) * P
                dve.wait_ge(sem("c_scores"), i + 1)
                if i >= 2:
                    dve.wait_ge(sem("c_exp"), 2 * (i - 1))
                x = psum[:, 1024 * (i % 2):1024 * (i % 2) + 1024].rearrange("p (c k) -> p c k", c=2)[:, :, 0:nk]
                y = smc[:, i % 2, :, 0:nk]
                dve.scalar_tensor_tensor(out=y, in0=x, scalar=C_HD ** -0.5,
                                         in1=mb[:, tt, 0:nk].unsqueeze(1).broadcast_to([P, 2, nk]), op0=ALU.mult,
                                         op1=ALU.add).then_inc(sem("c_masked"), 1)
                dve.wait_ge(sem("c_masked"), i + 1)
                link(dve.tensor_reduce(mxc[:, i % 2, 0:2], y, AX.X, ALU.max))
                dve.tensor_scalar(mxc[:, i % 2, 2:4], mxc[:, i % 2, 0:2], -1.0, None,
                                  ALU.mult).then_inc(sem("c_max"), 1)
            if i >= 1:
                u = i - 1
                tt, hp = c_units[u]
                dve.wait_ge(sem("c_exp"), 2 * u + 2)
                if u >= 4:
                    dve.wait_ge(sem("c_y"), u - 3)
                dve.reciprocal(rlc[:, u % 4, :], mxc[:, u % 2, 4:6]).then_inc(sem("c_rl"), 1)
                dve.wait_ge(sem("c_tr"), u + 1)
                if u >= 2:
                    dve.wait_ge(sem("c_pv"), u - 1)
                nq = 2 * (tt + 1)
                dve.tensor_copy(pcT[:, u % 2, 0:nq, :], bank[4 + u % 2][:, 0:nq * P]).then_inc(sem("c_wT"), 1)

    def y_src(st):
        y = za if st == "ab_out" else zc
        return lambda tt, b: (zb[:, tt, (b - 2) * W:(b - 1) * W] if st == "ab_out" and b >= 2 else
                              y[:, tt, b * W:(b + 1) * W])

    def y_ready(st):
        if st == "ab_out":
            return lambda tt, b: (sem("ya_done"), tt + 1) if b < 2 else (sem("yb_done"), tt + 1)
        return lambda tt, b: (sem("c_y"), nu)

    mats = {"ab_in": A["ab_w_in"][0], "ab_out": A["ab_w_out"][0], "c_in": A["c_w_in"][0], "c_out": A["c_w_out"][0]}
    end = order[-1]
    block = ctx.enter_context(nc.Block())

    @block.sync
    def _(sp):
        sp.dma_start(h[:], A["x"][0].rearrange("(t p) d -> p t d", p=P)).then_inc(sem("x_in"), 16)
        for st in order:
            b = base[st]
            if st.startswith("mlp"):
                l = int(st[-1])
                up = A["w_mlp_up"][l]
                down = A["w_mlp_down"][l]

                def quarter(Q, first):
                    for j in range(4):
                        load_slab(sp, b + 8 * Q + j, w_chunks(up, 0), Q * 4 * W + j * W, W, first and j == 0)
                    for j in range(4):
                        load_slab(sp, b + 8 * Q + 4 + j, w_chunks(down, Q), j * W, W)
                quarter(0, b == 0)
                with sp.Fori(1, 4) as Q:
                    quarter(Q, False)
            elif st.startswith("ple"):
                for j in range(4):
                    load_slab(sp, b + j, w_chunks(A["w_ple_gate"][int(st[-1])], 0), j * W, W, b + j == 0)
            elif st == "ab_in":
                for i, c in enumerate(ab_cols):
                    load_slab(sp, b + i, w_chunks(mats[st], 0), c, ab_slabs[i][2], b + i == 0)
            elif st == "c_in":
                w = w_chunks(mats[st], 0)
                load_slab(sp, b, w, 0, C_W, b == 0)
                with sp.Fori(1, 9) as i:
                    load_slab(sp, b + i, w, i * C_W, C_W)
            else:
                if st == "ab_out":
                    sp.wait_ge(sem("gated_y"), 8)
                for j in range(4):
                    load_slab(sp, b + j, w_chunks(mats[st], 0), j * W, W)
        for tt in range(TT):
            sp.wait_ge(*mark("h_ready", "end", 8))
            sp.dma_start(A["out"][0][tt * P:(tt + 1) * P, :], h[:, tt, :]).then_inc(sem("stored"), 16)
        sp.wait_ge(sem("stored"), 32)

    @block.gpsimd
    def _(pool):
        pool_setup(pool)
        for st in order:
            if st == "ab_in":
                ab_in_pool(pool)
                rwkv_pool(pool)
            if st == "c_in":
                c_pool(pool)
            if st.startswith("ple"):
                l = int(st[-1])
                if prv[st]:
                    pool.wait_ge(*mark("xT_lo", prv[st], 8))
                pool.dma_start(wple[:], A["w_ple_proj"][l].rearrange("(k p) n -> p k n", p=P))\
                    .then_inc(sem("ple_in"), 16)
                pool.dma_start(pin[:], A["p"][l, 0].rearrange("(t p) n -> p t n", p=P))\
                    .then_inc(sem("ple_in"), 16)
            if not st.endswith("_in"):
                g = {"ab_out": A["mix_post_g"][0], "c_out": A["mix_post_g"][1], "mlp0": A["mlp_post_g"][0],
                     "mlp1": A["mlp_post_g"][1], "ple0": A["ple_post_g"][0], "ple1": A["ple_post_g"][1]}[st]
                pool.wait_ge(*mark("xT_lo", st, 8))
                pool.dma_start(gpost[:], g.partition_broadcast(P)).then_inc(sem("gpost"), 16)

    @block.scalar
    def _(act):
        act_setup(act)
        for st in order:
            if st.startswith("mlp"):
                l = int(st[-1])
                prologue(split_hi, act, st)
                act_first(act, st, base[st], W, GAIN[st], h_squares(act, st))
                mlp_act(act, l, 0)
                with act.Fori(1, 4) as Q:
                    mlp_act(act, l, Q)
                last_junk[0] = mark("m_sq", st, 32)
            elif st.startswith("ple"):
                prologue(split_hi, act, st)
                ple_act(act, int(st[-1]))
            elif st == "ab_in":
                ab_in_act(act)
                rwkv_act(act)
            elif st == "c_in":
                c_in_act(act)
                c_act(act)
            else:
                out_act(act, st)

    @block.vector
    def _(dve):
        link = Link(dve, sem("dve_chain"))
        dve_setup(dve, link)
        for st in order:
            if st.startswith("mlp"):
                l = int(st[-1])
                prologue(split_lo, dve, st)
                h_first(dve, link, st, base[st], W, GAIN[st], prv[st])
                mlp_dve(dve, l, 0)
                with dve.Fori(1, 4) as Q:
                    mlp_dve(dve, l, Q)
            elif st.startswith("ple"):
                prologue(split_lo, dve, st)
                ple_dve(dve, link, int(st[-1]))
            elif st == "ab_in":
                ab_in_dve(dve, link)
                rwkv_dve(dve, link)
            elif st == "c_in":
                c_in_dve(dve, link)
                c_dve(dve, link)
            else:
                out_dve(dve, st)
        for b in range(4):
            h_update(dve, link, "end", end, b)

    @block.tensor
    def _(pe):
        pe.wait_ge(sem("consts"), N_CONSTS)
        pe.wait_ge(sem("gpre_in"), 64)
        pe.transpose(bank[7][:, 0:4 * KT], g_rows[:], ident[0:4 * KT, 0:4 * KT]).then_inc(sem("gpre_T"), 1)
        for st in order:
            if st.startswith("mlp"):
                l = int(st[-1])
                mlp_pe(pe, l, 0)
                with pe.Fori(1, 4) as Q:
                    mlp_pe(pe, l, Q)
            elif st.startswith("ple"):
                ple_pe(pe, int(st[-1]))
            elif st == "ab_in":
                ab_in_pe(pe)
                rwkv_pe(pe)
            elif st == "c_in":
                c_in_pe(pe)
                c_pe(pe)
            else:
                out_pe(pe, st, y_src(st), y_ready(st))

    ctx.close()


def kernel(**inputs):
    from concourse import bacc
    from concourse.bass_utils import run_bass_kernel_spmd

    nc = bacc.Bacc("TRN2", target_bir_lowering=False, num_devices=1)
    arrays, A = {}, {}
    for name, a in inputs.items():
        a = np.ascontiguousarray(a)
        arrays[f"in_{name}"] = a
        A[name] = nc.dram_tensor(f"in_{name}", a.shape, mybir.dt.from_np(a.dtype), kind="ExternalInput").ap()
    A["out"] = nc.dram_tensor("out_0", (1, T, D), F32, kind="ExternalOutput").ap()
    build(nc, A)
    r = run_bass_kernel_spmd(nc, [arrays], core_ids=[0])
    return r.results[0]["out_0"]
```

```python
from contextlib import ExitStack, contextmanager
import math

import numpy as np
import concourse.bass as bass
from concourse import mybir

F32 = mybir.dt.float32
F32R = mybir.dt.float32r
BF16 = mybir.dt.bfloat16
I32 = mybir.dt.int32
ALU = mybir.AluOpType
ACT = mybir.ActivationFunctionType
AX = mybir.AxisListType

P = 128
T = 256
TT = T // P
D = 2048
KT = D // P
DFF = 4 * D
PLE = 256
AW = 1024
BW = 1024
A_HEADS, A_DV, A_DC = 8, 128, 64
B_HEADS, BH = 16, 64
LW, LA, LG = 96, 96, 256
B_IN = 3 * BW + LW + LA + LG
A_IN = 3 * AW
C_HEADS, C_KV, C_HD = 16, 4, 128
IDX_H, IDX_D = 16, 64
C_IN = C_HEADS * C_HD + 2 * C_KV * C_HD + IDX_H * IDX_D + IDX_D + IDX_H
TOPK = T // 4
THETA = 500000.0
LAMBDA_INIT = 0.8 - 0.6 * math.exp(0.0)
NORM_EPS, SUBLN_EPS, LNX_EPS, LN_EPS = 1e-6, 1e-5, 64e-5, 1e-6
CH = 64
NEG = -1e30
TAKEN = -3e38
W = 512
KB = 1024
C_W = (IDX_H * IDX_D + IDX_D + IDX_H) // 3
FULL = ("ab", "mlp0", "ple0", "c", "mlp1", "ple1")


def plan_slabs(plan):
    base, s = {}, 0
    for st in plan:
        parts = {"ab": (("ab_in", 13), ("ab_out", 4)), "c": (("c_in", 9), ("c_out", 4))}.get(
            st, ((st, 32),) if st.startswith("mlp") else ((st, 4),))
        for name, n in parts:
            base[name] = s
            s += n
    return base


class Link:

    def __init__(self, eng, sem):
        self.eng, self.sem, self.n, self.extra = eng, sem, 0, 0

    def __call__(self, ins):
        ins.then_inc(self.sem, 1)
        self.n += 1
        self.eng.wait_ge(self.sem, self.extra + self.n)

    @contextmanager
    def loop(self, i, first, count, per):
        start = self.n
        self.extra = (i - first) * per
        yield
        assert self.n - start == per, (self.n - start, per)
        self.extra, self.n = 0, start + per * count


def build(nc, A, plan=FULL):
    base = plan_slabs(plan)
    ctx = ExitStack()
    sems = {}

    def sem(name):
        if name not in sems:
            sems[name] = ctx.enter_context(nc.semaphore(name))
        return sems[name]

    arena_bytes = 207 * KB + 768
    arena = ctx.enter_context(nc.sbuf_tensor("arena", [P, arena_bytes // 4], F32))
    origin = 16512

    def at(name, shape, dt, kb):
        size = int(np.prod(shape[1:])) * (2 if dt == BF16 else 4)
        assert kb * KB + size <= arena_bytes, name
        return nc.alloc_sbuf_tensor_at(name, shape, dt, offset=int(origin + kb * KB))

    psum = ctx.enter_context(nc.psum_tensor("psum", [P, 8 * 512], F32))
    bank = [psum[:, i * 512:(i + 1) * 512] for i in range(8)]

    h = at("h", [P, TT, D], F32, 0)
    uTh = at("uTh", [P, KT, T], F32R, 16)
    uTl = at("uTl", [P, KT, T], F32R, 32)
    raw = at("raw", [P, 4, 4, W], F32, 48)
    whi = at("whi", [P, 2, 4, W], F32R, 80)
    wlo = at("wlo", [P, 2, 4, W], F32R, 96)
    ident = at("ident", [P, P], F32, 112)
    m_su = at("m_su", [P, P], F32, 112.5)
    m_ui = at("m_ui", [P, P], F32, 113)
    m_l1 = at("m_l1", [P, P], F32, 113.5)
    m_lvt = at("m_lvt", [P, 6, P], F32, 114)
    causal = at("causal", [P, T], F32, 117)
    junk = at("junk", [P, W], BF16, 118)
    cosT = at("cosT", [P, TT, 24], F32, 119)
    sinT = at("sinT", [P, TT, 24], F32, 119.1875)
    gpre = at("gpre", [P, 4, KT], F32, 119.375)
    nwt = at("nwt", [P, 2, 32], F32, 207.5)
    g_rows = at("g_rows", [4 * KT, P], F32, 118)
    ssq = at("ssq", [P, TT, 4], F32, 119.625)
    hss = at("hss", [P, TT, 4], F32, 119.65625)
    st2 = at("st2", [P, 8], F32, 119.6875)
    rstd_m = at("rstd_m", [P, TT], F32, 119.71875)
    rstd_h = at("rstd_h", [P, TT], F32, 119.75)
    lam = at("lam", [P, 4], F32, 119.78125)
    first_half = at("first_half", [P, 6], F32, 119.8125)

    m = at("m", [P, TT, D], F32, 120)
    gpost = at("gpost", [P, D], F32, 136)
    hid = at("hid", [P, 2, TT, W], F32, 144)
    hTh = at("hTh", [P, KT, T], F32R, 152)
    hTl = at("hTl", [P, KT, T], F32R, 168)
    wple = at("wple", [P, 2, D], F32, 184)
    pT = at("pT", [P, 2, T], F32, 200)
    pin = at("pin", [P, TT, PLE], F32, 202)
    gate = at("gate", [P, TT, W], F32, 144)

    za = at("za", [P, TT, A_IN], F32, 120)
    zb = at("zb", [P, TT, B_IN], F32, 144)
    zprev = at("zprev", [P, 2, TT, W], F32, 171.5)
    mu = at("mu", [P, 2, W], F32, 179.5)
    qkT = at("qkT", [P, 2, T], F32, 183.5)
    sm = at("sm", [P, 2, 3 * P], F32, 185.5)
    pe_ = at("pe_", [P, 2, 3 * P], F32, 188.5)
    at_ = at("at_", [P, 3 * P], F32, 191.5)
    atT = at("atT", [P, 3, P], F32, 193)
    cau3 = at("cau3", [P, 3 * P], F32, 194.5)
    rt = at("rt", [P, 4, 64], F32, 196)
    lqk = at("lqk", [P, 4, A_DC], F32, 197)
    mx = at("mx", [P, 4, 4], F32, 198)
    subg = at("subg", [P, A_DV], F32, 118.5)
    r16 = at("r16", [P, 16], F32, 118.4375)
    asq = at("asq", [P, TT, AW], F32, 64)
    posi = at("posi", [P, TT], I32, 144)
    posf = at("posf", [P, TT], F32, 144.125)
    freq = at("freq", [P, 24], F32, 144.25)
    angle = at("angle", [P, 96], F32, 144.5)
    lw = at("lw", [P, TT, BW], F32, 183.5)
    av = at("av", [P, TT, BW], F32, 191.5)
    gv = [at(f"gv{tt}", [P, BW], F32, (179.5, 199.5)[tt]) for tt in range(TT)]
    kkv = at("kkv", [P, TT, BW], F32, 171.5)
    kk0 = za[:, :, AW:3 * AW].rearrange("p t (f c) -> p t f c", f=2)[:, :, :, 0:W]
    p_kk = at("p_kk", [P, BW], F32, 199.5)
    kk_sq = at("kk_sq", [P, BW], F32, 199.5)
    w2 = at("w2", [P, BW], F32, 48)
    a2 = at("a2", [P, BW], F32, 52)
    g2 = at("g2", [P, 2, BW], F32, 56)
    p_ka = at("p_ka", [P, BW], F32, 72)
    p_rk = at("p_rk", [P, BW], F32, 76)
    lnx_g = at("lnx_g", [P, BW], F32, 48)
    lnx_b = at("lnx_b", [P, BW], F32, 52)
    rkr = at("rkr", [P, TT, BW], F32, 56)
    loraT = at("loraT", [P, 4, T], F32, 203.5)
    ex1 = at("ex1", [P, TT, BW], F32, 80)
    ex2 = at("ex2", [P, TT, BW], F32, 88)
    bon = at("bon", [P, TT, B_HEADS], F32, 118)
    nrm = at("nrm", [P, TT, B_HEADS], F32, 118.125)
    WL = at("WL", [P, 8, 4], F32, 118.25)
    XT = [[at(f"{n}T{tt}", [P, 8, P], F32, (80 + 4 * i, (124, 128, 136, 140)[i])[tt])
           for i, n in enumerate(("A", "B", "K", "R"))] for tt in range(TT)]
    tmp_set = [[at(f"{n}{s}", [P, 4, P], F32, 96 + 2 * i + 8 * s) for i, n in
                enumerate(("MT", "Ti", "Y1"))] for s in range(2)]
    NT = at("NT", [P, 16, P], F32, 16)
    PT = at("PT", [P, 16, P], F32, 24)
    QT = at("QT", [P, 16, P], F32, 32)
    TTi = at("TTi", [P, 16, P], F32, 40)
    Xs = at("Xs", [P, BW], F32, 183.5)
    Us = at("Us", [P, BW], F32, 187.5)
    ST = at("ST", [P, 8, P], F32, 203.5)

    GAIN = {"ab_in": 0, "c_in": 1, "mlp0": 2, "mlp1": 3}

    def w_chunks(w, Q):
        v = w.rearrange("(Q q k p) n -> Q q p k n", q=4, k=4, p=P)
        return [v[Q, q] for q in range(4)]

    order = []
    for st_ in plan:
        order += {"ab": ["ab_in", "ab_out"], "c": ["c_in", "c_out"]}.get(st_, [st_])
    width = lambda st: C_W if st == "c_in" else W
    nxt = {a: (order[i + 1] if i + 1 < len(order) else None) for i, a in enumerate(order)}
    prv = {a: (order[i - 1] if i else None) for i, a in enumerate(order)}
    read_out = {"ab_in": ("ev_ab_in", 1, 12), "ab_out": ("m_out", 1, 3), "c_in": ("ev_c_in", 1, 8),
                "c_out": ("m_out", 1, 3), "mlp0": ("ev_dn", 1, 15), "mlp1": ("ev_dn", 1, 15),
                "ple0": ("ev_ple", 1, 3), "ple1": ("ev_ple", 1, 3)}

    updates = lambda st: st != order[0] and not st.endswith("_out")
    counts = {"m_sq": lambda st: 0 if st.endswith("_in") else 8,
              "m_out": lambda st: 4 if st.endswith("_out") else 0,
              "h_ready": lambda st: 4 if updates(st) else 0, "h_late": lambda st: 4 if updates(st) else 0,
              "m_gained": lambda st: 8 if updates(st) else 0, "m_late": lambda st: 4 if updates(st) else 0, "rstd_m": lambda st: 1 if updates(st) else 0,
              "gpost": lambda st: 0 if st.endswith("_in") else 16,
              "ev_ab_in": lambda st: 0, "ev_c_in": lambda st: 0,
              "h_sq": lambda st: 8 if st in GAIN else 0, "rstd": lambda st: 1 if st in GAIN else 0}
    for kind in ("xT", "xT_hi", "xT_lo"):
        counts[kind] = lambda st: 8
    for kind in ("sq_done", "hT", "hT_hi", "hT_lo", "ev_up", "ev_dn"):
        counts[kind] = lambda st: 16 if st.startswith("mlp") else 0
    for kind, n_ in (("gated", 4), ("emb", 4), ("ev_ple", 4), ("ple_in", 32), ("pT_mm", 1), ("pT", 1)):
        counts[kind] = lambda st, n_=n_: n_ if st.startswith("ple") else 0

    def mark(kind, st, v):
        before = order[:order.index(st)] if st in order else order
        return sem(kind), sum(counts[kind](a) for a in before) + v

    landed = [sem(f"landed{q}") for q in range(4)]
    hi_ready, lo_ready = sem("hi_ready"), sem("lo_ready")
    mm_used = sem("mm_used")

    def load_slab(sp, s, w, col, n, first=False):
        for q in range(4):
            if not first:
                sp.wait_ge(lo_ready, 4 * s - 3 + q)
            sp.dma_start(raw[:, q, :, 0:n], w[q][:, :, bass.ds(col, n)]).then_inc(landed[q], 16)

    def split_hi(act, s, q, n=W, fresh=False):
        act.wait_ge(landed[q], 16 * (s + 1))
        if not fresh:
            act.wait_ge(mm_used, 4 * s + q - 1)
        act.activation(whi[:, q % 2, :, 0:n], raw[:, q, :, 0:n], ACT.Copy).then_inc(hi_ready, 1)

    def split_lo(dve, s, q, n=W):
        dve.wait_ge(hi_ready, 4 * s + q + 1)
        dve.tensor_tensor(wlo[:, q % 2, :, 0:n], raw[:, q, :, 0:n], whi[:, q % 2, :, 0:n].bitcast(F32),
                          ALU.subtract).then_inc(lo_ready, 1)

    def mm_slab(pe, s, par_, n=W, free=None, before=None, lhs=(uTh, uTl)):
        if free:
            pe.wait_ge(*free)
        for q in range(4):
            if before:
                before(q)
            pe.wait_ge(lo_ready, 4 * s + q + 1)
            for k in range(4):
                for tt in range(TT):
                    o = bank[2 * par_ + tt][:, 0:n]
                    xh = lhs[0][:, 4 * q + k, tt * P:(tt + 1) * P]
                    xl = lhs[1][:, 4 * q + k, tt * P:(tt + 1) * P]
                    hi, lo = whi[:, q % 2, k, 0:n], wlo[:, q % 2, k, 0:n]
                    pe.matmul(o, xh, hi, start=(q == 0 and k == 0), stop=False)
                    pe.matmul(o, xh, lo, start=False, stop=False)
                    last = pe.matmul(o, xl, hi, start=False, stop=(q == 3 and k == 3))
            last.then_inc(mm_used, 1)

    def T_pe(pe, st, src, ready, b):
        for pr in range(2):
            g = 2 * b + pr
            if g >= 4:
                pe.wait_ge(*mark("xT_lo", st, g - 3))
            if g == 3 and st == order[0]:
                pe.wait_ge(sem("gpre_ready"), 1)
            if g == 3 and st.startswith("ple"):
                pe.wait_ge(*mark("pT", st, 1))
            for kk in range(2):
                for tt in range(TT):
                    if pr == 0 and kk == 0:
                        pe.wait_ge(*ready(tt, b))
                    c = (2 * pr + kk) * P
                    last = pe.transpose(bank[4 + g % 4][:, (2 * kk + tt) * P:(2 * kk + tt + 1) * P],
                                        src(tt, b)[:, c:c + P], ident[:])
            last.then_inc(sem("xT"), 1)

    def T_act(act, st, b, gain=None):
        for pr in range(2):
            g = 2 * b + pr
            act.wait_ge(*mark("xT", st, g + 1))
            for kk in range(2):
                k = 2 * g + kk
                sc = 1.0 if gain is None else gpre[:, gain, k:k + 1]
                last = act.activation(uTh[:, k, :], bank[4 + g % 4][:, kk * T:(kk + 1) * T], ACT.Copy, scale=sc)
            last.then_inc(sem("xT_hi"), 1)

    def T_dve(dve, st, b, gain=None):
        for pr in range(2):
            g = 2 * b + pr
            dve.wait_ge(*mark("xT_hi", st, g + 1))
            for kk in range(2):
                k = 2 * g + kk
                x = bank[4 + g % 4][:, kk * T:(kk + 1) * T]
                if gain is None:
                    last = dve.tensor_tensor(uTl[:, k, :], x, uTh[:, k, :].bitcast(F32), ALU.subtract)
                else:
                    last = dve.scalar_tensor_tensor(out=uTl[:, k, :], in0=x, scalar=gpre[:, gain, k:k + 1],
                                                    in1=uTh[:, k, :].bitcast(F32), op0=ALU.mult,
                                                    op1=ALU.subtract)
            last.then_inc(sem("xT_lo"), 1)

    def pe_first(pe, st, s, par_, src, ready, n=W, free=None):
        T_pe(pe, st, src, ready, 0)

        def before(q):
            for b in {0: (1,), 1: (), 2: (2, 3), 3: ()}[q] if st == "ab_out" else (q + 1,) if q < 3 else ():
                T_pe(pe, st, src, ready, b)
            pe.wait_ge(*mark("xT_lo", st, 2 * q + 2))
        mm_slab(pe, s, par_, n, free, before)

    def act_first(act, st, s, n, gain, squares=None):
        for b in range(4):
            if squares and st != order[0]:
                squares(b)
            T_act(act, st, b, gain)
            if b == 0 and st == order[0]:
                split_hi(act, s, 1, n, True)
            if squares and st == order[0]:
                squares(b)
            if b >= 2 and st != "ab_out":
                split_hi(act, s, b, n)
            if b == 1 and st == "ab_out":
                split_hi(act, s, 2, n)
                split_hi(act, s, 3, n)

    last_junk = [None]

    def square(act, x, total, signal, i, prev=None):
        prev = prev or last_junk[0]
        if prev:
            act.wait_ge(*prev)
        last_junk[0] = (signal, i)
        return act.activation(junk[:], x, ACT.Square, accum_out=total).then_inc(signal, 1)

    def h_src(tt, b):
        return h[:, tt, b * W:(b + 1) * W]

    def h_squares(act, st):
        def squares(b):
            for tt in range(TT):
                act.wait_ge(*h_ready(st)(tt, b))
                square(act, h_src(tt, b), hss[:, tt, b:b + 1], *mark("h_sq", st, 2 * b + tt + 1))
        return squares

    def late(st):
        return 3 if st == "end" else 2

    def h_ready(st):
        return lambda tt, b: ((sem(f"x_in{b}"), 16) if st == order[0] else
                              mark("h_ready", st, 2 * b + tt + 1) if b < late(st) else
                              mark("h_late", st, 2 * (b - late(st)) + tt + 1))

    def rsqrt(dve, link, x):
        n = x.free_size()
        y, t = nwt[:, 0, 0:n], nwt[:, 1, 0:n]
        link(dve.tensor_scalar(y.bitcast(I32), x.bitcast(I32), 1, None, ALU.logical_shift_right))
        link(dve.tensor_scalar(y.bitcast(I32), y.bitcast(I32), -1.0, float(0x5F3759DF), ALU.mult, ALU.add))
        for i in range(3):
            link(dve.tensor_tensor(t, y, y, ALU.mult))
            link(dve.scalar_tensor_tensor(out=t, in0=t, scalar=-0.5, in1=x, op0=ALU.mult, op1=ALU.mult))
            last = dve.scalar_tensor_tensor(out=y if i < 2 else x, in0=t, scalar=1.5, in1=y, op0=ALU.add,
                                            op1=ALU.mult)
            if i < 2:
                link(last)
        return last

    def rstd_from(dve, link, src, out_, n, eps):
        link(dve.tensor_reduce(out_, src, AX.X, ALU.add))
        link(dve.tensor_scalar(out_, out_, 1.0 / n, eps, ALU.mult, ALU.add))
        return rsqrt(dve, link, out_)

    def h_update(dve, link, st, prev, b):
        if b == 0:
            dve.wait_ge(*mark("m_sq", prev, 8))
            rstd_from(dve, link, ssq[:], rstd_m[:], D, NORM_EPS).then_inc(sem("rstd_m"), 1)
            dve.wait_ge(*mark("rstd_m", st, 1))
        dve.wait_ge(*mark("m_gained", st, 2 * b + 2))
        for tt in range(TT):
            dve.scalar_tensor_tensor(out=h_src(tt, b), in0=m[:, tt, b * W:(b + 1) * W], scalar=rstd_m[:, tt:tt + 1],
                                     in1=h_src(tt, b), op0=ALU.mult, op1=ALU.add).then_inc(sem("h_ready"), 1)

    def h_update_pool(pool, st, prev):
        pool.wait_ge(*mark("gpost", prev, 16))
        for b in range(4):
            pool.wait_ge(*mark("m_sq", prev, 2 * b + 2))
            if prev.endswith("_out"):
                pool.wait_ge(*mark("m_out", prev, b + 1))
            for tt in range(TT):
                mb = m[:, tt, b * W:(b + 1) * W]
                pool.tensor_tensor(mb, mb, gpost[:, b * W:(b + 1) * W], ALU.mult).then_inc(sem("m_gained"), 1)
        pool.wait_ge(*mark("rstd_m", st, 1))
        for b in range(late(st), 4):
            for tt in range(TT):
                mb, i = m[:, tt, b * W:(b + 1) * W], 2 * (b - late(st)) + tt + 1
                pool.wait_ge(*mark("m_gained", st, 2 * b + tt + 1))
                pool.tensor_tensor(mb, mb, rstd_m[:, tt:tt + 1].broadcast_to([P, W]),
                                   ALU.mult).then_inc(sem("m_late"), 1)
                pool.wait_ge(*mark("m_late", st, i))
                pool.tensor_tensor(h_src(tt, b), h_src(tt, b), mb, ALU.add).then_inc(sem("h_late"), 1)

    def h_first(dve, link, st, s, n, gain, prev):
        if prev:
            h_update(dve, link, st, prev, 0)
            h_update(dve, link, st, prev, 1)
        T_dve(dve, st, 0, gain)
        split_lo(dve, s, 1, n)
        T_dve(dve, st, 1, gain)
        for b in (2, 3):
            T_dve(dve, st, b, gain)
            split_lo(dve, s, b, n)
        if gain is not None:
            dve.wait_ge(*mark("h_sq", st, 8))
            rstd_from(dve, link, hss[:], rstd_h[:], D, NORM_EPS).then_inc(sem("rstd"), 1)

    def prologue(fn, eng, st):
        if st == order[0]:
            fn(eng, base[st], 0, width(st), *((True,) if fn is split_hi else ()))
        elif prv[st].endswith("_in"):
            for q in range(2):
                fn(eng, base[st], q, width(st))

    def free_of(st, i):
        if i >= 2:
            return mark(read_out[st][0], st, read_out[st][1] * (i - 1))
        if prv[st] is None:
            return None
        name, by, v = read_out[prv[st]]
        return mark(name, prv[st], by * (v + i))

    N_CONSTS = 7
    HALF_A, HALF_C = A_DC // 8, C_HD // 8
    chain = sem("pool_chain")

    def pool_setup(pool):
        n = [0]

        def link(ins):
            ins.then_inc(chain, 1)
            n[0] += 1
            pool.wait_ge(chain, n[0])

        def keep(ap, pattern, cm, base_, op=ALU.is_ge, fill=0.0):
            return pool.affine_select(out=ap, in_=ap, compare_op=op, fill=fill, base=base_, pattern=pattern,
                                      channel_multiplier=cm)
        link(pool.memset(ident[:], 0.0))
        keep(ident[:], [[-1, P]], 1, 0, ALU.not_equal, 1.0).then_inc(sem("consts"), 1)
        link(pool.memset(m_su[:], 1.0))
        v = m_su[:].rearrange("p (j c) -> p j c", c=CH)
        link(keep(v, [[-CH, 2], [0, CH]], 1, 0))
        keep(v, [[CH, 2], [1, CH]], -1, -1).then_inc(sem("consts"), 1)
        link(pool.memset(m_ui[:], 1.0))
        v = m_ui[:].rearrange("p (j c) -> p j c", c=CH)
        link(keep(v, [[-CH, 2], [0, CH]], 1, 0))
        keep(v, [[CH, 2], [1, CH]], -1, 0).then_inc(sem("consts"), 1)
        link(pool.memset(m_l1[:], 0.0))
        v = m_l1[:].rearrange("p (j c) -> p j c", c=2)[:, :, 1:2]
        keep(v, [[-2, P // 2], [0, 1]], 1, 0, ALU.not_equal, 1.0).then_inc(sem("consts"), 1)
        link(pool.memset(m_lvt[:], 0.0))
        for i in range(6):
            b = 1 << i
            v = m_lvt[:, i, :].rearrange("p (j c) -> p j c", c=2 * b)[:, :, 0:b]
            link(pool.memset(v, 1.0))
            link(keep(v, [[-2 * b, P // (2 * b)], [0, b]], 1, -b))
            link(keep(v, [[2 * b, P // (2 * b)], [0, b]], -1, 2 * b - 1))
        pool.memset(st2[:, 6:7], 0.0).then_inc(sem("consts"), 1)
        link(pool.memset(causal[:], 0.0))
        keep(causal[:, P:T], [[-1, P]], 1, 0, ALU.is_ge, NEG).then_inc(sem("consts"), 1)
        pool.memset(st2[:, 7:8], 0.0).then_inc(sem("consts"), 1)
        for half, f0 in ((HALF_A, 0), (HALF_C, HALF_A)):
            for j in range(half):
                v = np.float32(THETA) ** (-(np.float32(j) * np.float32(2.0) / np.float32(2 * half)))
                pool.memset(freq[:, f0 + j:f0 + j + 1], float(np.float32(v))).then_inc(sem("freqs"), 1)
        with nc.allow_non_contiguous_dma(reason="256 positions"):
            pool.dma_start(posi[:], A["positions"][0].rearrange("(t p) -> p t", p=P)).then_inc(sem("pos_in"), 16)

    def act_setup(act):
        act.wait_ge(sem("gpre_T"), 1)
        act.activation(gpre[:], bank[7][:, 0:4 * KT], ACT.Copy).then_inc(sem("gpre_ready"), 1)
        act.wait_ge(sem("gpre_ready"), 1)

    def dve_setup(dve, link):
        dve.wait_ge(sem("gpre_ready"), 1)

    def step(fn, eng, s, st, nn, done, n=None, mid=None, skip=False, last=False):
        n = n or width(st)
        if not skip:
            fn(eng, s, 2, n)
            fn(eng, s, 3, n)
        if mid:
            mid()
        if nn:
            fn(eng, s + 1, 0, nn)
            if not last:
                fn(eng, s + 1, 1, nn)
        if done:
            done()
        if nn and last and fn is split_hi:
            fn(eng, s + 1, 1, nn)

    def next_width(st):
        return width(nxt[st]) if nxt[st] and not st.endswith("_in") else None

    def T_mlp_pe(pe, l, Q, j):
        pe.wait_ge(*mark("sq_done", f"mlp{l}", 4 * Q + j + 1))
        if j >= 2:
            pe.wait_ge(*mark("hT_lo", f"mlp{l}", 4 * Q + j - 1))
        for pr in range(2):
            for kk in range(2):
                for tt in range(TT):
                    last = pe.transpose(bank[4 + 2 * (j % 2) + pr][:, (2 * kk + tt) * P:(2 * kk + tt + 1) * P],
                                        hid[:, j % 2, tt, (2 * pr + kk) * P:(2 * pr + kk + 1) * P], ident[:])
        last.then_inc(sem("hT"), 1)

    def T_mlp_split(eng, l, Q, j, high):
        eng.wait_ge(*mark("hT" if high else "hT_hi", f"mlp{l}", 4 * Q + j + 1))
        for pr in range(2):
            k = 4 * j + 2 * pr
            x = bank[4 + 2 * (j % 2) + pr][:]
            if high:
                last = eng.activation(hTh[:, k:k + 2, :], x, ACT.Copy)
            else:
                last = eng.tensor_tensor(hTl[:, k:k + 2, :], x, hTh[:, k:k + 2, :].bitcast(F32), ALU.subtract)
        last.then_inc(sem("hT_hi" if high else "hT_lo"), 1)

    def mlp_pe(pe, l, Q):
        st = f"mlp{l}"
        s = base[st] + 8 * Q
        par_ = lambda r: (base[st] + r) % 2
        up = lambda v: mark("ev_up", st, v)
        dn = lambda v: mark("ev_dn", st, v)
        first = isinstance(Q, int)
        if first:
            pe_first(pe, st, s, par_(0), h_src, h_ready(st), W, free_of(st, 0))
            mm_slab(pe, s + 1, par_(1), W, free_of(st, 1))
        else:
            mm_slab(pe, s, par_(0), W, dn(4 * Q - 1))
            mm_slab(pe, s + 1, par_(1), W, dn(4 * Q))
        for j in (2, 3):
            T_mlp_pe(pe, l, Q, j - 2)
            mm_slab(pe, s + j, par_(j), W, up(4 * Q + j - 1))
        T_mlp_pe(pe, l, Q, 2)

        def before(q):
            if q == 3:
                T_mlp_pe(pe, l, Q, 3)
            pe.wait_ge(*mark("hT_lo", f"mlp{l}", 4 * Q + q + 1))
        mm_slab(pe, s + 4, par_(4), W, up(4 * Q + 3), before, (hTh, hTl))
        mm_slab(pe, s + 5, par_(5), W, up(4 * Q + 4), None, (hTh, hTl))
        mm_slab(pe, s + 6, par_(6), W, dn(4 * Q + 1), None, (hTh, hTl))
        mm_slab(pe, s + 7, par_(7), W, dn(4 * Q + 2), None, (hTh, hTl))

    def mlp_act(act, l, Q):
        st = f"mlp{l}"
        first = isinstance(Q, int) and Q == 0
        final = isinstance(Q, int) and Q == 3
        for r in range(8):
            s, j, par_ = base[st] + 8 * Q + r, r % 4, (base[st] + r) % 2

            def relu():
                act.wait_ge(mm_used, 4 * s + 4)
                if first and r == 0:
                    act.wait_ge(*mark("rstd", st, 1))
                for tt in range(TT):
                    last = act.activation(hid[:, j % 2, tt, :], bank[2 * par_ + tt][:], ACT.Relu,
                                          scale=rstd_h[:, tt:tt + 1])
                last.then_inc(sem("ev_up"), 1)
                if j:
                    T_mlp_split(act, l, Q, j - 1, True)

            def squares():
                act.wait_ge(*mark("ev_dn", f"mlp{l}", 4 * Q + j + 1))
                for tt in range(TT):
                    square(act, m[:, tt, j * W:(j + 1) * W], ssq[:, tt, j:j + 1], *mark("m_sq", st, 2 * j + tt + 1))
            step(split_hi, act, s, st, W,
                 relu if r < 4 else squares if final else None, skip=first and r == 0,
                 last=final and r == 7,
                 mid=(lambda: T_mlp_split(act, l, Q, 3, True)) if r == 4 else None)

    def mlp_dve(dve, l, Q):
        st = f"mlp{l}"
        first = isinstance(Q, int) and Q == 0
        final = isinstance(Q, int) and Q == 3
        for r in range(8):
            s, j, par_ = base[st] + 8 * Q + r, r % 4, (base[st] + r) % 2

            def square():
                dve.wait_ge(*mark("ev_up", f"mlp{l}", 4 * Q + j + 1))
                x = hid[:, j % 2, :, :]
                dve.tensor_tensor(x, x, x, ALU.mult).then_inc(sem("sq_done"), 1)
                if j:
                    T_mlp_split(dve, l, Q, j - 1, False)

            def add():
                dve.wait_ge(mm_used, 4 * s + 4)
                for tt in range(TT):
                    x, y = bank[2 * par_ + tt][:], m[:, tt, j * W:(j + 1) * W]
                    last = dve.tensor_copy(y, x) if first else dve.tensor_tensor(y, y, x, ALU.add)
                last.then_inc(sem("ev_dn"), 1)
            step(split_lo, dve, s, st, W, add if r >= 4 else square, skip=first and r == 0, last=final and r == 7,
                 mid=(lambda: T_mlp_split(dve, l, Q, 3, False)) if r == 4 else None)

    def ple_pe(pe, l):
        st = f"ple{l}"
        pe.wait_ge(*mark("ple_in", f"ple{l}", 32))
        if not prv[st]:
            pe.wait_ge(sem("gpre_ready"), 1)
        for k in range(2):
            for tt in range(TT):
                last = pe.transpose(bank[7][:, (2 * k + tt) * P:(2 * k + tt + 1) * P],
                                    pin[:, tt, k * P:(k + 1) * P], ident[:])
        last.then_inc(sem("pT_mm"), 1)
        for j in range(4):
            s = base[st] + j
            if j == 0:
                pe_first(pe, st, s, s % 2, h_src, h_ready(st), W, free_of(st, 0))
            else:
                mm_slab(pe, s, s % 2, W, free_of(st, j))
                pe.wait_ge(*mark("gated", f"ple{l}", j))
            for tt in range(TT):
                for k in range(2):
                    last = pe.matmul(bank[6 + tt][:], pT[:, k, tt * P:(tt + 1) * P],
                                     wple[:, k, j * W:(j + 1) * W], start=(k == 0), stop=(k == 1))
            last.then_inc(sem("emb"), 1)

    def ple_act(act, l):
        st = f"ple{l}"
        act.wait_ge(*mark("pT_mm", st, 1))
        act.activation(pT[:], bank[7][:], ACT.Copy).then_inc(sem("pT"), 1)
        act_first(act, st, base[st], W, None)
        for j in range(4):
            s = base[st] + j

            def sigmoid():
                act.wait_ge(mm_used, 4 * s + 4)
                for tt in range(TT):
                    last = act.activation(gate[:, tt, :], bank[2 * (s % 2) + tt][:], ACT.Sigmoid)
                last.then_inc(sem("ev_ple"), 1)
                act.wait_ge(*mark("gated", f"ple{l}", j + 1))
                for tt in range(TT):
                    square(act, m[:, tt, j * W:(j + 1) * W], ssq[:, tt, j:j + 1], *mark("m_sq", st, 2 * j + tt + 1))
            step(split_hi, act, s, st, W if j < 3 else next_width(st), sigmoid, skip=(j == 0), last=(j == 3))

    def ple_dve(dve, link, l):
        st = f"ple{l}"
        h_first(dve, link, st, base[st], W, None, prv[st])
        for j in range(4):
            s = base[st] + j

            def gated():
                dve.wait_ge(*mark("ev_ple", f"ple{l}", j + 1))
                dve.wait_ge(*mark("emb", f"ple{l}", j + 1))
                for tt in range(TT):
                    last = dve.tensor_tensor(m[:, tt, j * W:(j + 1) * W], gate[:, tt, :], bank[6 + tt][:],
                                             ALU.mult)
                last.then_inc(sem("gated"), 1)
            step(split_lo, dve, s, st, W if j < 3 else next_width(st), gated, skip=(j == 0), last=(j == 3))

    def out_act(act, st):
        if st == "ab_out":
            act.wait_ge(sem("y_mm"), 4)
        act_first(act, st, base[st], W, None)
        for j in range(4):
            s = base[st] + j

            def keep():
                act.wait_ge(mm_used, 4 * s + 4)
                if j == 0:
                    act.wait_ge(*mark("xT", st, 8))
                for tt in range(TT):
                    square(act, bank[2 * (s % 2) + tt][:], ssq[:, tt, j:j + 1], *mark("m_sq", st, 2 * j + tt + 1))
                for tt in range(TT):
                    last = act.activation(m[:, tt, j * W:(j + 1) * W], bank[2 * (s % 2) + tt][:], ACT.Copy)
                last.then_inc(sem("m_out"), 1)
            step(split_hi, act, s, st, W if j < 3 else next_width(st), keep, skip=(j == 0), last=(j == 3))

    def out_dve(dve, link, st):
        for b in range(4):
            if st == "ab_out" and b in (0, 2):
                for k in ((0,) if b == 0 else range(1, 5)):
                    out_norm_dve(dve, link, 1, k)
            T_dve(dve, st, b)
            if b >= 2 and st != "ab_out":
                split_lo(dve, base[st], b)
        if st == "ab_out":
            dve.wait_ge(lo_ready, 4 * base[st] + 4)
        for j in range(4):
            step(split_lo, dve, base[st] + j, st, W if j < 3 else next_width(st), None, skip=(j == 0), last=(j == 3))

    def out_pe(pe, st, src, ready):
        if st == "ab_out":
            pe.wait_ge(sem("y_out"), 4)
        for j in range(4):
            s = base[st] + j
            if j == 0:
                pe_first(pe, st, s, s % 2, src, ready, W, free_of(st, 0))
            else:
                mm_slab(pe, s, s % 2, W, free_of(st, j))

    QB = (4, 5, 6, 7)

    def tr_pe(pe, name, groups, banks, first_waits=()):
        for w in first_waits:
            pe.wait_ge(*w)
        for g, items in enumerate(groups):
            if g >= len(banks):
                o = g - len(banks)
                pe.wait_ge(sem(f"{name}_out{o % 2}"), o // 2 + 1)
            for i, x in enumerate(items):
                rows = x.shape[1]
                last = pe.transpose(bank[banks[g % len(banks)]][0:rows, i * P:(i + 1) * P], x, ident[:])
            last.then_inc(sem(f"{name}_tr"), 1)

    def tr_out(eng, name, outs, banks, me):
        for g, (o, rows, c0, c1) in enumerate(outs):
            if g % 2 == me:
                eng.wait_ge(sem(f"{name}_tr"), g + 1)
                x = bank[banks[g % len(banks)]][0:rows, c0:c1]
                ins = eng.activation(o, x, ACT.Copy) if me == 0 else eng.tensor_copy(o, x)
                ins.then_inc(sem(f"{name}_out{me}"), 1)

    def tr_all(eng, name, n):
        for me in range(2):
            if (n + 1 - me) // 2:
                eng.wait_ge(sem(f"{name}_out{me}"), (n + 1 - me) // 2)

    def trig_act(act):
        act.wait_ge(sem("angles"), 2)
        act.activation(sinT[:], sinT[:], ACT.Sin).then_inc(sem("trig"), 1)
        act.activation(cosT[:], cosT[:], ACT.Sin).then_inc(sem("trig"), 1)

    def trig_dve(dve, link):
        ang, kq = angle[:, 0:48].rearrange("p (t f) -> p t f", t=TT), angle[:, 48:96].rearrange("p (t f) -> p t f", t=TT)
        dve.wait_ge(sem("pos_in"), 16)
        dve.wait_ge(sem("freqs"), 24)
        link(dve.tensor_copy(posf[:], posi[:]))
        for tt in range(TT):
            link(dve.tensor_scalar(ang[:, tt, :], freq[:], posf[:, tt:tt + 1], None, ALU.mult))
        magic = 1.5 * 2.0 ** 23
        link(dve.tensor_scalar(kq, ang, 1.0 / (2 * math.pi), magic, ALU.mult, ALU.add))
        link(dve.tensor_scalar(kq, kq, -magic, None, ALU.add))
        c1 = 6.28125
        c2 = float(np.float32(round((2 * math.pi - c1) * 2 ** 21) / 2 ** 21))
        c3 = 2 * math.pi - c1 - c2
        for c in (c1, c2, c3):
            link(dve.scalar_tensor_tensor(out=ang, in0=kq, scalar=-c, in1=ang, op0=ALU.mult, op1=ALU.add))
        lim = 3.1415925
        link(dve.tensor_scalar(ang, ang, lim, -lim, ALU.min, ALU.max))
        dve.tensor_copy(sinT[:], ang).then_inc(sem("angles"), 1)
        link(dve.scalar_tensor_tensor(out=kq, in0=ang, scalar=-1.0, in1=ang, op0=ALU.mult, op1=ALU.max))
        dve.tensor_scalar(cosT[:], kq, -1.0, math.pi / 2, ALU.mult, ALU.add).then_inc(sem("angles"), 1)

    def rope(dve, link, x, tt, f0, half, tmp):
        n = x.shape[1]
        c = cosT[:, tt, f0:f0 + half].unsqueeze(1).broadcast_to([P, n, half])
        s = sinT[:, tt, f0:f0 + half].unsqueeze(1).broadcast_to([P, n, half])
        x1, x2 = x[:, :, 0:half], x[:, :, half:2 * half]
        t = [tmp[:, i, 0:n * half].rearrange("p (a b) -> p a b", b=half) for i in range(4)]
        link(dve.tensor_tensor(t[0], x1, c, ALU.mult))
        link(dve.tensor_tensor(t[1], x2, s, ALU.mult))
        link(dve.tensor_tensor(t[2], x2, c, ALU.mult))
        link(dve.tensor_tensor(t[3], x1, s, ALU.mult))
        link(dve.tensor_tensor(x1, t[0], t[1], ALU.subtract))
        return dve.tensor_tensor(x2, t[2], t[3], ALU.add)

    NL = B_IN - 6 * W
    ab_slabs = [(za, (w * AW + g * W), W) for g in range(2) for w in range(3)] + \
               [(zb, 6 * W, NL)] + [(zb, i * W, W) for i in (2, 3, 0, 1, 4, 5)]
    ab_cols = [c if dst is za else A_IN + c for dst, c, _ in ab_slabs]
    N_AB = len(ab_slabs)
    R0 = 6
    H0 = 4

    def ab_in_pe(pe):
        st, b = "ab_in", base["ab_in"]
        ev = sem("ev_ab_in")
        for i, (_, _, n) in enumerate(ab_slabs):
            if i == 0:
                pe_first(pe, st, b, b % 2, h_src, h_ready(st), W, free_of(st, 0))
                continue

            def before(q):
                hd = i - H0
                if q == 0 and 1 <= hd <= A_HEADS:
                    head_weights_pe(pe, hd - 1)
                if q == 0 and 0 <= hd < A_HEADS:
                    head_transposes_pe(pe, hd)
                if q == 1 and 1 <= hd <= A_HEADS:
                    head_values_pe(pe, hd - 1)
                if q == 2 and 0 <= hd < A_HEADS:
                    head_scores_pe(pe, hd)
                if q == 3 and i - 10 in range(TT):
                    lora_transposes_pe(pe, i - 10)
                if q == 2 and i == N_AB - 1:
                    lora_pe(pe, 0)
            mm_slab(pe, b + i, (b + i) % 2, n, (ev, i - 1) if i > 1 else free_of(st, 1), before)

    def ab_in_act(act):
        st, b = "ab_in", base["ab_in"]
        prologue(split_hi, act, st)
        act_first(act, st, b, W, GAIN[st], h_squares(act, st))
        for i, (dst, col, n) in enumerate(ab_slabs):
            s, hd = b + i, i - H0
            if i:
                split_hi(act, s, 2, n)
                if 1 <= hd <= A_HEADS:
                    head_out_act(act, hd - 1)
                split_hi(act, s, 3, n)
                if i == N_AB - 1:
                    sigmoid_act(act, 0)
                if 0 <= hd < A_HEADS:
                    head_exp_act(act, hd)
            if i + 1 < N_AB:
                nn = ab_slabs[i + 1][2]
                split_hi(act, s + 1, 0, nn)
                if i - 10 in range(TT):
                    lora_out_act(act, i - 10)
                split_hi(act, s + 1, 1, nn)
            if i == 0:
                act.wait_ge(*mark("rstd", st, 1))
            act.wait_ge(mm_used, 4 * s + 4)
            for tt in range(TT):
                last = act.activation(dst[:, tt, col:col + n], bank[2 * (s % 2) + tt][:, 0:n], ACT.Copy,
                                      scale=rstd_h[:, tt:tt + 1])
            last.then_inc(sem("ev_ab_in"), 1)
            if i == 1:
                trig_act(act)
                act.wait_ge(sem("lam_sums"), 1)
                act.activation(lam[:, 0:2], lam[:, 0:2], ACT.Exp).then_inc(sem("lam_exp"), 1)
            if 0 <= hd < A_HEADS:
                head_weights_act(act, hd)
            if 0 <= hd + 1 < A_HEADS:
                head_transposes_act(act, hd + 1)
            if i == 8:
                act.wait_ge(sem("mixed"), 1)
                x = zb[:, :, 3 * BW:3 * BW + LW]
                act.activation(x, x, ACT.Tanh).then_inc(sem("lora_act"), 1)
                x = zb[:, :, 3 * BW + LW + LA:B_IN]
                act.activation(x, x, ACT.Sigmoid).then_inc(sem("lora_act"), 1)

    def ab_in_pool(pool):
        for i, n in enumerate(("diff_lq1", "diff_lk1", "diff_lq2", "diff_lk2")):
            pool.dma_start(lqk[:, i, :], A[n][0].partition_broadcast(P)).then_inc(sem("attn_in"), 16)
        pool.wait_ge(*mark("h_sq", "ab_in", 8))
        pool.dma_start(subg[:], A["diff_subln_g"][0].partition_broadcast(P)).then_inc(sem("subg_in"), 16)
        pool.wait_ge(sem("consts"), N_CONSTS)
        pool.tensor_copy(cau3[:, 0:P], causal[:, P:T]).then_inc(sem("mask_in"), 1)
        pool.tensor_copy(cau3[:, P:3 * P], causal[:]).then_inc(sem("mask_in"), 1)
        for i, (_, col, n) in enumerate(ab_slabs[R0:]):
            if i == 4:
                kk_pool(pool)
            if i == 5:
                lora_weights_pool(pool)
            if i == 6:
                kk_norm_pool(pool)
                lora_params_pool(pool)
            pool.wait_ge(sem("ev_ab_in"), R0 + i + 1)
            if i >= 2:
                pool.wait_ge(sem("mixed"), i - 1)
            slot, c = i % 2, slice(col, col + n)
            done = sem(f"shifted{slot}")
            pool.dma_start(mu[:, slot, 0:n], A["rwkv_mu"][0, c].partition_broadcast(P)).then_inc(done, 16)
            pool.memset(zprev[0:1, slot, 0, :], 0.0).then_inc(sem("zero_row"), 1)
            pool.dma_start(zprev[1:P, slot, :, 0:n], zb[0:P - 1, :, c]).then_inc(done, 16)
            pool.dma_start(zprev[0:1, slot, 1:2, 0:n], zb[P - 1:P, 0:1, c]).then_inc(done, 16)

    def kk_pool(pool):
        pool.dma_start(p_kk[:], A["rwkv_k_k"][0].partition_broadcast(P)).then_inc(sem("kk_in"), 16)
        pool.wait_ge(sem("mixed"), 3)
        pool.wait_ge(sem("a_pv"), 4)
        pool.wait_ge(sem("kk_in"), 16)
        pool.tensor_tensor(kk0, kv.rearrange("p t (f c) -> p t f c", f=2),
                           p_kk[:].rearrange("p (f c) -> p f c", f=2).unsqueeze(1).broadcast_to([P, TT, 2, W]),
                           ALU.mult).then_inc(sem("kk"), 1)
        pool.wait_ge(sem("kk"), 1)
        pool.memset(loraT[LW:LW + 1, 0:2, :], 1.0).then_inc(sem("ones"), 1)
        pool.wait_ge(sem("ones"), 1)
        for tt in range(TT):
            if tt:
                pool.wait_ge(sem("kk_sum"), 1)
            pool.tensor_tensor(kk_sq[:].rearrange("p (f c) -> p f c", f=2), kk0[:, tt], kk0[:, tt],
                               ALU.mult).then_inc(sem("kk"), 1)

    def kk_sum_dve(dve, tt):
        dve.wait_ge(sem("kk"), 2 + tt)
        dve.tensor_reduce(nrm[:, tt, :], kk_sq[:].rearrange("p (h c) -> p h c", c=BH), AX.X,
                          ALU.add).then_inc(sem("kk_sum"), 1)

    def kk_norm_dve(dve, link):
        dve.wait_ge(sem("kk_sum"), 2)
        n32 = nrm[:].rearrange("p t h -> p (t h)")
        link(dve.tensor_scalar(n32, n32, 1e-24, None, ALU.max))
        rsqrt(dve, link, n32).then_inc(sem("kk_norm"), 1)

    def kk_norm_pool(pool):
        pool.wait_ge(sem("kk_norm"), 1)
        for tt in range(TT):
            for f in range(2):
                x = kk0[:, tt, f].rearrange("p (h c) -> p h c", c=BH)
                pool.tensor_tensor(x, x, nrm[:, tt, 8 * f:8 * f + 8].unsqueeze(2).broadcast_to([P, 8, BH]),
                                   ALU.mult).then_inc(sem("kk"), 1)

    def lora_weights_pool(pool):
        pool.wait_ge(lo_ready, 4 * (base["ab_in"] + N_AB - 1) + 1)
        for dst, w, b in ((w2, "rwkv_w2", "rwkv_w0"), (a2, "rwkv_a2", "rwkv_a0")):
            pool.dma_start(dst[0:LW, :], A[w][0]).then_inc(sem("lora_in"), 16)
            pool.dma_start(dst[LW:LW + 1, :], A[b][0].unsqueeze(0)).then_inc(sem("lora_in"), 16)

    def lora_params_pool(pool):
        last_lo = 4 * (base["ab_in"] + N_AB - 1)
        pool.wait_ge(lo_ready, last_lo + 2)
        pool.dma_start(g2[:], A["rwkv_g2"][0].rearrange("(k p) n -> p k n", p=P)).then_inc(sem("g2_in"), 16)
        pool.wait_ge(lo_ready, last_lo + 4)
        pool.dma_start(p_ka[:], A["rwkv_k_a"][0].partition_broadcast(P)).then_inc(sem("ka_in"), 16)
        pool.dma_start(p_rk[:], A["rwkv_r_k"][0].rearrange("h c -> (h c)").partition_broadcast(P))\
            .then_inc(sem("rk_in"), 16)

    def mix_dve(dve, link, i):
        _, col, n = ab_slabs[R0 + i]
        slot = i % 2
        dve.wait_ge(sem(f"shifted{slot}"), 48 * (i // 2 + 1))
        dve.wait_ge(sem("zero_row"), i + 1)
        z, d = zb[:, :, col:col + n], zprev[:, slot, :, 0:n]
        link(dve.tensor_tensor(d, d, z, ALU.subtract))
        link(dve.tensor_tensor(d, d, mu[:, slot, 0:n].unsqueeze(1).broadcast_to([P, TT, n]), ALU.mult))
        dve.tensor_tensor(z, z, d, ALU.add).then_inc(sem("mixed"), 1)

    def rope_heads_dve(dve, link, g, w, tt):
        if w + tt == 0:
            dve.wait_ge(sem("ev_ab_in"), 3 * g + 2)
            dve.wait_ge(sem("trig"), 2)
        x = za[:, tt, w * AW + g * W:w * AW + (g + 1) * W].rearrange("p (h d) -> p h d", d=A_DC)
        last = rope(dve, link, x, tt, 0, HALF_A, rt)
        if w + tt < 2:
            link(last)
        else:
            last.then_inc(sem("roped"), 1)

    def ab_in_dve(dve, link):
        st, b = "ab_in", base["ab_in"]
        prologue(split_lo, dve, st)
        h_first(dve, link, st, b, W, GAIN[st], prv[st])
        for i, (_, _, n) in enumerate(ab_slabs):
            s, hd = b + i, i - H0
            if i:
                split_lo(dve, s, 2, n)
                if i in (3, 6):
                    rope_heads_dve(dve, link, i // 3 - 1, 0, 1)
                if i == 11:
                    kk_sum_dve(dve, 0)
                if 0 <= hd < A_HEADS:
                    head_mask_dve(dve, link, hd)
                split_lo(dve, s, 3, n)
                if i in (3, 6):
                    rope_heads_dve(dve, link, i // 3 - 1, 1, 0)
                if 0 <= hd < A_HEADS:
                    head_weights_dve(dve, link, hd)
            if i + 1 < N_AB:
                nn = ab_slabs[i + 1][2]
                split_lo(dve, s + 1, 0, nn)
                if i in (3, 6):
                    rope_heads_dve(dve, link, i // 3 - 1, 1, 1)
                if i == 11:
                    kk_sum_dve(dve, 1)
                    kk_norm_dve(dve, link)
                split_lo(dve, s + 1, 1, nn)
            if i == 0:
                trig_dve(dve, link)
                dve.wait_ge(sem("consts"), N_CONSTS)
                link(dve.tensor_reduce(first_half[:], m_lvt[:], AX.X, ALU.max))
                link(dve.tensor_scalar(first_half[:], first_half[:], -1.0, 1.0, ALU.mult, ALU.add))
                dve.wait_ge(sem("attn_in"), 64)
                for c in range(2):
                    link(dve.tensor_tensor(lqk[:, 2 * c, :], lqk[:, 2 * c, :], lqk[:, 2 * c + 1, :], ALU.mult))
                    last = dve.tensor_reduce(lam[:, c:c + 1], lqk[:, 2 * c, :], AX.X, ALU.add)
                    if c == 0:
                        link(last)
                last.then_inc(sem("lam_sums"), 1)
            if i == 2:
                dve.wait_ge(sem("lam_exp"), 1)
                link(dve.tensor_tensor(lam[:, 2:3], lam[:, 1:2], lam[:, 0:1], ALU.subtract))
                link(dve.tensor_scalar(lam[:, 2:3], lam[:, 2:3], -LAMBDA_INIT, None, ALU.add))
                dve.wait_ge(sem("mask_in"), 2)
            if i in (2, 5):
                rope_heads_dve(dve, link, i // 3, 0, 0)
            if i > R0:
                mix_dve(dve, link, i - R0 - 1)
        mix_dve(dve, link, N_AB - R0 - 1)

    PARTS3 = ((0, slice(0, P), 1), (1, slice(P, 3 * P), 2))

    def head_transposes_pe(pe, hd):
        pe.wait_ge(sem("roped"), hd // 4 + 1)
        if hd:
            pe.wait_ge(sem("qkT"), hd)
        for w in range(2):
            for tt in range(TT):
                last = pe.transpose(bank[4][:, (2 * w + tt) * P:(2 * w + tt + 1) * P],
                                    za[:, tt, w * AW + hd * P:w * AW + (hd + 1) * P], ident[:])
        last.then_inc(sem("qk_tr"), 1)

    def head_transposes_act(act, hd):
        act.wait_ge(sem("qk_tr"), hd + 1)
        act.activation(qkT[:], bank[4], ACT.Copy).then_inc(sem("qkT"), 1)

    def head_scores_pe(pe, hd):
        pe.wait_ge(sem("qkT"), hd + 1)
        if hd:
            pe.wait_ge(sem("a_masked"), hd)
            pe.wait_ge(sem("a_y"), hd)
        for tt, cols, _ in PARTS3:
            for c in range(2):
                r = slice(c * A_DC, (c + 1) * A_DC)
                last = pe.matmul(bank[5 + c][:, cols], qkT[r, 0, tt * P:(tt + 1) * P], qkT[r, 1, 0:(tt + 1) * P],
                                 start=True, stop=True)
        last.then_inc(sem("a_scores"), 1)

    def head_mask_dve(dve, link, hd):
        dve.wait_ge(sem("a_scores"), hd + 1)
        if hd:
            dve.wait_ge(sem("a_exp"), 4 * hd)
        x = psum[:, 5 * 512:7 * 512].rearrange("p (c k) -> p c k", c=2)[:, :, 0:3 * P]
        dve.scalar_tensor_tensor(out=sm[:], in0=x, scalar=A_DC ** -0.5,
                                 in1=cau3[:].unsqueeze(1).broadcast_to([P, 2, 3 * P]), op0=ALU.mult,
                                 op1=ALU.add).then_inc(sem("a_masked"), 1)
        dve.wait_ge(sem("a_masked"), hd + 1)
        for tt, cols, _ in PARTS3:
            last = dve.tensor_reduce(mx[:, 0, 2 * tt:2 * tt + 2], sm[:, :, cols], AX.X, ALU.max)
            link(last)
        dve.tensor_scalar(mx[:, 1, :], mx[:, 0, :], -1.0, None, ALU.mult).then_inc(sem("a_max"), 1)

    def head_exp_act(act, hd):
        act.wait_ge(sem("a_max"), hd + 1)
        if hd:
            act.wait_ge(sem("a_weights"), hd)
        for tt, cols, _ in PARTS3:
            for c in range(2):
                i = 2 * tt + c
                act.activation(pe_[:, c, cols], sm[:, c, cols], ACT.Exp, bias=mx[:, 1, i:i + 1],
                               accum_out=mx[:, 2, i:i + 1]).then_inc(sem("a_exp"), 1)

    def head_weights_dve(dve, link, hd):
        dve.wait_ge(sem("a_exp"), 4 * hd + 4)
        if hd:
            dve.wait_ge(sem("a_wT_tr"), hd)
        link(dve.reciprocal(mx[:, 3, :], mx[:, 2, :]))
        second = mx[:, 3, 1:4:2]
        link(dve.tensor_scalar(second, second, lam[:, 2:3], None, ALU.mult))
        for tt, cols, _ in PARTS3:
            link(dve.tensor_scalar(at_[:, cols], pe_[:, 0, cols], mx[:, 3, 2 * tt:2 * tt + 1], None, ALU.mult))
            last = dve.scalar_tensor_tensor(out=at_[:, cols], in0=pe_[:, 1, cols],
                                            scalar=mx[:, 3, 2 * tt + 1:2 * tt + 2], in1=at_[:, cols],
                                            op0=ALU.mult, op1=ALU.add)
            if tt == 0:
                link(last)
        last.then_inc(sem("a_weights"), 1)

    def head_weights_pe(pe, hd):
        pe.wait_ge(sem("a_weights"), hd + 1)
        if hd:
            pe.wait_ge(sem("a_wT"), hd)
        if hd + H0 - 10 in range(TT):
            pe.wait_ge(sem("lora_T"), hd + H0 - 9)
        for k in range(3):
            last = pe.transpose(bank[7][:, k * P:(k + 1) * P], at_[:, k * P:(k + 1) * P], ident[:])
        last.then_inc(sem("a_wT_tr"), 1)

    def head_weights_act(act, hd):
        act.wait_ge(sem("a_wT_tr"), hd + 1)
        act.activation(atT[:], bank[7][:, 0:3 * P], ACT.Copy).then_inc(sem("a_wT"), 1)

    def head_values_pe(pe, hd):
        pe.wait_ge(sem("a_wT"), hd + 1)
        for tt, _, n in PARTS3:
            for kb in range(n):
                last = pe.matmul(bank[5][:, tt * P:(tt + 1) * P], atT[:, tt + kb, :],
                                 za[:, kb, 2 * AW + hd * P:2 * AW + (hd + 1) * P], start=(kb == 0), stop=(kb == tt))
        last.then_inc(sem("a_pv"), 1)

    def head_out_act(act, hd):
        act.wait_ge(sem("a_pv"), hd + 1)
        act.activation(za[:, :, hd * P:(hd + 1) * P], bank[5][:, 0:T], ACT.Copy).then_inc(sem("a_y"), 1)

    y_heads = za[:, :, 0:AW].rearrange("p t (h d) -> p t h d", d=A_DV)

    def subln_dve(dve, link):
        dve.wait_ge(sem("a_sq"), 1)
        link(dve.tensor_reduce(r16[:].rearrange("p (t h) -> p t h", t=TT),
                               asq[:].rearrange("p t (h d) -> p t h d", d=A_DV), AX.X, ALU.add))
        link(dve.tensor_scalar(r16[:], r16[:], 1.0 / A_DV, SUBLN_EPS, ALU.mult, ALU.add))
        link(rsqrt(dve, link, r16[:]))
        dve.tensor_scalar(r16[:], r16[:], 1.0 - LAMBDA_INIT, None, ALU.mult).then_inc(sem("a_rms"), 1)

    def subln_square_pool(pool):
        pool.wait_ge(sem("a_y"), A_HEADS)
        pool.tensor_tensor(asq[:], za[:, :, 0:AW], za[:, :, 0:AW], ALU.mult).then_inc(sem("a_sq"), 1)

    def subln_pool(pool):
        pool.wait_ge(sem("a_rms"), 1)
        pool.wait_ge(sem("subg_in"), 16)
        for tt in range(TT):
            pool.tensor_tensor(y_heads[:, tt], y_heads[:, tt],
                               r16[:, tt * 8:tt * 8 + 8].unsqueeze(2).broadcast_to([P, 8, A_DV]),
                               ALU.mult).then_inc(sem("ya_scaled"), 1)
            pool.wait_ge(sem("ya_scaled"), tt + 1)
            pool.tensor_tensor(y_heads[:, tt], y_heads[:, tt], subg[:].unsqueeze(1).broadcast_to([P, 8, A_DV]),
                               ALU.mult).then_inc(sem("ya_done"), 1)

    lora_cuts = (0, LW, LW + LA, LW + LA + P, LW + LA + 2 * P)

    def lora_transposes_pe(pe, tt):
        pe.wait_ge(sem("lora_act"), 2)
        pe.wait_ge(sem("a_wT"), 10 + tt - H0)
        for j in range(4):
            x = zb[:, tt, 3 * BW + lora_cuts[j]:3 * BW + lora_cuts[j + 1]]
            last = pe.transpose(bank[7][0:lora_cuts[j + 1] - lora_cuts[j], j * P:(j + 1) * P], x, ident[:])
        last.then_inc(sem("lora_tr"), 1)

    def lora_out_act(act, tt):
        act.wait_ge(sem("lora_tr"), tt + 1)
        t = slice(tt * P, (tt + 1) * P)
        b2 = bank[7].rearrange("p (j t) -> p j t", j=4)
        act.activation(loraT[0:LW, 0:2, t], b2[0:LW, 0:2, :], ACT.Copy)
        act.activation(loraT[:, 2:4, t], b2[:, 2:4, :], ACT.Copy).then_inc(sem("lora_T"), 1)

    def lora_pe(pe, w):
        if w == 0:
            pe.wait_ge(sem("lora_in"), 64)
            pe.wait_ge(sem("ones"), 1)
            pe.wait_ge(sem("lora_T"), 2)
            pe.wait_ge(sem("a_wT"), A_HEADS)
            pe.wait_ge(sem("a_y"), A_HEADS)
        else:
            pe.wait_ge(sem("rw_sig"), 2)
        for tt in range(TT):
            for hf in range(2):
                last = pe.matmul(bank[4 + 2 * tt + hf], loraT[0:LW + 1, w, tt * P:(tt + 1) * P],
                                 (w2, a2)[w][0:LW + 1, hf * 512:(hf + 1) * 512], start=True, stop=True)
            last.then_inc(sem("lora_mm"), 1)

    def sigmoid_act(act, w):
        for tt in range(TT):
            act.wait_ge(sem("lora_mm"), 2 * w + tt + 1)
            if w + tt == 0:
                act.wait_ge(sem("a_weights"), A_HEADS)
                act.wait_ge(sem("a_pv"), A_HEADS)
            act.activation((lw, av)[w][:, tt, :], psum[:, (4 + 2 * tt) * 512:(6 + 2 * tt) * 512],
                           ACT.Sigmoid).then_inc(sem("rw_sig"), 1)

    t1 = at("t1", [P, TT, BW], F32, 96)
    ex3 = at("ex3", [P, TT, BW], F32, 104)
    rv, kv, vv = (zb[:, :, i * BW:(i + 1) * BW] for i in range(3))
    heads4 = lambda x: x.rearrange("p t (h c) -> p t h c", c=BH)
    over_t = lambda x: x[:].unsqueeze(1).broadcast_to([P, TT, BW])
    over_c = lambda x: x[:].unsqueeze(3).broadcast_to([P, TT, B_HEADS, BH])
    g2v = at("g2v", [P, TT, BW], F32, 171.5)
    XB = (4, 5, 6, 7)
    x_src = (kkv[:], av[:], kv, rv)

    def x_groups(tt):
        return [[x_src[i][:, tt, (4 * g + p) * P:(4 * g + p + 1) * P] for p in range(4)]
                for i in range(4) for g in range(2)]
    x_outs = [[(XT[tt][i][:, 4 * g:4 * g + 4, :], P, 0, 512) for i in range(4) for g in range(2)] for tt in range(TT)]
    slot_of = lambda hd: ((hd // 8) * 2 + hd % 2) * 4 + (hd // 2) % 4
    def halves(x, b, k):
        return x.rearrange("p (j c) -> p j c", c=2 * b)[:, :, k * b:(k + 1) * b]

    flat = lambda x: x[:].rearrange("p i t -> p (i t)")
    DV, DL = 14, 9

    def rwkv_pool(pool):
        subln_square_pool(pool)
        pool.wait_ge(sem("rw_b"), 1)
        pool.wait_ge(sem("ex"), 2)
        pool.tensor_tensor(av[:], av[:], ex2[:], ALU.mult).then_inc(sem("rw_x"), 1)
        pool.wait_ge(sem("rw_a"), 2)
        for s in range(2):
            pool.memset(tmp_set[s][2][:], 0.0).then_inc(sem("y1_zero"), 1)
        pool.wait_ge(sem("rw_gm"), 4)
        pool.memset(ST[:], 0.0).then_inc(sem("st_zero"), 1)
        pool.dma_start(lnx_g[:], A["rwkv_lnx_g"][0].partition_broadcast(P)).then_inc(sem("lnx_in"), 16)
        pool.dma_start(lnx_b[:], A["rwkv_lnx_b"][0].partition_broadcast(P)).then_inc(sem("lnx_in"), 16)
        tr_all(pool, "x0", 8)
        tr_all(pool, "x1", 8)
        for tt in range(TT):
            for gp in range(2):
                rd = 2 * tt + gp
                bc = lambda x: x.unsqueeze(1).broadcast_to([P, 4, P])
                for s in range(2):
                    g = 2 * gp + s
                    MT, Ti, Y1 = tmp_set[s]
                    pool.wait_ge(sem(f"dv{s}"), DV * rd + 1)
                    T_ = TTi[:, 4 * g:4 * g + 4, :]
                    pool.tensor_tensor(T_, MT[:], bc(m_l1[:]), ALU.mult).then_inc(sem("tt_m"), 1)
                    pool.wait_ge(sem("tt_m"), 2 * rd + s + 1)
                    pool.tensor_tensor(T_, T_, bc(ident[:]), ALU.add).then_inc(sem(f"tt{s}"), 1)
                if rd == 0:
                    pool.wait_ge(sem("rw_rk"), 2)
                    pool.wait_ge(sem("rk_in"), 16)
                    pool.tensor_tensor(rkr[:], rv, kv, ALU.mult).then_inc(sem("bonus"), 1)
                    pool.wait_ge(sem("bonus"), 1)
                    pool.tensor_tensor(rkr[:], rkr[:], over_t(p_rk), ALU.mult).then_inc(sem("bonus"), 1)
                if rd >= 2:
                    t = rd - 2
                    pool.wait_ge(sem("rw_g"), 2)
                    pool.wait_ge(sem("lnx_in"), 32)
                    pool.wait_ge(sem("bon"), 1)
                    g = gv[t][:]
                    o, v = g2v[:, t, :], vv[:, t, :].rearrange("p (h c) -> p h c", c=BH)
                    o3 = o.rearrange("p (h c) -> p h c", c=BH)
                    pool.tensor_tensor(o3, v, bon[:, t, :].unsqueeze(2).broadcast_to([P, B_HEADS, BH]),
                                       ALU.mult).then_inc(sem("gated_y"), 1)
                    pool.wait_ge(sem("gated_y"), 4 * t + 1)
                    pool.tensor_tensor(o, o, lnx_b[:], ALU.add).then_inc(sem("gated_y"), 1)
                    pool.wait_ge(sem("gated_y"), 4 * t + 2)
                    pool.tensor_tensor(o, o, g, ALU.mult).then_inc(sem("gated_y"), 1)
                    pool.wait_ge(sem("gated_y"), 4 * t + 3)
                    pool.tensor_tensor(g, g, lnx_g[:], ALU.mult).then_inc(sem("gated_y"), 1)
        subln_pool(pool)
        pool.wait_ge(lo_ready, 4 * base["ab_out"] + 2)
        for q in (2, 3):
            split_lo(pool, base["ab_out"], q)

    def rwkv_pe(pe):
        lora_pe(pe, 1)
        pe.wait_ge(sem("consts"), N_CONSTS)
        pe.wait_ge(sem("ev_ab_in"), N_AB)
        for mask, b0 in ((m_ui, 0), (m_su, 4)):
            if b0:
                pe.wait_ge(sem("rw_sig"), 4)
            for tt in range(TT):
                for hf in range(2):
                    last = pe.matmul(bank[b0 + 2 * tt + hf], mask[:], lw[:, tt, hf * 512:(hf + 1) * 512], start=True, stop=True)
            last.then_inc(sem("cum"), 1)
        pe.wait_ge(sem("ex"), 3)
        for p in range(8):
            for tt in range(TT):
                last = pe.matmul(bank[4][:, 4 * p + 2 * tt:4 * p + 2 * tt + 2], lw[:, tt, p * P:(p + 1) * P],
                                 m_ui[:, CH - 1:P:CH], start=True, stop=True)
        last.then_inc(sem("cum"), 1)
        pe.wait_ge(sem("g2_in"), 16)
        for tt in range(TT):
            for hf in range(2):
                o, c, t = bank[2 * tt + hf], slice(hf * 512, hf * 512 + 512), slice(tt * P, (tt + 1) * P)
                pe.matmul(o, loraT[:, 2, t], g2[:, 0, c], start=True, stop=False)
                pe.matmul(o, loraT[:, 3, t], g2[:, 1, c], start=False, stop=True).then_inc(sem("rw_gm"), 1)
        tr_pe(pe, "x0", x_groups(0), XB, [(sem("rw_x"), 1), (sem("rw_rk"), 2), (sem("rw_a"), 2), (sem("ex"), 4)])
        tr_all(pe, "x0", 8)
        tr_pe(pe, "x1", x_groups(1), XB)
        tr_all(pe, "x1", 8)
        for tt in range(TT):
            AT, BT, KT_, RT = XT[tt]
            if tt == 0:
                pe.wait_ge(sem("rw_g"), 2)
            if tt == 1:
                pe.wait_ge(sem("y_out"), 2)
                pe.wait_ge(sem("st_upd"), 4)
            for gp in range(2):
                rd = 2 * tt + gp
                if gp == 1:
                    for s in range(2):
                        pe.wait_ge(sem(f"dv{s}"), DV * rd)
                        pe.wait_ge(sem(f"y1c{s}"), 5 * rd)
                plan_ = ((BT, AT, 0), (AT, BT, 1), (KT_, AT, 2), (BT, RT, 3))
                for s in range(2):
                    r = slice(64 * s, 64 * s + 64)
                    for l_, r_, bk in plan_:
                        for i in range(4):
                            last = pe.matmul(bank[4 * s + bk][:, i * P:(i + 1) * P], l_[r, 4 * gp + i, :],
                                             r_[r, 4 * gp + i, :], start=True, stop=True)
                        last.then_inc(sem(f"mats{s}"), 1)
                for s in range(2):
                    r = slice(64 * s, 64 * s + 64)
                    pe.wait_ge(sem(f"dv{s}"), DV * rd + 2)
                    for i in range(4):
                        last = pe.matmul(bank[4 * s + 1][:, i * P:(i + 1) * P], KT_[r, 4 * gp + i, :],
                                         RT[r, 4 * gp + i, :], start=True, stop=True)
                    last.then_inc(sem(f"mats{s}"), 1)
                for li in range(1, 6):
                    for s in range(2):
                        MT, Ti, Y1 = tmp_set[s]
                        pe.wait_ge(sem(f"dv{s}"), DV * rd + (2 if li == 1 else 5 + 2 * (li - 1)))
                        for i in range(4):
                            last = pe.matmul(bank[4 * s][:, i * P:(i + 1) * P], MT[:, i, :], Ti[:, i, :],
                                             start=True, stop=True)
                        last.then_inc(sem(f"y1_{s}"), 1)
                    for s in range(2):
                        g = 2 * gp + s
                        MT, Ti, Y1 = tmp_set[s]
                        pe.wait_ge(sem(f"y1c{s}"), 5 * rd + li)
                        if li == 1:
                            pe.wait_ge(sem(f"tt{s}"), rd + 1)
                            pe.wait_ge(sem(f"dv{s}"), DV * rd + 4)
                        if li < 5:
                            for i in range(4):
                                last = pe.matmul(bank[4 * s + 2][:, i * P:(i + 1) * P], TTi[:, 4 * g + i, :],
                                                 Y1[:, i, :], start=True, stop=True)
                            last.then_inc(sem(f"dl{s}"), 1)
                        for i in range(4):
                            last = pe.matmul(bank[4 * s + 3][:, i * P:(i + 1) * P], Y1[:, i, :],
                                             TTi[:, 4 * g + i, :], start=True, stop=True)
                        last.then_inc(sem(f"dl{s}"), 1)
            for s in range(2):
                pe.wait_ge(sem(f"dv{s}"), DV * (2 * tt + 2))
                pe.wait_ge(sem(f"y1c{s}"), 5 * (2 * tt + 2))
            pe.wait_ge(sem("st_zero"), 1)
            for half in range(2):
                c = 2 * tt + half
                rows = slice(64 * half, 64 * half + 64)
                pair = lambda b, p: bank[b + p // 4][:, (p % 4) * P:(p % 4 + 1) * P]
                head = lambda b, hd: bank[b + hd // 8][rows, (hd % 8) * BH:(hd % 8 + 1) * BH]
                if c:
                    pe.wait_ge(sem("x_out0"), c)
                    pe.wait_ge(sem("x_out1"), c)
                for hd in range(16):
                    pe.matmul(head(0, hd), NT[rows, slot_of(hd), rows], vv[rows, tt, hd * BH:(hd + 1) * BH], start=(hd % 8 == 0), stop=False)
                for p in range(8):
                    if c and p % 4 == 0:
                        pe.wait_ge(sem("st_upd"), 2 * c - 1 + p // 4)
                    last = pe.matmul(pair(0, p)[rows, :], AT[:, p, rows], ST[:, p, :], start=False, stop=(p % 4 == 3))
                    if p % 4 == 3:
                        last.then_inc(sem("x_mm"), 1)
                if c < 3:
                    for p in range(8):
                        cc = slice(p * P, (p + 1) * P)
                        pe.matmul(pair(6, p), ident[:], ST[:, p, :], start=(p % 4 == 0), stop=False)
                        pe.matmul(pair(6, p), kv[rows, tt, cc], vv[rows, tt, cc], start=False, stop=False)
                for hd in range(16):
                    if hd % 8 == 0:
                        pe.wait_ge(sem(f"x_out{hd // 8}"), c + 1)
                    last = pe.matmul(head(2, hd), TTi[rows, slot_of(hd), rows],
                                     Xs[rows, hd * BH:(hd + 1) * BH], start=True, stop=True)
                    if hd % 8 == 7:
                        last.then_inc(sem("u_mm"), 1)
                if c:
                    pe.wait_ge(sem("y_out"), c)
                for p in range(8):
                    pe.matmul(pair(4, p)[rows, :], RT[:, p, rows], ST[:, p, :], start=(p % 4 == 0), stop=False)
                    for hd in (2 * p, 2 * p + 1):
                        pe.matmul(head(4, hd), QT[rows, slot_of(hd), rows],
                                  vv[rows, tt, hd * BH:(hd + 1) * BH], start=False, stop=False)
                if c < 3:
                    for p in range(8):
                        if p % 4 == 0:
                            pe.wait_ge(sem(f"u_out{p // 4}"), c + 1)
                        cc = slice(p * P, (p + 1) * P)
                        last = pe.matmul(pair(6, p), av[rows, tt, cc], Us[rows, cc], start=False, stop=(p % 4 == 3))
                        if p % 4 == 3:
                            last.then_inc(sem("s_mm"), 1)
                else:
                    for e in range(2):
                        pe.wait_ge(sem(f"u_out{e}"), c + 1)
                for hd in range(16):
                    last = pe.matmul(head(4, hd), PT[rows, slot_of(hd), rows],
                                     Us[rows, hd * BH:(hd + 1) * BH], start=False, stop=(hd % 8 == 7))
                last.then_inc(sem("y_mm"), 1)

    def rwkv_act(act):
        sigmoid_act(act, 1)
        dec = -math.exp(-0.5)
        act.wait_ge(sem("cum"), 1)
        act.activation(ex1[:], psum[:, 0:4 * 512], ACT.Exp, scale=dec).then_inc(sem("ex"), 1)
        act.activation(ex2[:], psum[:, 0:4 * 512], ACT.Exp, scale=-dec).then_inc(sem("ex"), 1)
        act.wait_ge(sem("cum"), 2)
        act.activation(ex3[:], psum[:, 4 * 512:8 * 512], ACT.Exp, scale=dec).then_inc(sem("ex"), 1)
        act.wait_ge(sem("cum"), 3)
        act.activation(WL[:], bank[4][:, 0:32], ACT.Exp, scale=dec).then_inc(sem("ex"), 1)
        act.wait_ge(sem("mixed"), N_AB - R0)
        for tt in range(TT):
            act.wait_ge(sem("rw_gm"), 2 * tt + 2)
            act.activation(gv[tt][:], psum[:, 2 * tt * 512:(2 * tt + 2) * 512], ACT.Copy).then_inc(sem("rw_g"), 1)
        tr_out(act, "x0", x_outs[0], XB, 0)
        tr_out(act, "x1", x_outs[1], XB, 0)
        for tt in range(TT):
            if tt == 1:
                prologue(split_hi, act, "ab_out")
            for half in range(2):
                c = 2 * tt + half
                rows = slice(64 * half, 64 * half + 64)
                act.wait_ge(sem("x_mm"), 2 * c + 1)
                act.activation(Xs[rows, 0:512], bank[0][rows, :], ACT.Copy).then_inc(sem("x_out0"), 1)
                act.wait_ge(sem("u_mm"), 2 * c + 1)
                act.activation(Us[rows, 0:512], bank[2][rows, :], ACT.Copy).then_inc(sem("u_out0"), 1)
                act.wait_ge(sem("y_mm"), c + 1)
                act.activation(zb[rows, tt, 0:BW], psum[rows, 4 * 512:6 * 512], ACT.Copy).then_inc(sem("y_out"), 1)

    def rwkv_dve(dve, link):
        dve.wait_ge(sem("rw_sig"), 4)
        dve.wait_ge(sem("ka_in"), 16)
        dve.wait_ge(mm_used, 4 * (base["ab_in"] + N_AB))
        link(dve.scalar_tensor_tensor(out=t1[:], in0=av[:], scalar=-1.0, in1=over_t(p_ka), op0=ALU.add, op1=ALU.mult))
        link(dve.scalar_tensor_tensor(out=kv, in0=t1[:], scalar=1.0, in1=kv, op0=ALU.add, op1=ALU.mult))
        dve.wait_ge(sem("kk"), 7)
        a4 = lambda x: x[:].rearrange("p t (f c) -> p t f c", f=2)
        dve.tensor_tensor(a4(av), kk0, a4(av), ALU.mult).then_inc(sem("rw_b"), 1)
        dve.wait_ge(sem("ex"), 2)
        dve.tensor_tensor(rv, rv, ex1[:], ALU.mult).then_inc(sem("rw_rk"), 1)
        dve.tensor_tensor(kv, kv, ex2[:], ALU.mult).then_inc(sem("rw_rk"), 1)
        dve.wait_ge(sem("ex"), 3)
        for tt in range(TT):
            dve.scalar_tensor_tensor(out=a4(kkv)[:, tt], in0=kk0[:, tt], scalar=-1.0, in1=a4(ex3)[:, tt],
                                     op0=ALU.mult, op1=ALU.mult).then_inc(sem("rw_a"), 1)
        dve.wait_ge(sem("rw_rk"), 2)
        dve.wait_ge(sem("rw_a"), 2)
        dve.wait_ge(sem("rw_x"), 1)
        tr_out(dve, "x0", x_outs[0], XB, 1)
        tr_out(dve, "x1", x_outs[1], XB, 1)
        dve.wait_ge(sem("y1_zero"), 2)
        for tt in range(TT):
            for gp in range(2):
                rd = 2 * tt + gp
                bc = lambda x: x.unsqueeze(1).broadcast_to([P, 4, P])
                b4 = lambda i: bank[i].rearrange("p (i t) -> p i t", i=4)
                for s in range(2):
                    MT, Ti, Y1 = tmp_set[s]
                    dv = sem(f"dv{s}")
                    dve.wait_ge(sem(f"mats{s}"), 5 * rd + 1)
                    if rd:
                        dve.wait_ge(sem(f"tt{s}"), rd)
                    dve.tensor_tensor(MT[:], b4(4 * s), bc(m_su[:]), ALU.mult).then_inc(dv, 1)
                    dve.wait_ge(sem(f"mats{s}"), 5 * rd + 2)
                    link(dve.tensor_tensor(Ti[:], b4(4 * s + 1), bc(m_lvt[:, 0, :]), ALU.mult))
                    dve.tensor_tensor(Ti[:], Ti[:], bc(ident[:]), ALU.add).then_inc(dv, 1)
                for s in range(2):
                    g = 2 * gp + s
                    dv = sem(f"dv{s}")
                    sl = slice(4 * g, 4 * g + 4)
                    dve.wait_ge(sem(f"mats{s}"), 5 * rd + 4)
                    dve.tensor_tensor(NT[:, sl, :], b4(4 * s + 2), bc(m_su[:]), ALU.mult).then_inc(dv, 1)
                    dve.tensor_tensor(PT[:, sl, :], b4(4 * s + 3), bc(m_ui[:]), ALU.mult).then_inc(dv, 1)
                    dve.wait_ge(sem(f"mats{s}"), 5 * rd + 5)
                    dve.tensor_tensor(QT[:, sl, :], b4(4 * s + 1), bc(m_ui[:]), ALU.mult).then_inc(dv, 1)
                for li in range(1, 6):
                    for s in range(2):
                        dve.wait_ge(sem(f"y1_{s}"), 5 * rd + li)
                        quarters = lambda x: x.rearrange("p i (j c) -> p i j c", c=2 << li)[:, :, :, 0:1 << li]
                        dve.tensor_tensor(quarters(tmp_set[s][2][:]), quarters(b4(4 * s)),
                                          quarters(bc(m_lvt[:, li, :])), ALU.mult).then_inc(sem(f"y1c{s}"), 1)
                    for s in range(2):
                        g = 2 * gp + s
                        MT, Ti, Y1 = tmp_set[s]
                        dv, T_ = sem(f"dv{s}"), halves(TTi[:, 4 * g:4 * g + 4, :].rearrange("p i t -> p (i t)"), 1 << li, 1)
                        if li < 5:
                            dve.wait_ge(sem(f"dl{s}"), DL * rd + 2 * li)
                            x = halves(flat(Ti), 1 << li, 0)
                            dve.tensor_tensor(x, x, halves(bank[4 * s + 2], 1 << li, 0), ALU.add).then_inc(dv, 1)
                        else:
                            dve.wait_ge(sem(f"dl{s}"), DL * rd + 9)
                        dve.scalar_tensor_tensor(out=T_, in0=halves(bank[4 * s + 3], 1 << li, 1),
                                                 scalar=first_half[:, li:li + 1], in1=T_, op0=ALU.mult,
                                                 op1=ALU.add).then_inc(dv, 1)
                    if rd == 3:
                        out_norm_dve(dve, link, 0, li - 1)
                if rd == 1:
                    dve.wait_ge(sem("bonus"), 2)
                    dve.tensor_reduce(bon[:], heads4(rkr[:]), AX.X, ALU.add).then_inc(sem("bon"), 1)
                if rd == 2:
                    subln_dve(dve, link)
            for half in range(2):
                c = 2 * tt + half
                rows = slice(64 * half, 64 * half + 64)
                dve.wait_ge(sem("x_mm"), 2 * c + 2)
                dve.tensor_copy(Xs[rows, 512:1024], bank[1][rows, :]).then_inc(sem("x_out1"), 1)
                dve.wait_ge(sem("u_mm"), 2 * c + 2)
                dve.tensor_copy(Us[rows, 512:1024], bank[3][rows, :]).then_inc(sem("u_out1"), 1)
                if c == 3:
                    prologue(split_lo, dve, "ab_out")
                for g in range(2 if c < 3 else 0):
                    dve.wait_ge(sem("s_mm"), 2 * c + 1 + g)
                    for e in range(2):
                        hs = slice(64 * e, 64 * e + 64)
                        x2 = bank[6 + g][hs, :].rearrange("p (a t) -> p a t", a=4)[:, :, hs]
                        last = dve.tensor_tensor(ST[hs, 4 * g:4 * g + 4, hs], x2,
                                                 WL[hs, 4 * g:4 * g + 4, c:c + 1].broadcast_to([64, 4, 64]), ALU.mult)
                    last.then_inc(sem("st_upd"), 1)

    def out_norm_dve(dve, link, tt, k):
        y, s = rv[:, tt, :], nrm[:, tt, :]
        by_head = lambda x: x.rearrange("p (h c) -> p h c", c=BH)
        y3, sq = by_head(y), by_head(Xs[:])
        over = s.unsqueeze(2).broadcast_to([P, B_HEADS, BH])
        if k == 0:
            dve.wait_ge(sem("y_out"), 2 * tt + 2)
            link(dve.tensor_reduce(s, y3, AX.X, ALU.add))
            link(dve.tensor_scalar(s, s, -1.0 / BH, None, ALU.mult))
        if k == 1:
            link(dve.tensor_tensor(y3, y3, over, ALU.add))
        if k == 2:
            link(dve.tensor_tensor(sq, y3, y3, ALU.mult))
            link(dve.tensor_reduce(s, sq, AX.X, ALU.add))
        if k == 3:
            link(dve.tensor_scalar(s, s, 1.0 / BH, LNX_EPS, ALU.mult, ALU.add))
            link(rsqrt(dve, link, s))
        if k == 4:
            dve.wait_ge(sem("gated_y"), 4 * tt + 4)
            for b in range(2):
                c, hd = slice(b * W, (b + 1) * W), slice(b * B_HEADS // 2, (b + 1) * B_HEADS // 2)
                link(dve.tensor_tensor(y3[:, hd], y3[:, hd], over[:, hd], ALU.mult))
                link(dve.tensor_tensor(y[:, c], y[:, c], gv[tt][:, c], ALU.mult))
                dve.tensor_tensor(y[:, c], y[:, c], g2v[:, tt, c], ALU.add).then_inc(sem("yb_done"), 1)

    C1, C2 = C_HEADS * C_HD, C_HEADS * C_HD + C_KV * C_HD
    C3 = C2 + C_KV * C_HD
    C4 = C3 + IDX_H * IDX_D
    C5 = C4 + IDX_D
    zc = at("zc", [P, TT, C_IN], F32, 120)
    qTc = at("qTc", [P, C_HEADS, T], F32, 153)
    kTc = at("kTc", [P, C_KV, T], F32, 169)
    qiT = at("qiT", [P, IDX_H // 2, T], F32, 173)
    kiT = at("kiT", [P, T], F32, 181)
    score = at("score", [P, TT, T], F32, 182)
    mb = at("mb", [P, TT, T], F32, 184)
    rl_ = at("rl_", [P, 2, 2, T], F32, 186)
    smc = at("smc", [P, 2, 2, T], F32, 190)
    pc = at("pc", [P, 2, 2, T], F32, 194)
    pcT = at("pcT", [P, 2, 4, P], F32, 198)
    kid = at("kid", [P, TT, P], F32, 202)
    rtc = at("rtc", [P, 4, 256], F32, 203)
    mxc = at("mxc", [P, 2, 8], F32, 152.625)
    rlc = at("rlc", [P, 4, 2], F32, 152.75)
    m8 = at("m8", [P, 8], F32, 152.8125)
    ikg = at("ikg", [P, 2, IDX_D], F32, 190)
    wis = at("wis", [P, TT, IDX_H], F32, 190.5)
    ki2 = at("ki2", [P, TT, IDX_D], F32, 191)
    lns = at("lns", [P, 4], F32, 191.5)
    c_slabs = [(C3 + j * C_W, C_W) for j in range(3)] + [(C1, W), (C2, W)] + [(j * W, W) for j in range(4)]
    N_C = len(c_slabs)
    T_LN, T_QI, T_UNITS, T_TOPK = 13, 18, 20, 28
    qk_blocks = [(3, 17, 29, 4), (5, 25, 30, 6), (6, 29, 32, 4), (7, 33, 35, 6), (8, 37, 37, 4)]
    c_units = [(tt, hp) for tt in range(TT) for hp in range(8)]
    nu = len(c_units)

    def c_side_pe(pe, t):
        if t == T_QI:
            pe.wait_ge(sem("qi_roped"), 1)
            for g in range(4):
                for j, hp in enumerate((2 * g, 2 * g + 1)):
                    for tt in range(TT):
                        last = pe.transpose(bank[4 + g][:, (2 * j + tt) * P:(2 * j + tt + 1) * P],
                                            zc[:, tt, C3 + hp * P:C3 + (hp + 1) * P], ident[:])
                last.then_inc(sem("qi_tr"), 1)
        if t == T_QI + 1:
            pe.wait_ge(sem("qi_out"), 1)
            for tt in range(TT):
                last = pe.transpose(bank[4][:, tt * P:(tt + 1) * P], kid[:, tt, :], ident[:])
            last.then_inc(sem("qi_tr"), 1)
        if T_UNITS <= t < T_UNITS + nu // 2:
            for i in (2 * (t - T_UNITS), 2 * (t - T_UNITS) + 1):
                tt, hp = c_units[i]
                nk = (tt + 1) * P
                if i == 0:
                    pe.wait_ge(sem("qi_out"), 5)
                if i >= 2:
                    pe.wait_ge(sem("i_relu"), i - 1)
                for j in range(2):
                    r = slice(64 * j, 64 * j + 64)
                    last = pe.matmul(bank[4 + 2 * (i % 2) + j][:, 0:nk], qiT[r, hp, tt * P:(tt + 1) * P], kiT[r, 0:nk],
                                     start=True, stop=True)
                last.then_inc(sem("i_mm"), 1)
        for n, (i, _, t_tr, b) in enumerate(qk_blocks):
            if t == t_tr:
                pe.wait_ge(sem("qc_roped"), n + 1)
                if n == 0:
                    pe.wait_ge(sem("i_relu"), nu)
                if n >= 2:
                    pe.wait_ge(sem("qc_out"), 2 * n - 2)
                col = c_slabs[i][0]
                for g in range(2):
                    for j in range(2):
                        for tt in range(TT):
                            c = col + (2 * g + j) * P
                            last = pe.transpose(bank[b + g][:, (2 * j + tt) * P:(2 * j + tt + 1) * P],
                                                zc[:, tt, c:c + P], ident[:])
                    last.then_inc(sem("qc_tr"), 1)

    def c_side_act(act, t):
        if t == T_QI:
            for g in range(4):
                act.wait_ge(sem("qi_tr"), g + 1)
                act.activation(qiT[:, 2 * g:2 * g + 2, :], bank[4 + g], ACT.Copy).then_inc(sem("qi_out"), 1)
        if t == T_QI + 1:
            act.wait_ge(sem("qi_tr"), 5)
            act.activation(kiT[:], bank[4][:, 0:T], ACT.Copy).then_inc(sem("qi_out"), 1)
        if T_UNITS <= t < T_UNITS + nu // 2:
            for i in (2 * (t - T_UNITS), 2 * (t - T_UNITS) + 1):
                tt, hp = c_units[i]
                nk = (tt + 1) * P
                act.wait_ge(sem("i_mm"), i + 1)
                if i >= 2:
                    act.wait_ge(sem("i_added"), 2 * (i - 1))
                b0 = (4 + 2 * (i % 2)) * 512
                x = psum[:, b0:b0 + 1024].rearrange("p (c k) -> p c k", c=2)[:, :, 0:nk]
                act.activation(rl_[:, i % 2, :, 0:nk], x, ACT.Relu).then_inc(sem("i_relu"), 1)
        for n, (i, _, t_tr, b) in enumerate(qk_blocks):
            if t == t_tr:
                for g in range(2):
                    act.wait_ge(sem("qc_tr"), 2 * n + g + 1)
                    o = kTc[:, 2 * g:2 * g + 2, :] if n == 0 else qTc[:, 4 * (n - 1) + 2 * g:4 * (n - 1) + 2 * g + 2, :]
                    act.activation(o, bank[b + g], ACT.Copy).then_inc(sem("qc_out"), 1)

    def c_side_dve(dve, link, t):
        x = zc[:, :, C4:C5]
        over64 = lambda v: v.unsqueeze(2).broadcast_to([P, TT, IDX_D])
        mean, var = lns[:, 0:2], lns[:, 2:4]
        if t == T_LN:
            dve.wait_ge(sem("ev_c_in"), 3)
            link(dve.tensor_reduce(mean, x, AX.X, ALU.add))
            link(dve.tensor_scalar(mean, mean, -1.0 / IDX_D, None, ALU.mult))
            link(dve.tensor_tensor(x, x, over64(mean), ALU.add))
            link(dve.tensor_tensor(ki2[:], x, x, ALU.mult))
            link(dve.tensor_reduce(var, ki2[:], AX.X, ALU.add))
            link(dve.tensor_scalar(var, var, 1.0 / IDX_D, LN_EPS, ALU.mult, ALU.add))
            link(rsqrt(dve, link, var))
            link(dve.tensor_tensor(x, x, over64(var), ALU.mult))
        if t == T_LN + 1:
            dve.wait_ge(sem("ikg_in"), 32)
            link(dve.tensor_tensor(x, x, ikg[:, 0, :].unsqueeze(1).broadcast_to([P, TT, IDX_D]), ALU.mult))
            link(dve.tensor_tensor(x, x, ikg[:, 1, :].unsqueeze(1).broadcast_to([P, TT, IDX_D]), ALU.add))
            link(dve.tensor_scalar(wis[:], zc[:, :, C5:C_IN], float((IDX_H * IDX_D) ** -0.5), None, ALU.mult))
            for tt in range(TT):
                link(rope(dve, link, zc[:, tt, C4:C5].unsqueeze(1), tt, 0, HALF_A, rtc))
                for j in range(2):
                    dve.tensor_copy(kid[:, tt, j * 64:(j + 1) * 64], zc[:, tt, C4:C5])
        if t - T_LN - 2 in range(TT):
            tt = t - T_LN - 2
            last = rope(dve, link, zc[:, tt, C3:C4].rearrange("p (h d) -> p h d", d=IDX_D), tt, 0, HALF_A, rtc)
            if tt == 0:
                link(last)
            else:
                last.then_inc(sem("qi_roped"), 1)
        for n, (i, t_rope, _, _) in enumerate(qk_blocks):
            if t == t_rope:
                dve.wait_ge(sem("ev_c_in"), i + 1)
                dve.wait_ge(sem("qi_roped"), 1)
                if n:
                    dve.wait_ge(sem("qc_roped"), n)
                col = c_slabs[i][0]
                for tt in range(TT):
                    last = rope(dve, link, zc[:, tt, col:col + W].rearrange("p (h d) -> p h d", d=C_HD), tt, HALF_A,
                                HALF_C, rtc)
                    if tt == 0:
                        link(last)
                last.then_inc(sem("qc_roped"), 1)
        added = sem("i_added")
        if T_UNITS <= t < T_UNITS + nu // 2:
            for i in (2 * (t - T_UNITS), 2 * (t - T_UNITS) + 1):
                tt, hp = c_units[i]
                nk = (tt + 1) * P
                dve.wait_ge(sem("i_relu"), i + 1)
                for j in range(2):
                    w_, sc, y = wis[:, tt, 2 * hp + j:2 * hp + j + 1], score[:, tt, 0:nk], rl_[:, i % 2, j, 0:nk]
                    if hp + j == 0:
                        dve.tensor_scalar(sc, y, w_, None, ALU.mult).then_inc(added, 1)
                    else:
                        dve.scalar_tensor_tensor(out=sc, in0=y, scalar=w_, in1=sc, op0=ALU.mult,
                                                 op1=ALU.add).then_inc(added, 1)
                    dve.wait_ge(added, 2 * i + j + 1)
        if t - T_TOPK in range(4 * TT):
            tt, part = (t - T_TOPK) // 4, (t - T_TOPK) % 4
            nk = (tt + 1) * P
            sc, ca = score[:, tt, 0:nk], causal[:, T - nk:T]
            if part == 0:
                link(dve.tensor_tensor(sc, sc, ca, ALU.add))
            for _ in range(TOPK // 32):
                link(dve.max(m8[:], sc))
                link(dve.match_replace(sc, m8[:], sc, TAKEN))
            if part == 3:
                link(dve.tensor_scalar(mb[:, tt, 0:nk], sc, TAKEN / 2, NEG, ALU.is_gt, ALU.mult))
                link(dve.tensor_tensor(mb[:, tt, 0:nk], mb[:, tt, 0:nk], ca, ALU.add))

    def c_in_pe(pe):
        st, b = "c_in", base["c_in"]
        pe_first(pe, st, b, b % 2, h_src, h_ready(st), c_slabs[0][1], free_of(st, 0))
        for i in range(1, N_C):
            mm_slab(pe, b + i, (b + i) % 2, c_slabs[i][1], (sem("ev_c_in"), i - 1) if i > 1 else free_of(st, 1),
                    lambda q: c_side_pe(pe, 4 * i + q))

    def c_in_side(fn, side, eng, st, keep):
        b = base[st]
        for i in range(N_C):
            s, n = b + i, c_slabs[i][1]
            for q in (2, 3):
                if i:
                    fn(eng, s, q, n)
                    side(4 * i + q - 1)
            for q in (0, 1):
                if i + 1 < N_C:
                    fn(eng, s + 1, q, c_slabs[i + 1][1])
                if q == 1 and keep:
                    keep(i)
                if i:
                    side(4 * i + q + 3)

    def c_in_act(act):
        st, b = "c_in", base["c_in"]
        prologue(split_hi, act, st)
        act_first(act, st, b, c_slabs[0][1], GAIN[st], h_squares(act, st))

        def keep(i):
            if i == 0:
                act.wait_ge(*mark("rstd", st, 1))
            act.wait_ge(mm_used, 4 * (b + i) + 4)
            col, n = c_slabs[i]
            for tt in range(TT):
                last = act.activation(zc[:, tt, col:col + n], bank[2 * ((b + i) % 2) + tt][:, 0:n], ACT.Copy,
                                      scale=rstd_h[:, tt:tt + 1])
            last.then_inc(sem("ev_c_in"), 1)
        c_in_side(split_hi, lambda t: c_side_act(act, t), act, st, keep)

    def c_in_dve(dve, link):
        st, b = "c_in", base["c_in"]
        prologue(split_lo, dve, st)
        h_first(dve, link, st, b, c_slabs[0][1], GAIN[st], prv[st])
        dve.wait_ge(sem("trig"), 2)
        c_in_side(split_lo, lambda t: c_side_dve(dve, link, t), dve, st, None)

    def c_pool(pool):
        pool.wait_ge(sem("ev_c_in"), 1)
        for i, n in enumerate(("idx_k_g", "idx_k_b")):
            pool.dma_start(ikg[:, i, :], A[n][0].partition_broadcast(P)).then_inc(sem("ikg_in"), 16)
        pool.wait_ge(lo_ready, 4 * base["c_out"])
        prologue(split_lo, pool, "c_out")

    def c_pe(pe):
        c_side_pe(pe, 4 * N_C + 1)
        pe.wait_ge(sem("qc_out"), 2 * len(qk_blocks))
        pe.wait_ge(sem("ev_c_in"), N_C)
        for i in range(nu + 3):
            if i < nu:
                tt, hp = c_units[i]
                nk = (tt + 1) * P
                if i >= 2:
                    pe.wait_ge(sem("c_masked"), i - 1)
                for j in range(2):
                    last = pe.matmul(bank[2 * (i % 2) + j][:, 0:nk], qTc[:, 2 * hp + j, tt * P:(tt + 1) * P],
                                     kTc[:, hp // 2, 0:nk], start=True, stop=True)
                last.then_inc(sem("c_scores"), 1)
            if 0 <= i - 2 < nu:
                u = i - 2
                tt, hp = c_units[u]
                pe.wait_ge(sem("c_exp"), 2 * u + 2)
                if u >= 2:
                    pe.wait_ge(sem("c_wT"), u - 1)
                for j in range(2):
                    for kb in range(tt + 1):
                        q = j * (tt + 1) + kb
                        last = pe.transpose(bank[4 + u % 2][:, q * P:(q + 1) * P], pc[:, u % 2, j, kb * P:(kb + 1) * P],
                                            ident[:])
                last.then_inc(sem("c_tr"), 1)
            if 0 <= i - 3 < nu:
                u = i - 3
                tt, hp = c_units[u]
                pe.wait_ge(sem("c_wT"), u + 1)
                if u >= 2:
                    pe.wait_ge(sem("c_y"), u - 1)
                for j in range(2):
                    for kb in range(tt + 1):
                        last = pe.matmul(bank[6 + u % 2][:, j * P:(j + 1) * P], pcT[:, u % 2, j * (tt + 1) + kb, :],
                                         zc[:, kb, C2 + (hp // 2) * P:C2 + (hp // 2 + 1) * P],
                                         start=(kb == 0), stop=(kb == tt))
                last.then_inc(sem("c_pv"), 1)

    def c_act(act):
        prologue(split_hi, act, "c_out")
        c_side_act(act, 4 * N_C + 1)
        for i in range(nu + 3):
            if i < nu:
                tt, hp = c_units[i]
                nk = (tt + 1) * P
                act.wait_ge(sem("c_max"), i + 1)
                if i >= 2:
                    act.wait_ge(sem("c_tr"), i - 1)
                for j in range(2):
                    act.activation(pc[:, i % 2, j, 0:nk], smc[:, i % 2, j, 0:nk], ACT.Exp,
                                   bias=mxc[:, i % 2, 2 + j:3 + j],
                                   accum_out=mxc[:, i % 2, 4 + j:5 + j]).then_inc(sem("c_exp"), 1)
            if 0 <= i - 3 < nu:
                u = i - 3
                tt, hp = c_units[u]
                act.wait_ge(sem("c_pv"), u + 1)
                act.wait_ge(sem("c_rl"), u + 1)
                for j in range(2):
                    hd = 2 * hp + j
                    last = act.activation(zc[:, tt, hd * P:(hd + 1) * P], bank[6 + u % 2][:, j * P:(j + 1) * P],
                                          ACT.Copy, scale=rlc[:, u % 4, j:j + 1])
                last.then_inc(sem("c_y"), 1)

    def c_dve(dve, link):
        c_side_dve(dve, link, 4 * N_C + 1)
        for i in range(nu + 2):
            if i < nu:
                tt, hp = c_units[i]
                nk = (tt + 1) * P
                dve.wait_ge(sem("c_scores"), i + 1)
                if i >= 2:
                    dve.wait_ge(sem("c_exp"), 2 * (i - 1))
                x = psum[:, 1024 * (i % 2):1024 * (i % 2) + 1024].rearrange("p (c k) -> p c k", c=2)[:, :, 0:nk]
                y = smc[:, i % 2, :, 0:nk]
                dve.scalar_tensor_tensor(out=y, in0=x, scalar=C_HD ** -0.5,
                                         in1=mb[:, tt, 0:nk].unsqueeze(1).broadcast_to([P, 2, nk]), op0=ALU.mult,
                                         op1=ALU.add).then_inc(sem("c_masked"), 1)
            if i >= 2:
                u = i - 2
                nq = 2 * (c_units[u][0] + 1)
                dve.wait_ge(sem("c_tr"), u + 1)
                if u >= 2:
                    dve.wait_ge(sem("c_pv"), u - 1)
                dve.tensor_copy(pcT[:, u % 2, 0:nq, :], bank[4 + u % 2][:, 0:nq * P]).then_inc(sem("c_wT"), 1)
            if i < nu:
                dve.wait_ge(sem("c_masked"), i + 1)
                dve.tensor_reduce(mxc[:, i % 2, 0:2], y, AX.X, ALU.max).then_inc(sem("c_top"), 1)
            if i >= 2:
                dve.wait_ge(sem("c_exp"), 2 * u + 2)
                if u >= 4:
                    dve.wait_ge(sem("c_y"), u - 3)
                dve.reciprocal(rlc[:, u % 4, :], mxc[:, u % 2, 4:6]).then_inc(sem("c_rl"), 1)
            if i < nu:
                dve.wait_ge(sem("c_top"), i + 1)
                if i >= 2:
                    dve.wait_ge(sem("c_rl"), i - 1)
                dve.tensor_scalar(mxc[:, i % 2, 2:4], mxc[:, i % 2, 0:2], -1.0, None,
                                  ALU.mult).then_inc(sem("c_max"), 1)
        dve.wait_ge(lo_ready, 4 * base["c_out"] + 2)

    def y_src(st):
        y = za if st == "ab_out" else zc
        return lambda tt, b: (zb[:, tt, (b - 2) * W:(b - 1) * W] if st == "ab_out" and b >= 2 else
                              y[:, tt, b * W:(b + 1) * W])

    def y_ready(st):
        if st == "ab_out":
            return lambda tt, b: (sem("ya_done"), tt + 1) if b < 2 else (sem("yb_done"), 2 * tt + b - 1)
        return lambda tt, b: (sem("c_y"), nu)

    mats = {"ab_in": A["ab_w_in"][0], "ab_out": A["ab_w_out"][0], "c_in": A["c_w_in"][0], "c_out": A["c_w_out"][0]}
    end = order[-1]
    block = ctx.enter_context(nc.Block())

    @block.sync
    def _(sp):
        for i, g in enumerate((A["mix_pre_g"][0], A["mix_pre_g"][1], A["mlp_pre_g"][0], A["mlp_pre_g"][1])):
            sp.dma_start(g_rows[KT * i:KT * (i + 1), :], g.rearrange("(k p) -> k p", p=P)).then_inc(sem("gpre_in"), 16)
        for st in order:
            b = base[st]
            if st.startswith("mlp"):
                l = int(st[-1])
                up = A["w_mlp_up"][l]
                down = A["w_mlp_down"][l]

                def quarter(Q, first):
                    for j in range(4):
                        load_slab(sp, b + 8 * Q + j, w_chunks(up, 0), Q * 4 * W + j * W, W, first and j == 0)
                    for j in range(4):
                        load_slab(sp, b + 8 * Q + 4 + j, w_chunks(down, Q), j * W, W)
                quarter(0, b == 0)
                with sp.Fori(1, 4) as Q:
                    quarter(Q, False)
            elif st.startswith("ple"):
                for j in range(4):
                    load_slab(sp, b + j, w_chunks(A["w_ple_gate"][int(st[-1])], 0), j * W, W, b + j == 0)
            elif st == "ab_in":
                for i, c in enumerate(ab_cols):
                    if i == 0:
                        for q in range(4):
                            c4 = slice(q * W, (q + 1) * W)
                            sp.dma_start(h[:, :, c4], A["x"][0].rearrange("(t p) d -> p t d", p=P)[:, :, c4])\
                                .then_inc(sem(f"x_in{q}"), 16)
                            sp.dma_start(raw[:, q, :, :], w_chunks(mats[st], 0)[q][:, :, c:c + W])\
                                .then_inc(landed[q], 16)
                        continue
                    load_slab(sp, b + i, w_chunks(mats[st], 0), c, ab_slabs[i][2], b + i == 0)
            elif st == "c_in":
                w = w_chunks(mats[st], 0)
                for i, (col, n) in enumerate(c_slabs):
                    load_slab(sp, b + i, w, col, n, b + i == 0)
            else:
                if st == "ab_out":
                    sp.wait_ge(sem("gated_y"), 8)
                for j in range(4):
                    load_slab(sp, b + j, w_chunks(mats[st], 0), j * W, W)
        for b in range(4):
            sp.wait_ge(*h_ready("end")(1, b))
            c4 = slice(b * W, (b + 1) * W)
            sp.dma_start(A["out"][0].rearrange("(t p) d -> p t d", p=P)[:, :, c4], h[:, :, c4])\
                .then_inc(sem("stored"), 16)
        sp.wait_ge(sem("stored"), 64)

    @block.gpsimd
    def _(pool):
        pool_setup(pool)
        for st in order:
            if st == "ab_in":
                ab_in_pool(pool)
                rwkv_pool(pool)
            if st.startswith("ple"):
                l = int(st[-1])
                if prv[st]:
                    pool.wait_ge(*mark("xT_lo", prv[st], 8))
                pool.dma_start(wple[:], A["w_ple_proj"][l].rearrange("(k p) n -> p k n", p=P))\
                    .then_inc(sem("ple_in"), 16)
                pool.dma_start(pin[:], A["p"][l, 0].rearrange("(t p) n -> p t n", p=P))\
                    .then_inc(sem("ple_in"), 16)
            if updates(st) and prv[st]:
                h_update_pool(pool, st, prv[st])
            if st == "c_in":
                c_pool(pool)
            if not st.endswith("_in"):
                g = {"ab_out": A["mix_post_g"][0], "c_out": A["mix_post_g"][1], "mlp0": A["mlp_post_g"][0],
                     "mlp1": A["mlp_post_g"][1], "ple0": A["ple_post_g"][0], "ple1": A["ple_post_g"][1]}[st]
                pool.wait_ge(*mark("xT_lo", st, 8))
                pool.dma_start(gpost[:], g.partition_broadcast(P)).then_inc(sem("gpost"), 16)

        h_update_pool(pool, "end", end)

    @block.scalar
    def _(act):
        act_setup(act)
        for st in order:
            if st.startswith("mlp"):
                l = int(st[-1])
                prologue(split_hi, act, st)
                act_first(act, st, base[st], W, GAIN[st], h_squares(act, st))
                mlp_act(act, l, 0)
                with act.Fori(1, 3) as Q:
                    mlp_act(act, l, Q)
                mlp_act(act, l, 3)
            elif st.startswith("ple"):
                prologue(split_hi, act, st)
                ple_act(act, int(st[-1]))
            elif st == "ab_in":
                ab_in_act(act)
                rwkv_act(act)
            elif st == "c_in":
                c_in_act(act)
                c_act(act)
            else:
                out_act(act, st)

    @block.vector
    def _(dve):
        link = Link(dve, sem("dve_chain"))
        dve_setup(dve, link)
        for st in order:
            if st.startswith("mlp"):
                l = int(st[-1])
                prologue(split_lo, dve, st)
                h_first(dve, link, st, base[st], W, GAIN[st], prv[st])
                mlp_dve(dve, l, 0)
                with dve.Fori(1, 3) as Q:
                    mlp_dve(dve, l, Q)
                mlp_dve(dve, l, 3)
            elif st.startswith("ple"):
                prologue(split_lo, dve, st)
                ple_dve(dve, link, int(st[-1]))
            elif st == "ab_in":
                ab_in_dve(dve, link)
                rwkv_dve(dve, link)
            elif st == "c_in":
                c_in_dve(dve, link)
                c_dve(dve, link)
            else:
                out_dve(dve, link, st)
        for b in range(late("end")):
            h_update(dve, link, "end", end, b)

    @block.tensor
    def _(pe):
        pe.wait_ge(sem("consts"), 1)
        pe.wait_ge(sem("gpre_in"), 64)
        pe.transpose(bank[7][:, 0:4 * KT], g_rows[:], ident[0:4 * KT, 0:4 * KT]).then_inc(sem("gpre_T"), 1)
        for st in order:
            if st.startswith("mlp"):
                l = int(st[-1])
                mlp_pe(pe, l, 0)
                with pe.Fori(1, 4) as Q:
                    mlp_pe(pe, l, Q)
            elif st.startswith("ple"):
                ple_pe(pe, int(st[-1]))
            elif st == "ab_in":
                ab_in_pe(pe)
                rwkv_pe(pe)
            elif st == "c_in":
                c_in_pe(pe)
                c_pe(pe)
            else:
                out_pe(pe, st, y_src(st), y_ready(st))

    ctx.close()


def kernel(**inputs):
    from concourse import bacc
    from concourse.bass_utils import run_bass_kernel_spmd

    nc = bacc.Bacc("TRN2", target_bir_lowering=False, num_devices=1)
    arrays, A = {}, {}
    for name, a in inputs.items():
        a = np.ascontiguousarray(a)
        arrays[f"in_{name}"] = a
        A[name] = nc.dram_tensor(f"in_{name}", a.shape, mybir.dt.from_np(a.dtype), kind="ExternalInput").ap()
    A["out"] = nc.dram_tensor("out_0", (1, T, D), F32, kind="ExternalOutput").ap()
    build(nc, A)
    r = run_bass_kernel_spmd(nc, [arrays], core_ids=[0])
    return r.results[0]["out_0"]
```
